# Optimizing a Trainium2 kernel written in Bass

```python
import jax, jax.numpy as jnp
from jax import lax
import numpy as np

D_MODEL = 2048
BATCH = 1
SEQ = 256
DEPTH = 2

PLE_DIM = 256
N_EVEN = (DEPTH + 1) // 2
N_ODD = DEPTH // 2
CHUNK = 64
CONV_W = 4
EPS = 1e-6
A_DK = 128
A_WIDTH = D_MODEL // 2
A_HEADS = A_WIDTH // A_DK
A_DV = A_WIDTH // A_HEADS
A_QK = A_HEADS * A_DK
B_WIDTH = D_MODEL // 2
B_BLOCK = 128
B_BLOCKS = B_WIDTH // B_BLOCK
LRU_C = 8.0
C_DK = 128
C_DV = 256
C_WIDTH = D_MODEL
C_HEADS = C_WIDTH // C_DV
C_QK = C_HEADS * C_DK
EVEN_IN = 2 * A_QK + 2 * A_WIDTH + 2 * B_WIDTH
EVEN_MIX = A_WIDTH + B_WIDTH
ODD_IN = 2 * C_QK + 3 * C_WIDTH + 2 * C_HEADS
ODD_MIX = C_WIDTH


def rmsnorm(x, g):
    xf = x.astype(jnp.float32)
    y = xf * lax.rsqrt(jnp.mean(xf * xf, axis=-1, keepdims=True) + EPS)
    return (y * g.astype(jnp.float32)).astype(x.dtype)

def head_rmsnorm(y, g):
    b, s, h, d = y.shape
    yn = y * lax.rsqrt(jnp.mean(y * y, axis=-1, keepdims=True) + EPS)
    return (yn * g.astype(jnp.float32).reshape(h, d)).reshape(b, s, h * d)

def causal_conv(u, w, bias):
    k_w = w.shape[0]
    s = u.shape[1]
    up = jnp.pad(u, ((0, 0), (k_w - 1, 0), (0, 0)))
    out = bias
    for k in range(k_w):
        out = out + up[:, k:k + s, :] * w[k]
    return out

def to_chunks(t):
    b, s = t.shape[:2]
    t = t.reshape((b, s // CHUNK, CHUNK) + t.shape[2:])
    return jnp.moveaxis(t, (1, 3), (0, 2))

def from_chunks(t):
    nc, b, h, c, d = t.shape
    return t.transpose(1, 0, 3, 2, 4).reshape(b, nc * c, h, d)

def hgrn2(q_pre, f_pre, v, lb):
    bsz, s, h, dk = q_pre.shape
    dv = v.shape[-1]
    lb = lb.reshape(h, dk)
    fp = f_pre.astype(jnp.float32)
    q = jax.nn.silu(q_pre.astype(jnp.float32))
    f = lb + (1.0 - lb) * jax.nn.sigmoid(fp)
    log_f = jnp.log(f)
    k = (1.0 - lb) * jax.nn.sigmoid(-fp)
    causal = jnp.tril(jnp.ones((CHUNK, CHUNK), dtype=bool))

    def step(state, inp):
        qc, kc, vc, gc = inp
        b = jnp.cumsum(gc, axis=2)
        diff = b[:, :, :, None, :] - b[:, :, None, :, :]
        w = jnp.exp(jnp.where(causal[:, :, None], diff, -jnp.inf))
        attn = jnp.einsum('bhtd,bhsd,bhtsd->bhts', qc, kc, w)
        o = (jnp.einsum('bhtd,bhde->bhte', qc * jnp.exp(b), state)
             + jnp.einsum('bhts,bhse->bhte', attn, vc))
        b_last = b[:, :, -1:, :]
        new_state = (jnp.exp(b_last[:, :, 0, :, None]) * state
                     + jnp.einsum('bhsd,bhse->bhde', kc * jnp.exp(b_last - b), vc))
        return new_state, o

    s0 = jnp.zeros((bsz, h, dk, dv), jnp.float32)
    xs = (to_chunks(q), to_chunks(k), to_chunks(v.astype(jnp.float32)), to_chunks(log_f))
    _, o = lax.scan(step, s0, xs)
    return from_chunks(o)

def rg_lru(xc, w_r, b_r, w_i, b_i, lam):
    bsz, s, wdt = xc.shape
    xf = xc.astype(jnp.float32)
    xh = xf.reshape(bsz, s, B_BLOCKS, B_BLOCK)
    r = jax.nn.sigmoid(jnp.einsum('bsnc,ncd->bsnd', xh, w_r.astype(jnp.float32)).reshape(bsz, s, wdt)
                       + b_r.astype(jnp.float32))
    ig = jax.nn.sigmoid(jnp.einsum('bsnc,ncd->bsnd', xh, w_i.astype(jnp.float32)).reshape(bsz, s, wdt)
                        + b_i.astype(jnp.float32))
    log_a = -LRU_C * r * jax.nn.softplus(-lam.astype(jnp.float32))
    a = jnp.exp(log_a)
    u = jnp.sqrt(-jnp.expm1(2.0 * log_a)) * (ig * xf)

    def combine(left, right):
        a1, b1 = left
        a2, b2 = right
        return a1 * a2, a2 * b1 + b2

    _, hs = lax.associative_scan(combine, (a, u), axis=1)
    return hs

def mlstm(q, k, v, li, lf):
    bsz, s, h, dk = q.shape
    dv = v.shape[-1]
    q = q.astype(jnp.float32) * (dk ** -0.5)
    causal = jnp.tril(jnp.ones((CHUNK, CHUNK), dtype=bool))

    def step(carry, inp):
        c_st, n_st, m_st = carry
        qc, kc, vc, lic, lfc = inp
        b = jnp.cumsum(lfc, axis=-1)
        dmat = jnp.where(causal, b[..., :, None] - b[..., None, :] + lic[..., None, :], -jnp.inf)
        inter = b + m_st[..., None]
        m_t = jnp.maximum(jnp.max(dmat, axis=-1), inter)
        wts = jnp.exp(dmat - m_t[..., None])
        g_inter = jnp.exp(inter - m_t)
        sc = jnp.einsum('bhtd,bhsd->bhts', qc, kc) * wts
        num = (g_inter[..., None] * jnp.einsum('bhtd,bhde->bhte', qc, c_st)
               + jnp.einsum('bhts,bhse->bhte', sc, vc))
        den = g_inter * jnp.einsum('bhtd,bhd->bht', qc, n_st) + jnp.sum(sc, axis=-1)
        hout = num / jnp.maximum(jnp.abs(den), jnp.exp(-m_t))[..., None]
        b_last = b[..., -1]
        logw = b_last[..., None] - b + lic
        m_new = jnp.maximum(b_last + m_st, jnp.max(logw, axis=-1))
        decay = jnp.exp(b_last + m_st - m_new)
        kw = kc * jnp.exp(logw - m_new[..., None])[..., None]
        c_new = decay[..., None, None] * c_st + jnp.einsum('bhsd,bhse->bhde', kw, vc)
        n_new = decay[..., None] * n_st + jnp.sum(kw, axis=2)
        return (c_new, n_new, m_new), hout

    init = (jnp.zeros((bsz, h, dk, dv), jnp.float32),
            jnp.zeros((bsz, h, dk), jnp.float32),
            jnp.zeros((bsz, h), jnp.float32))
    xs = (to_chunks(q), to_chunks(k.astype(jnp.float32)), to_chunks(v.astype(jnp.float32)),
          to_chunks(li), to_chunks(lf))
    _, hs = lax.scan(step, init, xs)
    return from_chunks(hs)

def first_inputs(seed: int = 0) -> dict:
    key = jax.random.key(seed)
    ks = jax.random.split(key, 32)

    def nrm(k, shape, scale):
        return jax.random.normal(k, shape, jnp.float32) * scale

    u = jax.random.uniform(ks[12], (N_EVEN, B_WIDTH), jnp.float32, minval=0.9, maxval=0.999)
    a0 = u ** (1.0 / LRU_C)
    return {
        "x": nrm(ks[0], (BATCH, SEQ, D_MODEL), 1.0),
        "p": nrm(ks[1], (DEPTH, BATCH, SEQ, PLE_DIM), 1.0),
        "e_norm": 1.0 + nrm(ks[2], (N_EVEN, D_MODEL), 0.02),
        "e_w_in": nrm(ks[3], (N_EVEN, D_MODEL, EVEN_IN), D_MODEL ** -0.5),
        "a_lb_logits": nrm(ks[4], (N_EVEN + 1, A_QK), 0.1),
        "a_norm": 1.0 + nrm(ks[5], (N_EVEN, A_WIDTH), 0.02),
        "b_conv_w": nrm(ks[6], (N_EVEN, CONV_W, B_WIDTH), CONV_W ** -0.5),
        "b_conv_b": nrm(ks[7], (N_EVEN, B_WIDTH), 0.01),
        "b_w_r": nrm(ks[8], (N_EVEN, B_BLOCKS, B_BLOCK, B_BLOCK), B_BLOCK ** -0.5),
        "b_b_r": nrm(ks[9], (N_EVEN, B_WIDTH), 0.1),
        "b_w_i": nrm(ks[10], (N_EVEN, B_BLOCKS, B_BLOCK, B_BLOCK), B_BLOCK ** -0.5),
        "b_b_i": nrm(ks[11], (N_EVEN, B_WIDTH), 0.1),
        "b_lambda": jnp.log(a0) - jnp.log1p(-a0),
        "e_w_out": nrm(ks[13], (N_EVEN, EVEN_MIX, D_MODEL), EVEN_MIX ** -0.5),
        "o_norm": 1.0 + nrm(ks[14], (N_ODD, D_MODEL), 0.02),
        "o_w_in": nrm(ks[15], (N_ODD, D_MODEL, ODD_IN), D_MODEL ** -0.5),
        "c_conv_w": nrm(ks[16], (N_ODD, CONV_W, 2 * C_QK), CONV_W ** -0.5),
        "c_conv_b": nrm(ks[17], (N_ODD, 2 * C_QK), 0.01),
        "c_b_i": nrm(ks[18], (N_ODD, C_HEADS), 0.1),
        "c_b_f": jnp.linspace(3.0, 6.0, C_HEADS, dtype=jnp.float32)[None, :] + nrm(ks[19], (N_ODD, C_HEADS), 0.1),
        "c_norm": 1.0 + nrm(ks[20], (N_ODD, C_WIDTH), 0.02),
        "o_w_out": nrm(ks[21], (N_ODD, ODD_MIX, D_MODEL), ODD_MIX ** -0.5),
        "ple_w": nrm(ks[22], (DEPTH, PLE_DIM, D_MODEL), PLE_DIM ** -0.5),
        "ple_norm": 1.0 + nrm(ks[23], (DEPTH, D_MODEL), 0.02),
        "ple_gate_w": nrm(ks[24], (DEPTH, D_MODEL, D_MODEL), D_MODEL ** -0.5),
        "final_norm": 1.0 + nrm(ks[25], (D_MODEL,), 0.02),
    }

def first_block(x, p, e_norm, e_w_in, a_lb_logits, a_norm, b_conv_w, b_conv_b, b_w_r, b_b_r,
              b_w_i, b_b_i, b_lambda, e_w_out, o_norm, o_w_in, c_conv_w, c_conv_b, c_b_i,
              c_b_f, c_norm, o_w_out, ple_w, ple_norm, ple_gate_w, final_norm):
    bsz, s, _ = x.shape
    lbs = jnp.cumsum(jax.nn.softmax(a_lb_logits.astype(jnp.float32), axis=0), axis=0)
    h = x
    for i in range(DEPTH):
        j = i // 2
        hn = rmsnorm(h, e_norm[j] if i % 2 == 0 else o_norm[j])
        if i % 2 == 0:
            u = hn @ e_w_in[j]
            o0 = 0
            qa = u[..., o0:o0 + A_QK]; o0 += A_QK
            fa = u[..., o0:o0 + A_QK]; o0 += A_QK
            ia = u[..., o0:o0 + A_WIDTH]; o0 += A_WIDTH
            za = u[..., o0:o0 + A_WIDTH]; o0 += A_WIDTH
            xb = u[..., o0:o0 + B_WIDTH]; o0 += B_WIDTH
            zb = u[..., o0:o0 + B_WIDTH]
            ya = hgrn2(qa.reshape(bsz, s, A_HEADS, A_DK), fa.reshape(bsz, s, A_HEADS, A_DK),
                       ia.reshape(bsz, s, A_HEADS, A_DV), lbs[j])
            ya = head_rmsnorm(ya, a_norm[j]) * jax.nn.silu(za.astype(jnp.float32))
            xc = causal_conv(xb, b_conv_w[j], b_conv_b[j])
            yb = rg_lru(xc, b_w_r[j], b_b_r[j], b_w_i[j], b_b_i[j], b_lambda[j])
            yb = yb * jax.nn.silu(zb.astype(jnp.float32))
            y = jnp.concatenate([ya, yb], axis=-1).astype(h.dtype)
            mix = y @ e_w_out[j]
        else:
            u = hn @ o_w_in[j]
            o0 = 0
            qk = u[..., o0:o0 + 2 * C_QK]; o0 += 2 * C_QK
            v = u[..., o0:o0 + C_WIDTH]; o0 += C_WIDTH
            og = u[..., o0:o0 + C_WIDTH]; o0 += C_WIDTH
            z = u[..., o0:o0 + C_WIDTH]; o0 += C_WIDTH
            ig = u[..., o0:o0 + C_HEADS]; o0 += C_HEADS
            fg = u[..., o0:o0 + C_HEADS]
            qk = jax.nn.silu(causal_conv(qk, c_conv_w[j], c_conv_b[j]))
            q = qk[..., :C_QK].reshape(bsz, s, C_HEADS, C_DK)
            k = qk[..., C_QK:].reshape(bsz, s, C_HEADS, C_DK)
            li = ig.astype(jnp.float32) + c_b_i[j].astype(jnp.float32)
            lf = jax.nn.log_sigmoid(fg.astype(jnp.float32) + c_b_f[j].astype(jnp.float32))
            yc = mlstm(q, k, v.reshape(bsz, s, C_HEADS, C_DV), li, lf)
            yc = (head_rmsnorm(yc, c_norm[j]) * jax.nn.sigmoid(og.astype(jnp.float32))
                  * jax.nn.silu(z.astype(jnp.float32)))
            mix = yc.astype(h.dtype) @ o_w_out[j]
        h = h + mix
        pl = rmsnorm(p[i].astype(h.dtype) @ ple_w[i], ple_norm[i])
        h = h + jax.nn.sigmoid(h @ ple_gate_w[i]) * pl
    return rmsnorm(h, final_norm)


N_EVEN_2 = (DEPTH + 1) // 2
N_ODD_2 = DEPTH // 2
N_MEM = 256
ROPE_THETA = 500000.0
ROT_FRAC = 4
Q_BLOCK = 128

MLA_HEADS = 8
MLA_Q_RANK = 512
MLA_KV_RANK = 256
MLA_NOPE = 128
MLA_ROPE = 64
MLA_V = 128
MOBA_HEADS = 8
MOBA_DH = 128
MOBA_BLOCK = 256
MOBA_TOPK = 3
MOBA_QCHUNK = 32
SWA_HEADS = 16
SWA_KV_HEADS = 2
SWA_DH = 64
SWA_WINDOW = 128
DIL_HEADS = 6
DIL_DH = 128
DIL_PATTERNS = ((128, 1), (512, 4), (2048, 16))
MEM_HEADS = 4
MEM_DH = 128

MEMQ_W = MEM_HEADS * MEM_DH
EVEN_VW = MLA_HEADS * MLA_V + MOBA_HEADS * MOBA_DH + MEMQ_W
EVEN_SPLITS = (MLA_Q_RANK, MLA_KV_RANK, MLA_ROPE, 3 * MOBA_HEADS * MOBA_DH, MEMQ_W, EVEN_VW)
EVEN_IN_2 = sum(EVEN_SPLITS)
ODD_VW = SWA_HEADS * SWA_DH + DIL_HEADS * DIL_DH + MEMQ_W
ODD_SPLITS = ((SWA_HEADS + 2 * SWA_KV_HEADS) * SWA_DH, 3 * DIL_HEADS * DIL_DH, MEMQ_W, ODD_VW)
ODD_IN_2 = sum(ODD_SPLITS)


def split_cols(h, sizes):
    return jnp.split(h, [int(i) for i in np.cumsum(sizes)[:-1]], axis=-1)

def rms_norm(x, g):
    xf = x.astype(jnp.float32)
    y = xf * lax.rsqrt(jnp.mean(xf * xf, axis=-1, keepdims=True) + EPS)
    return (y * g.astype(jnp.float32)).astype(x.dtype)

def apply_rope(x, rot_dim):
    S = x.shape[1]
    inv = 1.0 / (ROPE_THETA ** (jnp.arange(0, rot_dim, 2, dtype=jnp.float32) / rot_dim))
    ang = jnp.arange(S, dtype=jnp.float32)[:, None] * inv[None, :]
    c, s = jnp.cos(ang)[None, :, None, :], jnp.sin(ang)[None, :, None, :]
    xr = x[..., :rot_dim].astype(jnp.float32)
    x1, x2 = xr[..., : rot_dim // 2], xr[..., rot_dim // 2:]
    rot = jnp.concatenate([x1 * c - x2 * s, x1 * s + x2 * c], axis=-1).astype(x.dtype)
    return jnp.concatenate([rot, x[..., rot_dim:]], axis=-1)

def causal_attention_qblocks(q, k, v, scale):
    B, H, S, dq = q.shape
    nb = S // Q_BLOCK
    qb = q.reshape(B, H, nb, Q_BLOCK, dq).transpose(2, 0, 1, 3, 4)
    kpos = jnp.arange(S)

    def one(args):
        qi, n = args
        s = jnp.einsum('bhqd,bhkd->bhqk', qi, k).astype(jnp.float32) * scale
        qpos = n * Q_BLOCK + jnp.arange(Q_BLOCK)
        s = jnp.where(kpos[None, :] <= qpos[:, None], s, -jnp.inf)
        p = jax.nn.softmax(s, axis=-1).astype(v.dtype)
        return jnp.einsum('bhqk,bhkd->bhqd', p, v)

    o = lax.map(one, (qb, jnp.arange(nb)))
    return o.transpose(1, 2, 0, 3, 4).reshape(B, H, S, v.shape[-1])

def moba_attention(q, k, v):
    B, H, S, dh = q.shape
    L = MOBA_BLOCK
    nblk = -(-S // L)
    Sp = nblk * L
    pad = ((0, 0), (0, 0), (0, Sp - S), (0, 0))
    kb = jnp.pad(k, pad).reshape(B, H, nblk, L, dh)
    vb = jnp.pad(v, pad).reshape(B, H, nblk, L, dh)
    kmean = jnp.mean(kb.astype(jnp.float32), axis=3)
    topk = min(MOBA_TOPK, nblk - 1)
    scale = dh ** -0.5
    QC = MOBA_QCHUNK
    nc = S // QC
    qc = q.reshape(B, H, nc, QC, dh).transpose(2, 0, 1, 3, 4)
    offs = jnp.arange(L)
    gather = jax.vmap(jax.vmap(lambda t, i: t[i]))

    def one(args):
        qi, c = args
        blk = (c * QC) // L
        qpos = c * QC + jnp.arange(QC)
        k_own = lax.dynamic_index_in_dim(kb, blk, axis=2, keepdims=False)
        v_own = lax.dynamic_index_in_dim(vb, blk, axis=2, keepdims=False)
        s_own = jnp.einsum('bhqd,bhld->bhql', qi, k_own).astype(jnp.float32) * scale
        s_own = jnp.where((blk * L + offs)[None, :] <= qpos[:, None], s_own, -jnp.inf)
        if topk == 0:
            p = jax.nn.softmax(s_own, axis=-1).astype(v.dtype)
            return jnp.einsum('bhql,bhld->bhqd', p, v_own)
        gate = jnp.einsum('bhqd,bhnd->bhqn', qi.astype(jnp.float32), kmean)
        gate = jnp.where(jnp.arange(nblk) < blk, gate, -jnp.inf)
        _, idx = lax.top_k(gate, topk)
        valid = jnp.arange(topk) < blk
        kg = gather(kb, idx)
        vg = gather(vb, idx)
        s_sel = jnp.einsum('bhqd,bhqkld->bhqkl', qi, kg).astype(jnp.float32) * scale
        s_sel = jnp.where(valid[:, None], s_sel, -jnp.inf)
        s_all = jnp.concatenate([s_sel.reshape(B, H, QC, topk * L), s_own], axis=-1)
        p = jax.nn.softmax(s_all, axis=-1).astype(v.dtype)
        p_sel = p[..., : topk * L].reshape(B, H, QC, topk, L)
        return (jnp.einsum('bhqkl,bhqkld->bhqd', p_sel, vg)
                + jnp.einsum('bhql,bhld->bhqd', p[..., topk * L:], v_own))

    o = lax.map(one, (qc, jnp.arange(nc)))
    return o.transpose(1, 2, 0, 3, 4).reshape(B, H, S, dh)

def banded_attention(q, k, v, max_dist, scale):
    B, Hk, G, L, dh = q.shape
    QB = Q_BLOCK
    nb = -(-L // QB)
    Lp = nb * QB
    qp = jnp.pad(q, ((0, 0), (0, 0), (0, 0), (0, Lp - L), (0, 0))).reshape(B, Hk, G, nb, QB, dh)
    kp = jnp.pad(k, ((0, 0), (0, 0), (QB, Lp - L), (0, 0)))
    vp = jnp.pad(v, ((0, 0), (0, 0), (QB, Lp - L), (0, 0)))
    kband = jnp.concatenate([kp[:, :, :Lp].reshape(B, Hk, nb, QB, dh),
                             kp[:, :, QB:].reshape(B, Hk, nb, QB, dh)], axis=3)
    vband = jnp.concatenate([vp[:, :, :Lp].reshape(B, Hk, nb, QB, dh),
                             vp[:, :, QB:].reshape(B, Hk, nb, QB, dh)], axis=3)
    s = jnp.einsum('bkgnqd,bknsd->bkgnqs', qp, kband).astype(jnp.float32) * scale
    dist = QB + jnp.arange(QB)[:, None] - jnp.arange(2 * QB)[None, :]
    kpos = jnp.arange(nb)[:, None] * QB - QB + jnp.arange(2 * QB)[None, :]
    mask = ((dist >= 0) & (dist <= max_dist))[None] & (kpos >= 0)[:, None, :]
    s = jnp.where(mask, s, -jnp.inf)
    m = jnp.max(s, axis=-1, keepdims=True)
    p = jnp.exp(s - m)
    l = jnp.sum(p, axis=-1, keepdims=True)
    o = jnp.einsum('bkgnqs,bknsd->bkgnqd', (p / l).astype(v.dtype), vband)
    lse = (m + jnp.log(l))[..., 0]
    return (o.reshape(B, Hk, G, Lp, dh)[:, :, :, :L], lse.reshape(B, Hk, G, Lp)[:, :, :, :L])

def dilated_attention(q, k, v):
    B, S, H, dh = q.shape
    outs, lses = [], []
    for window, dil in DIL_PATTERNS:
        L = S // dil

        def to_sub(t):
            return t.reshape(B, L, dil, H, dh).transpose(0, 2, 3, 1, 4).reshape(B * dil, H, L, dh)

        o, lse = banded_attention(to_sub(q)[:, :, None], to_sub(k), to_sub(v), window // dil, dh ** -0.5)
        outs.append(o[:, :, 0].reshape(B, dil, H, L, dh).transpose(0, 3, 1, 2, 4).reshape(B, S, H, dh))
        lses.append(lse[:, :, 0].reshape(B, dil, H, L).transpose(0, 3, 1, 2).reshape(B, S, H))
    w = jax.nn.softmax(jnp.stack(lses, axis=0), axis=0)
    return jnp.sum(w[..., None] * jnp.stack(outs, axis=0).astype(jnp.float32), axis=0).astype(q.dtype)

def memory_attention(q_mem, mem, mem_norm_g, w_mem_kv):
    B, S, _ = q_mem.shape
    kv = (rms_norm(mem, mem_norm_g) @ w_mem_kv).reshape(B, -1, 2, MEM_HEADS, MEM_DH)
    q = q_mem.reshape(B, S, MEM_HEADS, MEM_DH)
    s = jnp.einsum('bshd,bmhd->bhsm', q, kv[:, :, 0]).astype(jnp.float32) * MEM_DH ** -0.5
    p = jax.nn.softmax(s, axis=-1).astype(q.dtype)
    return jnp.einsum('bhsm,bmhd->bshd', p, kv[:, :, 1]).reshape(B, S, MEMQ_W)

def even_layer(x, mem, norm_g, w_in, q_norm_g, w_uq, kv_norm_g, w_ukv, mem_norm_g, w_mem_kv, w_out):
    B, S, _ = x.shape
    h = rms_norm(x, norm_g) @ w_in
    c_q, c_kv, k_pe, qkv_b, q_mem, gate = split_cols(h, EVEN_SPLITS)
    q_a = (rms_norm(c_q, q_norm_g) @ w_uq).reshape(B, S, MLA_HEADS, MLA_NOPE + MLA_ROPE)
    q_a = jnp.concatenate([q_a[..., :MLA_NOPE], apply_rope(q_a[..., MLA_NOPE:], MLA_ROPE)], axis=-1)
    kv_a = (rms_norm(c_kv, kv_norm_g) @ w_ukv).reshape(B, S, MLA_HEADS, MLA_NOPE + MLA_V)
    k_pe = apply_rope(k_pe[:, :, None, :], MLA_ROPE)
    k_a = jnp.concatenate([kv_a[..., :MLA_NOPE],
                           jnp.broadcast_to(k_pe, (B, S, MLA_HEADS, MLA_ROPE))], axis=-1)
    v_a = kv_a[..., MLA_NOPE:]
    o_a = causal_attention_qblocks(q_a.transpose(0, 2, 1, 3), k_a.transpose(0, 2, 1, 3),
                                   v_a.transpose(0, 2, 1, 3), (MLA_NOPE + MLA_ROPE) ** -0.5)
    o_a = o_a.transpose(0, 2, 1, 3).reshape(B, S, MLA_HEADS * MLA_V)
    qkv_b = qkv_b.reshape(B, S, 3, MOBA_HEADS, MOBA_DH)
    rot = MOBA_DH // ROT_FRAC
    q_b = apply_rope(qkv_b[:, :, 0], rot).transpose(0, 2, 1, 3)
    k_b = apply_rope(qkv_b[:, :, 1], rot).transpose(0, 2, 1, 3)
    v_b = qkv_b[:, :, 2].transpose(0, 2, 1, 3)
    o_b = moba_attention(q_b, k_b, v_b).transpose(0, 2, 1, 3).reshape(B, S, MOBA_HEADS * MOBA_DH)
    o_m = memory_attention(q_mem, mem, mem_norm_g, w_mem_kv)
    y = jnp.concatenate([o_a, o_b.astype(o_a.dtype), o_m.astype(o_a.dtype)], axis=-1) * jax.nn.silu(gate)
    return x + (y @ w_out).astype(x.dtype)

def odd_layer(x, mem, norm_g, w_in, sinks, mem_norm_g, w_mem_kv, w_out):
    B, S, _ = x.shape
    h = rms_norm(x, norm_g) @ w_in
    qkv_c, qkv_d, q_mem, gate = split_cols(h, ODD_SPLITS)
    q_c, k_c, v_c = split_cols(qkv_c, (SWA_HEADS * SWA_DH, SWA_KV_HEADS * SWA_DH, SWA_KV_HEADS * SWA_DH))
    rot_c = SWA_DH // ROT_FRAC
    G = SWA_HEADS // SWA_KV_HEADS
    q_c = apply_rope(q_c.reshape(B, S, SWA_HEADS, SWA_DH), rot_c)
    k_c = apply_rope(k_c.reshape(B, S, SWA_KV_HEADS, SWA_DH), rot_c)
    v_c = v_c.reshape(B, S, SWA_KV_HEADS, SWA_DH)
    qg = q_c.reshape(B, S, SWA_KV_HEADS, G, SWA_DH).transpose(0, 2, 3, 1, 4)
    o_c, lse_c = banded_attention(qg, k_c.transpose(0, 2, 1, 3), v_c.transpose(0, 2, 1, 3),
                                  SWA_WINDOW - 1, SWA_DH ** -0.5)
    o_c = o_c.transpose(0, 3, 1, 2, 4).reshape(B, S, SWA_HEADS, SWA_DH)
    lse_c = lse_c.transpose(0, 3, 1, 2).reshape(B, S, SWA_HEADS)
    sink_w = jax.nn.sigmoid(lse_c - sinks.astype(jnp.float32))
    o_c = (o_c.astype(jnp.float32) * sink_w[..., None]).astype(x.dtype).reshape(B, S, SWA_HEADS * SWA_DH)
    qkv_d = qkv_d.reshape(B, S, 3, DIL_HEADS, DIL_DH)
    rot_d = DIL_DH // ROT_FRAC
    o_d = dilated_attention(apply_rope(qkv_d[:, :, 0], rot_d), apply_rope(qkv_d[:, :, 1], rot_d),
                            qkv_d[:, :, 2]).reshape(B, S, DIL_HEADS * DIL_DH)
    o_m = memory_attention(q_mem, mem, mem_norm_g, w_mem_kv)
    y = jnp.concatenate([o_c, o_d.astype(o_c.dtype), o_m.astype(o_c.dtype)], axis=-1) * jax.nn.silu(gate).astype(o_c.dtype)
    return x + (y @ w_out).astype(x.dtype)

def second_inputs(seed: int = 0) -> dict:
    key = jax.random.key(seed)
    ks = jax.random.split(key, 20)

    def dense(k, shape):
        return jax.random.normal(k, shape, jnp.float32) * shape[-2] ** -0.5

    def gain(k, shape):
        return 1.0 + 0.02 * jax.random.normal(k, shape, jnp.float32)

    return {
        "x": jax.random.normal(ks[0], (BATCH, SEQ, D_MODEL), jnp.float32),
        "mem": jax.random.normal(ks[1], (BATCH, N_MEM, D_MODEL), jnp.float32),
        "ev_norm_g": gain(ks[2], (N_EVEN_2, D_MODEL)),
        "ev_w_in": dense(ks[3], (N_EVEN_2, D_MODEL, EVEN_IN_2)),
        "ev_q_norm_g": gain(ks[4], (N_EVEN_2, MLA_Q_RANK)),
        "ev_w_uq": dense(ks[5], (N_EVEN_2, MLA_Q_RANK, MLA_HEADS * (MLA_NOPE + MLA_ROPE))),
        "ev_kv_norm_g": gain(ks[6], (N_EVEN_2, MLA_KV_RANK)),
        "ev_w_ukv": dense(ks[7], (N_EVEN_2, MLA_KV_RANK, MLA_HEADS * (MLA_NOPE + MLA_V))),
        "ev_mem_norm_g": gain(ks[8], (N_EVEN_2, D_MODEL)),
        "ev_w_mem_kv": dense(ks[9], (N_EVEN_2, D_MODEL, 2 * MEMQ_W)),
        "ev_w_out": dense(ks[10], (N_EVEN_2, EVEN_VW, D_MODEL)),
        "od_norm_g": gain(ks[11], (N_ODD_2, D_MODEL)),
        "od_w_in": dense(ks[12], (N_ODD_2, D_MODEL, ODD_IN_2)),
        "od_sinks": 0.5 * jax.random.normal(ks[13], (N_ODD_2, SWA_HEADS), jnp.float32),
        "od_mem_norm_g": gain(ks[14], (N_ODD_2, D_MODEL)),
        "od_w_mem_kv": dense(ks[15], (N_ODD_2, D_MODEL, 2 * MEMQ_W)),
        "od_w_out": dense(ks[16], (N_ODD_2, ODD_VW, D_MODEL)),
        "final_norm_g": gain(ks[17], (D_MODEL,)),
    }

def second_block(x, mem, ev_norm_g, ev_w_in, ev_q_norm_g, ev_w_uq, ev_kv_norm_g, ev_w_ukv,
              ev_mem_norm_g, ev_w_mem_kv, ev_w_out, od_norm_g, od_w_in, od_sinks,
              od_mem_norm_g, od_w_mem_kv, od_w_out, final_norm_g):
    for layer in range(DEPTH):
        i = layer // 2
        if layer % 2 == 0:
            x = even_layer(x, mem, ev_norm_g[i], ev_w_in[i], ev_q_norm_g[i], ev_w_uq[i],
                           ev_kv_norm_g[i], ev_w_ukv[i], ev_mem_norm_g[i], ev_w_mem_kv[i], ev_w_out[i])
        else:
            x = odd_layer(x, mem, od_norm_g[i], od_w_in[i], od_sinks[i], od_mem_norm_g[i],
                          od_w_mem_kv[i], od_w_out[i])
    return rms_norm(x, final_norm_g)


def setup_inputs(seed=0):
    out = dict(first_inputs(seed))
    for name, value in second_inputs(seed + 1).items():
        if name != "x":
            out[name + "_2"] = value
    return out


def reference(
    x, p, e_norm, e_w_in, a_lb_logits, a_norm, b_conv_w, b_conv_b, b_w_r, b_b_r, b_w_i, b_b_i,
    b_lambda, e_w_out, o_norm, o_w_in, c_conv_w, c_conv_b, c_b_i, c_b_f, c_norm, o_w_out, ple_w,
    ple_norm, ple_gate_w, final_norm, mem_2, ev_norm_g_2, ev_w_in_2, ev_q_norm_g_2, ev_w_uq_2,
    ev_kv_norm_g_2, ev_w_ukv_2, ev_mem_norm_g_2, ev_w_mem_kv_2, ev_w_out_2, od_norm_g_2,
    od_w_in_2, od_sinks_2, od_mem_norm_g_2, od_w_mem_kv_2, od_w_out_2, final_norm_g_2,
):
    x = first_block(
        x, p, e_norm, e_w_in, a_lb_logits, a_norm, b_conv_w, b_conv_b, b_w_r, b_b_r, b_w_i,
        b_b_i, b_lambda, e_w_out, o_norm, o_w_in, c_conv_w, c_conv_b, c_b_i, c_b_f, c_norm,
        o_w_out, ple_w, ple_norm, ple_gate_w, final_norm,
    )
    return second_block(
        x, mem_2, ev_norm_g_2, ev_w_in_2, ev_q_norm_g_2, ev_w_uq_2, ev_kv_norm_g_2, ev_w_ukv_2,
        ev_mem_norm_g_2, ev_w_mem_kv_2, ev_w_out_2, od_norm_g_2, od_w_in_2, od_sinks_2,
        od_mem_norm_g_2, od_w_mem_kv_2, od_w_out_2, final_norm_g_2,
    )


_drawn_inputs = setup_inputs


def setup_inputs(seed=0):
    import zlib

    import numpy as np

    out = dict(_drawn_inputs(seed))
    spreads = {}
    factors = {'e_norm': 4.604,
     'a_lb_logits': 8.0,
     'a_norm': 7.356,
     'b_conv_b': 3.951,
     'b_b_r': 8.0,
     'b_b_i': 8.0,
     'o_norm': 5.548,
     'c_conv_b': 8.0,
     'c_b_i': 8.0,
     'c_norm': 8.0,
     'ple_norm': 4.487,
     'ev_norm_g_2': 8.0,
     'ev_q_norm_g_2': 8.0,
     'ev_kv_norm_g_2': 8.0,
     'ev_mem_norm_g_2': 8.0,
     'od_norm_g_2': 8.0,
     'od_sinks_2': 48.776,
     'od_mem_norm_g_2': 8.0,
     'final_norm_g_2': 7.852}
    for name, (base, spread) in spreads.items():
        noise = np.random.default_rng([zlib.crc32(name.encode()), seed]).standard_normal(out[name].shape)
        drawn = base * np.exp(spread * noise) if base else spread * noise
        out[name] = __import__('jax').numpy.asarray(drawn.astype(out[name].dtype))
    for name, factor in factors.items():
        out[name] = (out[name] * factor).astype(out[name].dtype)
    return out
```

```python
import numpy as np

T = 256
P = 128
D = 2048
KD = D // P
EPS = 1e-6
RAW_SLOTS = 4
SPLIT_SLOTS = 2
CELLS_MAX = 6
NEG = -1.0e30


def stage_table():
    return [
        ("ein", "xa", 16, 20, 2),
        ("ein_zb", "xa", 16, 4, 2),
        ("ple0", "xs", 2, 8, 2),
        ("eout", "xb", 16, 8, 2),
        ("gate0", "xa", 16, 8, 2),
        ("ogate", "xb", 16, 1, 1),
        ("oqk", "xb", 16, 8, 2),
        ("ov", "xb", 16, 8, 2),
        ("oog", "xb", 16, 8, 2),
        ("oz", "xb", 16, 8, 2),
        ("ple1", "xs", 2, 8, 2),
        ("oout", "xa", 16, 8, 2),
        ("gate1", "xb", 16, 8, 2),
        ("evkpe", "xa", 16, 1, 1),
        ("evc", "xa", 16, 3, 2),
        ("evmem", "xb", 16, 4, 2),
        ("uq", "xs", 4, 6, 2),
        ("ukv", "xs", 2, 8, 2),
        ("evgate_a", "xa", 16, 4, 2),
        ("evmoba", "xa", 16, 14, 2),
        ("evgate_b", "xa", 16, 6, 2),
        ("evout", "xb", 20, 8, 2),
        ("odin", "xa", 16, 16, 2),
        ("odmem", "xb", 16, 4, 2),
        ("odgate", "xa", 16, 9, 2),
        ("odout", "xb", 18, 8, 2),
    ]


def unit_cells(blocks, nb):
    if blocks == 2:
        return [[(k, b)] for b in range(nb) for k in range(blocks)]
    n = 8 if blocks >= 16 else 4
    small, more = divmod(blocks, n)
    out, k = [], 0
    for q in range(n):
        m = small + (q < more)
        out.append([(kk, b) for kk in range(k, k + m) for b in range(nb)])
        k += m
    return out


class Stage:

    def __init__(self, row, unit0, pair0):
        self.name, self.x, self.blocks, self.pairs, self.nb = row
        self.units = unit_cells(self.blocks, self.nb)
        self.upp = len(self.units)
        self.unit0, self.pair0 = unit0, pair0


def stages():
    out, unit0, pair0 = {}, 0, 0
    for row in stage_table():
        s = Stage(row, unit0, pair0)
        out[s.name] = s
        unit0 += s.pairs * s.upp
        pair0 += s.pairs
    return out


COLS = [
    ("e_norm", 16), ("a_lb0", 8), ("a_lb1", 8), ("a_norm", 8), ("b_conv_w", 32), ("b_conv_b", 8),
    ("b_b_r", 8), ("b_b_i", 8), ("b_lambda", 8), ("o_norm", 16), ("c_conv_w", 64), ("c_conv_b", 16),
    ("c_gate_b", 1), ("c_norm", 16), ("ple_norm0", 16), ("ple_norm1", 16), ("final_norm", 16),
    ("ev_norm", 16), ("ev_q_norm", 4), ("ev_kv_norm", 2), ("ev_mem_norm", 16), ("od_norm", 16),
    ("sinks", 16), ("od_mem_norm", 16), ("final_norm_2", 16),
]
COL_AT, _n = {}, 0
for _name, _w in COLS:
    COL_AT[_name] = _n
    _n += _w
NCOLS = _n
ROW_I, ROW_F = 0, 32


def build(nc, A, out, upto=99):
    import concourse.bass as bass
    from concourse import mybir
    from contextlib import ExitStack

    F32, F32R, U8 = mybir.dt.float32, mybir.dt.float32r, mybir.dt.uint8
    ALU, ACT = mybir.AluOpType, mybir.ActivationFunctionType
    AX = mybir.AxisListType.X
    ADD, SUB, MUL, MAX = ALU.add, ALU.subtract, ALU.mult, ALU.max
    ds = bass.ds
    ST = stages()

    ctx = ExitStack()
    with ctx:
        def sb(name, shape, dt=F32):
            return ctx.enter_context(nc.sbuf_tensor(name, shape, dt))

        def sem(name):
            return ctx.enter_context(nc.semaphore(name))

        with nc.sbuf_tensor("oa", [P, 32, T], F32) as oa:
            pass
        xa = sb("xa", [P, 16, 2 * T], F32R)
        with nc.sbuf_tensor("ob", [P, 40, T], F32) as ob:
            pass
        xb = sb("xb", [P, 20, 2 * T], F32R)
        xs = sb("xs", [P, 6, 2 * T], F32R)
        h = sb("h", [P, KD, T])
        w = sb("w", [P, 44, T])
        raw = sb("raw", [P, RAW_SLOTS, CELLS_MAX * P])
        w_hi = sb("w_hi", [P, SPLIT_SLOTS, CELLS_MAX * P], F32R)
        w_lo = sb("w_lo", [P, SPLIT_SLOTS, CELLS_MAX * P], F32R)
        cross = sb("cross", [P, 2, 2, T])
        tb = sb("tb", [P, 2, T])
        sq = sb("sq", [P, 2, 2, T])
        rs = sb("rs", [P, 4, T])
        RS_LAYER, RS_PLE, RS_Q, RS_MEM = range(4)
        RS_KV = RS_PLE
        sm = sb("sm", [P, 2, 2, T])
        pt = sb("pt", [P, 2, 2, T])
        small = sb("small", [P, 64])
        cols = sb("cols", [P, NCOLS])
        ident = sb("ident", [P, P])
        ones = sb("ones", [P, P])
        gsel = sb("gsel", [P, 2, P])
        masks = sb("masks", [P, 4, 2, T])
        rope = sb("rope", [P, 2, 2, T])
        rot = sb("rot", [P, 2, P])
        lvl = sb("lvl", [P, 8, P], U8)
        ps = ctx.enter_context(nc.psum_tensor("ps", [P, 8, 512], F32))
        X = {"xa": xa, "xb": xb, "xs": xs}
        M_LSTM, M_CAUSAL, M_SWA, M_DIL = range(4)

        def col(name, n=None, at=0):
            c = COL_AT[name]
            return cols[:, c:c + dict(COLS)[name]] if n is None else cols[:, ds(c + at, n)]

        def wide(ap, n):
            return ap.unsqueeze(2).to_broadcast([P, n, T])

        def along(ap, n):
            return ap.unsqueeze(1).to_broadcast([P, n, T])

        x_loaded, cols_loaded, consts_loaded = sem("x_loaded"), sem("cols_loaded"), sem("consts_loaded")
        unit_loaded = [sem(f"unit_loaded{i}") for i in range(RAW_SLOTS)]
        hi_done, lo_ready, unit_used = sem("hi_done"), sem("lo_ready"), sem("unit_used")
        cross_ready, pair_out, stored = sem("cross_ready"), sem("pair_out"), sem("stored")
        x_ready = sem("x_ready")
        sq_ready, sq_used, var_ready, std_ready = sem("sq_ready"), sem("sq_used"), sem("var_ready"), sem("std_ready")
        dve_step, act_step = sem("dve_step"), sem("act_step")
        ones_set = sem("ones_set")
        stream_loaded = [sem("stream_loaded0"), sem("stream_loaded1")]
        stream_split = sem("stream_split")
        out_stored = sem("out_stored")
        h_ready = sem("h_ready")
        par_in, par_exp, par_done = sem("par_in"), sem("par_exp"), sem("par_done")
        hg_sig, hg_q, hg_logf, hg_qk = sem("hg_sig"), sem("hg_q"), sem("hg_logf"), sem("hg_qk")
        hg_diff, hg_exp, hg_lv_in, hg_lv_out, hg_masked = (
            sem("hg_diff"), sem("hg_exp"), sem("hg_lv_in"), sem("hg_lv_out"), sem("hg_masked"))
        v_turned, v_copied = sem("v_turned"), sem("v_copied")
        hg_o, hg_ocopied = sem("hg_o"), sem("hg_ocopied")
        hn_sums, hn_var, hn_std, hn_gate = sem("hn_sums"), sem("hn_var"), sem("hn_std"), sem("hn_gate")
        lr_conv, lr_w, lr_pre, lr_act, lr_th, lr_fix, lr_root = (
            sem("lr_conv"), sem("lr_w"), sem("lr_pre"), sem("lr_act"), sem("lr_th"), sem("lr_fix"), sem("lr_root"))
        y_gate, y_done = sem("y_gate"), sem("y_done")
        g_sig, g_pre = sem("g_sig"), sem("g_pre")
        cv_pre, cv_sig, cv_done = sem("cv_pre"), sem("cv_sig"), sem("cv_done")
        mg_in, mg_exp, mg_lf, mg_g, mg_gcols, mg_max = (
            sem("mg_in"), sem("mg_exp"), sem("mg_lf"), sem("mg_g"), sem("mg_gcols"), sem("mg_max"))
        ml_s, ml_mask, ml_e, ml_p, ml_o, ml_den, ml_h, ml_sums, ml_var, ml_std = (
            sem("ml_s"), sem("ml_mask"), sem("ml_e"), sem("ml_p"), sem("ml_o"), sem("ml_den"), sem("ml_h"),
            sem("ml_sums"), sem("ml_var"), sem("ml_std"))
        ml_sq = sem("ml_sq")
        rp_sums, rp_taken, rope_loaded = sem("rp_sums"), sem("rp_taken"), sem("rope_loaded")
        at_s, at_neg, at_e, at_p, at_turned, at_pt, at_o, at_done = (
            sem("at_s"), sem("at_neg"), sem("at_e"), sem("at_p"), sem("at_turned"), sem("at_pt"), sem("at_o"),
            sem("at_done"))

        XR, n = {}, 0
        for name, pairs in (("x", 8), ("p0", 1), ("y0", 8), ("h0", 8), ("h1", 8), ("p1", 1), ("y1", 8),
                            ("h2", 8), ("mem2", 8), ("x2", 8), ("cq", 2), ("ckv", 1), ("y2", 10),
                            ("x3", 8), ("mem3", 8), ("y3", 9)):
            XR[name] = n
            n += pairs
        NORMS, n = {}, 0
        for i, (name, pairs) in enumerate((("x", 8), ("ple0", 8), ("h1", 8), ("ple1", 8), ("first", 8), ("mem", 8),
                                           ("x2", 8), ("cq", 2), ("ckv", 1), ("x3", 8), ("last", 8))):
            NORMS[name] = (i, n, pairs)
            n += pairs
        STORED, n = {}, 0
        for name in ("ein", "ein_zb", "ogate", "oqk", "ov", "oog", "oz", "evkpe", "evc", "evmem", "uq", "ukv",
                     "evmoba", "odin", "odmem"):
            STORED[name] = n
            n += ST[name].pairs
        HR = {"gate0": 0, "gate1": 8, "x2": 16, "evout": 17, "odout": 25, "last": 33}

        class Steps:

            def __init__(self, eng, s):
                self.eng, self.s, self.n = eng, s, 0

            def post(self, ins):
                self.n = self.n + 1
                ins.then_inc(self.s, 1)

            def wait(self):
                self.eng.wait_ge(self.s, self.n)

            def __call__(self, ins):
                self.post(ins)
                self.wait()

        def pairs_loop(eng, count, body, first=0, steps=None, per=0):
            trips = (count - first) // 2
            if trips >= 2:
                n0 = steps.n if steps else 0
                with eng.Fori(0, trips) as i:
                    for k in range(2):
                        if steps:
                            steps.n = n0 + i * (2 * per) + k * per
                        body(i * 2 + (first + k), (first + k) % 2)
                if steps:
                    steps.n = n0 + trips * 2 * per
                first += 2 * trips
            for p in range(first, count):
                body(p, p % 2)

        def banks(st, par, nb=None):
            at = 2 * ((st.pair0 + par) % 2)
            return slice(at, at + (nb or st.nb))

        block = ctx.enter_context(nc.Block())

        @block.sync
        def _(sp):
            def load(st):
                wd = A["w_" + st.name]

                def pair(p, par):
                    at = 0
                    for q, cells in enumerate(st.units):
                        slot, n = q % RAW_SLOTS, len(cells) * P
                        before = st.unit0 + p * st.upp + q - RAW_SLOTS + 1
                        if not (isinstance(p, int) and before <= 0):
                            sp.wait_ge(lo_ready, before)
                        src = wd[p] if isinstance(p, int) else wd[ds(p, 1)].rearrange("o p c -> (o p) c")
                        sp.dma_start(raw[:, slot, 0:n], src[:, at:at + n]).then_inc(unit_loaded[slot], 16)
                        at += n

                if st.unit0 == 0:
                    pair(0, 0)
                pairs_loop(sp, st.pairs, pair, first=int(st.unit0 == 0))

            for name in [r[0] for r in stage_table()]:
                load(ST[name])
            sp.wait_ge(h_ready, HR["last"] + 1)
            sp.dma_start(out, h[:, :, :]).then_inc(out_stored, 16)
            sp.wait_ge(out_stored, 16)

        @block.gpsimd
        def _(pool):
            pool.wait_ge(ones_set, 1)

            def split(st):
                def pair(p, par):
                    for q, cells in enumerate(st.units):
                        slot, two, n = q % RAW_SLOTS, q % SPLIT_SLOTS, len(cells) * P
                        unit = st.unit0 + p * st.upp + q
                        turn = st.unit0 // RAW_SLOTS + p * (st.upp // RAW_SLOTS) + q // RAW_SLOTS
                        pool.wait_ge(unit_loaded[slot], turn * 16 + 16)
                        if not (isinstance(p, int) and unit < SPLIT_SLOTS):
                            pool.wait_ge(unit_used, unit - SPLIT_SLOTS + 1)
                        nc.gpsimd.tensor_tensor(w_hi[:, two, 0:n].rearrange("p (c s) -> p c s", s=P),
                                                raw[:, slot, 0:n].rearrange("p (c s) -> p c s", s=P),
                                                ones[:, :].unsqueeze(1).to_broadcast([P, n // P, P]),
                                                MUL).then_inc(hi_done, 1)
                        pool.wait_ge(hi_done, unit + 1)
                        nc.gpsimd.tensor_tensor(w_lo[:, two, 0:n], raw[:, slot, 0:n],
                                                w_hi[:, two, 0:n].bitcast(F32), SUB).then_inc(lo_ready, 1)

                if st.unit0 == 0:
                    pair(0, 0)
                pairs_loop(pool, st.pairs, pair, first=int(st.unit0 == 0))

            for name in [r[0] for r in stage_table()]:
                split(ST[name])

        @block.tensor
        def _(pe):
            mm = nc.tensor.matmul

            def product(st, p, par):
                x, x0 = X[st.x], 4 if st.name == "ukv" else 0
                pair = st.pair0 + p
                if not (isinstance(p, int) and pair < 2):
                    pe.wait_ge(pair_out, pair - 1)
                bank = banks(st, par).start
                for q, cells in enumerate(st.units):
                    pe.wait_ge(lo_ready, st.unit0 + p * st.upp + q + 1)
                    for c, (k, b) in enumerate(cells):
                        at = slice(c * P, c * P + P)
                        mm(ps[:, bank + b, :], w_hi[:, q % SPLIT_SLOTS, at], x[:, x0 + k, :],
                           start=(k == 0), stop=False)
                        ins = mm(ps[:, bank + b, 0:T], w_lo[:, q % SPLIT_SLOTS, at], x[:, x0 + k, 0:T],
                                 start=False, stop=(k == st.blocks - 1))
                    ins.then_inc(unit_used, 1)

            def products(name, first=0, count=None):
                st = ST[name]
                pairs_loop(pe, st.pairs if count is None else count, lambda p, par: product(st, p, par), first)

            def inputs(name, pairs):
                pe.wait_ge(x_ready, XR[name] + pairs)

            def sum_squares(name):
                i, at, pairs = NORMS[name]
                if i:
                    pe.wait_ge(var_ready, i)
                for j in range(pairs):
                    pe.wait_ge(sq_ready, at + j + 1)
                    for b in range(2):
                        ins = mm(ps[:, 7, 0:T], ones[:, :], sq[:, (at + j) % 2, b, :],
                                 start=(j == 0 and b == 0), stop=(j == pairs - 1 and b == 1))
                    ins.then_inc(sq_used, 1)

            turned = [0]

            def turn_values(name_blocks, buf, after_stored):
                pe.wait_ge(stored, after_stored)
                for k in range(0, len(name_blocks), 2):
                    n = turned[0]
                    if n >= 2:
                        pe.wait_ge(v_copied, n - 1)
                    for j, bl in enumerate(name_blocks[k:k + 2]):
                        for tt in range(2):
                            ins = nc.tensor.transpose(ps[:, 4 + n % 2, (2 * j + tt) * P:(2 * j + tt + 1) * P],
                                                      buf[:, bl, tt * P:(tt + 1) * P], ident[:, :])
                    ins.then_inc(v_turned, 1)
                    turned[0] += 1

            pe.wait_ge(consts_loaded, 16 * 6)
            pe.wait_ge(ones_set, 1)
            inputs("x", 8)
            products("ein", 0, 2)
            sum_squares("x")
            products("ein", 2)
            products("ein_zb")
            if upto < 1:
                return

            turn_values(range(16, 24), w, STORED["ein"] + 12)
            pe.wait_ge(v_copied, 4)
            for g in range(2):
                for level in range(9):
                    n = 9 * g + level
                    if level == 0:
                        pe.wait_ge(hg_qk, 2)
                        q_, k_ = w[:, 4 * g:4 * g + 4, :], ob[:, 8 + 4 * g:12 + 4 * g, :]
                    else:
                        pe.wait_ge(hg_lv_in, 8 * g + level)
                        q_, k_ = ob[:, 20:24, :], ob[:, 24:28, :]
                    if n:
                        pe.wait_ge(hg_masked, n)
                    for hd in range(4):
                        if level < 8:
                            for tt in range(2):
                                c = hd * T + tt * P
                                ins = mm(ps[:, 4 + c // 512, c % 512:c % 512 + P], k_[:, hd, tt * P:(tt + 1) * P],
                                         q_[:, hd, tt * P:(tt + 1) * P], start=True, stop=True)
                        else:
                            ins = mm(ps[:, 4, hd * P:(hd + 1) * P], k_[:, hd, 0:P], q_[:, hd, P:T],
                                     start=True, stop=True)
                    ins.then_inc(hg_lv_out, 1)
                pe.wait_ge(hg_masked, 9 * g + 9)
                a = ob[:, 28:34, :].rearrange("p a b -> p (a b)")
                if g:
                    pe.wait_ge(hg_ocopied, 2)
                for hd in range(4):
                    v = w[:, 16 + 4 * g + hd, :]
                    o = ps[:, 6 + hd // 2, (hd % 2) * T:(hd % 2 + 1) * T]
                    mm(o[:, 0:P], v[:, 0:P], a[:, hd * T:hd * T + P], start=True, stop=True)
                    mm(o[:, P:T], v[:, 0:P], a[:, 1024 + hd * P:1024 + hd * P + P], start=True, stop=False)
                    ins = mm(o[:, P:T], v[:, P:T], a[:, hd * T + P:hd * T + T], start=False, stop=True)
                ins.then_inc(hg_o, 1)
            for hd in range(8):
                if hd % 2 == 0:
                    pe.wait_ge(hg_ocopied, 4)
                    pe.wait_ge(hn_gate, hd // 2 + 1)
                ins = mm(ps[:, 4 + hd // 2, (hd % 2) * T:(hd % 2 + 1) * T], ones[:, :], ob[:, 16 + hd, :],
                         start=True, stop=True)
            ins.then_inc(hn_sums, 1)
            if upto < 2:
                return
            pe.wait_ge(lr_w, 32)
            pe.wait_ge(hn_var, 1)
            for n in range(8):
                pe.wait_ge(lr_conv, n + 1)
                if n >= 2:
                    pe.wait_ge(lr_act, 2 * n - 2)
                for j in range(2):
                    wt = ob[:, 16 + 4 * j:20 + 4 * j, :].rearrange("p a b -> p (a b)")
                    ins = mm(ps[:, 4 + n % 2, j * T:(j + 1) * T], wt[:, n * P:(n + 1) * P], ob[:, 8 + n, :],
                             start=True, stop=True)
                ins.then_inc(lr_pre, 1)
            if upto < 3:
                return

            def tail(l, x_y, x_h):
                inputs(f"p{l}", 1)
                products(f"ple{l}")
                sum_squares(f"ple{l}")
                inputs(x_y, 8)
                products("eout" if l == 0 else "oout")
                inputs(x_h, 8)
                products(f"gate{l}")

            tail(0, "y0", "h0")
            if upto < 4:
                return
            inputs("h1", 8)
            products("ogate")
            products("oqk", 0, 1)
            sum_squares("h1")
            products("oqk", 1)
            products("ov")
            products("oog")
            products("oz")
            if upto < 5:
                return
            pe.wait_ge(mg_lf, 1)
            gx, gb, gm = w[:, 32, :], w[:, 33, :], w[:, 34, :]
            mm(ps[:, 6, 0:T], gsel[:, 0, :], gx, start=True, stop=False)
            mm(ps[:, 6, 0:T], gsel[:, 1, :], gb, start=False, stop=True).then_inc(mg_g, 1)
            for st_ in range(2):
                c = slice(8 * st_, 8 * st_ + 8)
                mm(ps[:, 7, c], gx[:, st_ * P:(st_ + 1) * P], gsel[:, 0, 0:8], start=True, stop=False)
                ins = mm(ps[:, 7, c], gb[:, st_ * P:(st_ + 1) * P], gsel[:, 1, 0:8], start=False, stop=True)
            ins.then_inc(mg_g, 1)
            turn_values(range(16, 32), w, STORED["ov"] + 8)
            pe.wait_ge(v_copied, 12)
            pe.wait_ge(cv_done, 16)
            pe.wait_ge(mg_max, 1)
            pe.wait_ge(mg_gcols, 1)

            def ml_scores(hd):
                if hd:
                    pe.wait_ge(ml_p, hd)
                    pe.wait_ge(ml_den, hd)
                for kt in range(2):
                    mm(ps[:, 4, kt * T:(kt + 1) * T], w[:, 8 + hd, kt * P:(kt + 1) * P], w[:, hd, :],
                       start=True, stop=True)
                one_m = ident[:, hd:hd + 1].to_broadcast([P, P])
                one_b = ident[:, ROW_F + hd:ROW_F + hd + 1].to_broadcast([P, P])
                mm(ps[:, 5, 0:T], one_m, gm, start=True, stop=True)
                mm(ps[:, 5, T:2 * T], one_m, gm, start=True, stop=False)
                mm(ps[:, 5, T:2 * T], one_b, gb, start=False, stop=True).then_inc(ml_s, 1)

            for hd in range(8):
                ml_scores(hd)
                pe.wait_ge(ml_p, hd + 1)
                if hd:
                    pe.wait_ge(ml_h, hd)
                for eb in range(2):
                    for kt in range(2):
                        mm(ps[:, 6, eb * T:(eb + 1) * T], w[:, 16 + 2 * hd + eb, kt * P:(kt + 1) * P],
                           pt[:, 0, kt, :], start=(kt == 0), stop=(kt == 1))
                if hd:
                    pe.wait_ge(ml_var, hd)
                for kt in range(2):
                    ins = mm(ps[:, 7, 0:T], ones[:, :], pt[:, 0, kt, :], start=(kt == 0), stop=(kt == 1))
                ins.then_inc(ml_o, 1)
                pe.wait_ge(ml_sq, hd + 1)
                for eb in range(2):
                    ins = mm(ps[:, 7, T:2 * T], ones[:, :], pt[:, 1, eb, :], start=(eb == 0), stop=(eb == 1))
                ins.then_inc(ml_sums, 1)
            if upto < 6:
                return
            tail(1, "y1", "h2")
            if upto < 7:
                return
            sum_squares("first")
            sum_squares("mem")
            inputs("x2", 8)
            products("evkpe")
            products("evc", 0, 1)
            sum_squares("x2")
            products("evc", 1)
            inputs("mem2", 8)
            products("evmem")
            sum_squares("cq")
            sum_squares("ckv")
            inputs("cq", 2)
            products("uq")
            inputs("ckv", 1)
            products("ukv")
            if upto < 8:
                return

            rotated = [0]

            def rotate(blocks, kind, after_stored):
                pe.wait_ge(stored, after_stored)
                for k in range(0, len(blocks), 2):
                    n = rotated[0]
                    if n >= 2:
                        pe.wait_ge(rp_taken, n - 1)
                    for j, bl in enumerate(blocks[k:k + 2]):
                        ins = mm(ps[:, 6 + n % 2, j * T:(j + 1) * T], rot[:, kind, :], w[:, bl, :],
                                 start=True, stop=True)
                    ins.then_inc(rp_sums, 1)
                    rotated[0] += 1

            def scores(heads, a):
                for i, hd in enumerate(heads):
                    if a + i >= 2:
                        pe.wait_ge(at_done, a + i - 1)
                    for qt in range(2):
                        qs = slice(qt * P, (qt + 1) * P)
                        parts = hd["qk"]
                        for j, (qb_, kb_, p0, pn) in enumerate(parts):
                            ins = mm(ps[:, 4 + i, qt * T:(qt + 1) * T], w[p0:p0 + pn, qb_, qs], w[p0:p0 + pn, kb_, :],
                                     start=(j == 0), stop=(j == len(parts) - 1))
                    ins.then_inc(at_s, 1)

            def outputs(heads, a):
                for i in range(len(heads)):
                    pe.wait_ge(at_p, a + i + 1)
                    if a + i >= 2:
                        pe.wait_ge(at_pt, a + i - 1)
                    for qt in range(2):
                        for kt in range(2):
                            ins = nc.tensor.transpose(ps[:, 6 + i, kt * T + qt * P:kt * T + (qt + 1) * P],
                                                      sm[:, i, qt, kt * P:(kt + 1) * P], ident[:, :])
                    ins.then_inc(at_turned, 1)
                for i, hd in enumerate(heads):
                    pe.wait_ge(at_pt, a + i + 1)
                    vb, v0, vn, p0 = hd["v"]
                    for kt in range(2):
                        ins = mm(ps[p0:p0 + vn, 4 + i, 0:T], w[:, vb, kt * P + v0:kt * P + v0 + vn], pt[:, i, kt, :],
                                 start=(kt == 0), stop=(kt == 1))
                    ins.then_inc(at_o, 1)

            def attend(couples, gate, a):
                scores(couples[0], a)
                p = 0
                for c, heads in enumerate(couples):
                    outputs(heads, a + 2 * c)
                    if c + 1 < len(couples):
                        scores(couples[c + 1], a + 2 * c + 2)
                    if heads[-1]["gate"] is not None:
                        product(ST[gate], p, p % 2)
                        p += 1

            rotate(MLA_ROPE, 0, STORED["uq"] + 6)
            turn_values(MLA_V, w, STORED["ukv"] + 8)
            pe.wait_ge(rp_taken, rotated[0])
            pe.wait_ge(v_copied, turned[0])
            attend(MLA_COUPLES, "evgate_a", 0)
            products("evmoba")
            rotate(MOBA_ROPE, 1, STORED["evmoba"] + 14)
            turn_values(MOBA_V, w, STORED["evmoba"] + 14)
            pe.wait_ge(rp_taken, rotated[0])
            pe.wait_ge(v_copied, turned[0])
            attend(MOBA_COUPLES, "evgate_b", 8)
            inputs("y2", 10)
            products("evout")
            if upto < 9:
                return
            inputs("x3", 8)
            products("odin", 0, 2)
            sum_squares("x3")
            products("odin", 2)
            inputs("mem3", 8)
            products("odmem")
            pe.wait_ge(rope_loaded, 32 * 2)
            rotate(SWA_ROPE, 0, STORED["odin"] + 16)
            rotate(DIL_ROPE, 1, STORED["odin"] + 16)
            turn_values(OD_V, w, STORED["odmem"] + 4)
            pe.wait_ge(rp_taken, rotated[0])
            pe.wait_ge(v_copied, turned[0])
            attend(OD_COUPLES, "odgate", 20)
            inputs("y3", 9)
            products("odout")
            sum_squares("last")

        @block.scalar
        def _(act):
            step = Steps(act, act_step)
            af = nc.scalar.activation

            for buf, name, s in ((cols, "cols", cols_loaded), (h, "x", x_loaded)):
                act.dma_start(buf[:], A[name]).then_inc(s, 16)
            for buf, name in ((ident, "ident"), (gsel, "gsel"), (masks, "masks"), (ob[:, 36:40, :], "lvl"),
                              (rope, "rope_ev"), (rot, "rot_ev")):
                act.dma_start(buf if name == "lvl" else buf[:], A[name]).then_inc(consts_loaded, 16)

            def stream(n, src, wait=True):
                if wait and n >= 2:
                    act.wait_ge(stream_split, n - 1)
                act.dma_start(sm[:, n % 2, :, :], src).then_inc(stream_loaded[n % 2], 16)

            def crossed(st, p, par):
                pair = st.pair0 + p
                act.wait_ge(unit_used, st.unit0 + p * st.upp + st.upp)
                if not (isinstance(p, int) and pair < 2):
                    act.wait_ge(pair_out, pair - 1)
                af(cross[:, (st.pair0 + par) % 2, 0:st.nb, :], ps[:, banks(st, par), T:2 * T],
                   ACT.Copy).then_inc(cross_ready, 1)

            def cross_all(name, first=0, count=None):
                st = ST[name]
                pairs_loop(act, st.pairs if count is None else count, lambda p, par: crossed(st, p, par), first)

            def squares(name, src, ready):
                i, at, pairs = NORMS[name]
                for j in range(pairs):
                    if ready:
                        s, base, each = ready
                        act.wait_ge(s, base + (j + 1) * each if each else base)
                    if at + j >= 2:
                        act.wait_ge(sq_used, at + j - 1)
                    af(sq[:, (at + j) % 2, :, :], src(j), ACT.Square).then_inc(sq_ready, 1)

            def root(name, which):
                i = NORMS[name][0]
                act.wait_ge(var_ready, i + 1)
                af(rs[:, which, :], tb[:, 0, :], ACT.Sqrt).then_inc(std_ready, 1)

            copied = [0]

            def copy_values(blocks, buf):
                for k in range(0, len(blocks), 2):
                    n = copied[0]
                    act.wait_ge(v_turned, n + 1)
                    nb = len(blocks[k:k + 2])
                    if nb == 2 and blocks[k + 1] != blocks[k] + 1:
                        for j in range(2):
                            ins = af(buf[:, blocks[k + j], :], ps[:, 4 + n % 2, j * T:(j + 1) * T], ACT.Copy)
                            if j == 0:
                                step.post(ins)
                    else:
                        ins = af(buf[:, blocks[k]:blocks[k] + nb, :].rearrange("p a b -> p (a b)"),
                                 ps[:, 4 + n % 2, 0:nb * T], ACT.Copy)
                    ins.then_inc(v_copied, 1)
                    copied[0] += 1

            act.wait_ge(par_in, 1)
            af(small[:, 0:24], small[:, 0:24], ACT.Exp).then_inc(par_exp, 1)
            act.wait_ge(x_loaded, 16)
            squares("x", lambda j: h[:, 2 * j:2 * j + 2, :], None)
            root("x", RS_LAYER)
            stream(0, A["p"][0])
            cross_all("ein", 0, 2)
            cross_all("ein", 2)
            cross_all("ein_zb")
            if upto < 1:
                return
            act.wait_ge(stored, STORED["ein"] + 12)
            act.wait_ge(par_done, 1)
            sg = ob[:, 16:24, :]
            af(sg, w[:, 0:8, :], ACT.Sigmoid).then_inc(hg_sig, 1)
            af(ob[:, 8:16, :], w[:, 8:16, :], ACT.Sigmoid, scale=-1.0).then_inc(hg_sig, 1)
            act.wait_ge(hg_q, 1)
            af(sg, w[:, 8:16, :], ACT.Sigmoid).then_inc(hg_sig, 1)
            act.wait_ge(hg_sig, 3)
            for hd in range(8):
                af(w[:, 8 + hd, :], ob[:, 16 + hd, :], ACT.Ln, bias=small[:, 24 + hd:25 + hd],
                   scale=small[:, 32 + hd:33 + hd]).then_inc(hg_logf, 1)
            copy_values(range(16, 24), w)
            for g in range(2):
                for level in range(1, 9):
                    n = 8 * g + level
                    e = ob[:, 16:20, :] if level % 2 else ob[:, 34:38, :]
                    act.wait_ge(hg_diff, n)
                    af(e, e, ACT.Exp).then_inc(hg_exp, 1)
                act.wait_ge(hg_o, g + 1)
                for k in range(2):
                    af(w[:, 4 * g + 2 * k:4 * g + 2 * k + 2, :].rearrange("p a b -> p (a b)"), ps[:, 6 + k, :],
                       ACT.Copy).then_inc(hg_ocopied, 1)
            act.wait_ge(hg_ocopied, 4)
            for k in range(4):
                af(ob[:, 16 + 2 * k:18 + 2 * k, :], w[:, 2 * k:2 * k + 2, :], ACT.Square).then_inc(hn_gate, 1)
            act.wait_ge(stored, STORED["ein_zb"] + 4)
            af(ob[:, 24:32, :], w[:, 24:32, :], ACT.Sigmoid).then_inc(hn_gate, 1)
            act.wait_ge(hn_var, 1)
            af(ob[:, 16:24, :], ob[:, 32:40, :], ACT.Sqrt).then_inc(hn_std, 1)
            if upto < 2:
                return
            act.wait_ge(hn_gate, 6)
            for j, name in enumerate(("w_r", "w_i")):
                act.dma_start(ob[:, 16 + 4 * j:20 + 4 * j, :].rearrange("p a b -> p (a b)"), A[name]).then_inc(lr_w, 16)
            for n in range(8):
                act.wait_ge(lr_pre, n + 1)
                for j, b in enumerate(("b_b_r", "b_b_i")):
                    af(w[:, 8 + 8 * j + n, :], ps[:, 4 + n % 2, j * T:(j + 1) * T], ACT.Sigmoid,
                       bias=col(b, 1, n)).then_inc(lr_act, 1)
            act.wait_ge(lr_act, 16)
            for n in range(8):
                af(ob[:, 24 + n, :], w[:, 8 + n, :], ACT.Tanh, scale=small[:, 40 + n:41 + n]).then_inc(lr_th, 1)
            for n in range(8):
                af(ob[:, 16 + n, :], w[:, 8 + n, :], ACT.Exp, scale=small[:, 48 + n:49 + n]).then_inc(lr_th, 1)
            act.wait_ge(lr_fix, 1)
            af(ob[:, 24:32, :], ob[:, 24:32, :], ACT.Sqrt, scale=2.0).then_inc(lr_root, 1)
            act.wait_ge(lr_fix, 2)
            af(ob[:, 32:40, :], ob[:, 0:8, :], ACT.Sigmoid).then_inc(lr_root, 1)
            if upto < 3:
                return

            def tail(l):
                pl = [w[:, 16 + 2 * j:18 + 2 * j, :] for j in range(8)]
                cross_all(f"ple{l}")
                squares(f"ple{l}", lambda j: pl[j], (pair_out, ST[f"ple{l}"].pair0, 1))
                root(f"ple{l}", RS_PLE)
                cross_all("eout" if l == 0 else "oout")
                st = ST[f"gate{l}"]

                def pair(p, par):
                    crossed(st, p, par)
                    act.wait_ge(g_pre, 8 * l + p + 1)
                    af(tb[:, :, :], tb[:, :, :], ACT.Sigmoid).then_inc(g_sig, 1)

                pairs_loop(act, 8, pair)

            tail(0)
            if upto < 4:
                return
            squares("h1", lambda j: h[:, 2 * j:2 * j + 2, :], (h_ready, HR["gate0"] + 8, 0))
            root("h1", RS_LAYER)
            cross_all("ogate")
            cross_all("oqk")
            cross_all("ov")
            cross_all("oog")
            cross_all("oz")
            if upto < 5:
                return
            act.wait_ge(mg_in, 1)
            af(w[:, 36, :], w[:, 36, :], ACT.Exp, scale=-1.0).then_inc(mg_exp, 1)
            for n in range(16):
                act.wait_ge(cv_pre, n + 1)
                if n >= 2:
                    act.wait_ge(cv_done, n - 1)
                af(sm[:, n % 2, 0, :], w[:, 38 + n % 2, :], ACT.Sigmoid).then_inc(cv_sig, 1)
            act.wait_ge(mg_g, 2)
            af(small[:, 0:16], ps[:, 7, 0:16], ACT.Copy).then_inc(mg_gcols, 1)
            copy_values(range(16, 32), w)
            act.wait_ge(mg_gcols, 1)
            act.wait_ge(cv_done, 16)
            for hd in range(8):
                act.wait_ge(ml_mask, hd + 1)
                for kt in range(2):
                    af(sm[:, 0, kt, :], sm[:, 0, kt, :], ACT.Exp, scale=-1.0,
                       bias=small[:, 8 * kt + hd:8 * kt + hd + 1]).then_inc(ml_e, 1)
                act.wait_ge(ml_s, hd + 1)
                if hd:
                    act.wait_ge(ml_den, hd)
                af(w[:, 40, :], ps[:, 5, T:2 * T], ACT.Exp, scale=-1.0).then_inc(ml_e, 1)
                act.wait_ge(ml_o, hd + 1)
                af(w[:, 41, :], ps[:, 7, 0:T], ACT.Abs).then_inc(ml_e, 1)
                act.wait_ge(ml_h, hd + 1)
                if hd:
                    act.wait_ge(ml_sums, hd)
                af(pt[:, 1, :, :], w[:, 16 + 2 * hd:18 + 2 * hd, :], ACT.Square).then_inc(ml_sq, 1)
                act.wait_ge(ml_var, hd + 1)
                af(w[:, 41, :], w[:, 42, :], ACT.Sqrt).then_inc(ml_std, 1)
            act.wait_ge(stored, STORED["oz"] + 8)
            af(w[:, 0:16, :], oa[:, 0:16, :], ACT.Sigmoid).then_inc(y_gate, 1)
            act.wait_ge(y_done, 1)
            af(w[:, 0:16, :], oa[:, 16:32, :], ACT.Sigmoid).then_inc(y_gate, 1)
            act.wait_ge(ml_std, 8)
            stream(1, A["p"][1])
            if upto < 6:
                return
            tail(1)
            if upto < 7:
                return
            squares("first", lambda j: h[:, 2 * j:2 * j + 2, :], (h_ready, HR["gate1"] + 8, 0))
            root("first", RS_LAYER)
            i, at, pairs = NORMS["mem"]
            for j in range(pairs):
                stream(2 + j, A["mem"][j])
                act.wait_ge(stream_loaded[j % 2], 16 * (2 + j // 2))
                if at + j >= 2:
                    act.wait_ge(sq_used, at + j - 1)
                af(sq[:, (at + j) % 2, :, :], sm[:, j % 2, :, :], ACT.Square).then_inc(sq_ready, 1)
                act.wait_ge(sq_ready, at + j + 1)
            root("mem", RS_MEM)
            squares("x2", lambda j: h[:, 2 * j:2 * j + 2, :], (h_ready, HR["x2"] + 1, 0))
            root("x2", RS_LAYER)
            cross_all("evkpe")
            cross_all("evc")
            cross_all("evmem")
            squares("cq", lambda j: w[:, 29 + 2 * j:31 + 2 * j, :], (stored, STORED["evc"] + 3, 0))
            squares("ckv", lambda j: w[:, 33:35, :], None)
            root("cq", RS_Q)
            root("ckv", RS_KV)
            cross_all("uq")
            cross_all("ukv")
            if upto < 8:
                return

            def exps(heads, a):
                for i, hd in enumerate(heads):
                    act.wait_ge(at_neg, a + i + 1)
                    s4 = small[:, 16 * i:16 * i + 16]
                    for qt in range(2):
                        ins = af(sm[:, i, qt, :], sm[:, i, qt, :], ACT.Exp, bias=s4[:, qt:qt + 1],
                                 accum_out=s4[:, 2 + qt:3 + qt])
                        if qt == 0 or hd["sink"] is not None:
                            step.post(ins)
                    if hd["sink"] is not None:
                        ins = af(s4[:, 4:6], s4[:, 0:2], ACT.Exp, bias=col("sinks", 1, hd["sink"]))
                    ins.then_inc(at_e, 1)

            def turned_copy(heads, a):
                for i in range(len(heads)):
                    act.wait_ge(at_turned, a + i + 1)
                    af(pt[:, i, :, :].rearrange("p a b -> p (a b)"), ps[:, 6 + i, :], ACT.Copy).then_inc(at_pt, 1)

            gates = [16]

            def gated(st, p):
                crossed(st, p, p % 2)
                act.wait_ge(g_pre, gates[0] + 1)
                af(cross[:, (st.pair0 + p) % 2, :, :], tb[:, :, :], ACT.Sigmoid).then_inc(g_sig, 1)
                gates[0] += 1

            def attend(couples, gate, a):
                p, due = 0, False
                for c, heads in enumerate(couples):
                    exps(heads, a + 2 * c)
                    if due:
                        gated(ST[gate], p)
                        p += 1
                    turned_copy(heads, a + 2 * c)
                    due = heads[-1]["gate"] is not None
                gated(ST[gate], p)

            copy_values(MLA_V, w)
            attend(MLA_COUPLES, "evgate_a", 0)
            cross_all("evmoba")
            copy_values(MOBA_V, w)
            attend(MOBA_COUPLES, "evgate_b", 8)
            act.wait_ge(at_done, 20)
            for buf, name in ((rope, "rope_od"), (rot, "rot_od")):
                act.dma_start(buf[:], A[name]).then_inc(rope_loaded, 32)
            cross_all("evout")
            if upto < 9:
                return
            squares("x3", lambda j: h[:, 2 * j:2 * j + 2, :], (h_ready, HR["evout"] + 8, 0))
            root("x3", RS_LAYER)
            for j in range(8):
                stream(10 + j, A["mem"][j])
            cross_all("odin")
            cross_all("odmem")
            copy_values(OD_V, w)
            attend(OD_COUPLES, "odgate", 20)
            cross_all("odout")
            squares("last", lambda j: h[:, 2 * j:2 * j + 2, :], (h_ready, HR["odout"] + 8, 0))
            root("last", RS_LAYER)

        @block.vector
        def _(dve):
            step = Steps(dve, dve_step)
            tt, ts, stt, cp = (nc.vector.tensor_tensor, nc.vector.tensor_scalar, nc.vector.scalar_tensor_tensor,
                               nc.vector.tensor_copy)

            def split(src, gain, x, kt, count):
                if gain is not None:
                    step(tt(tb[:, :, :], src, wide(gain, 2), MUL))
                    src = tb[:, :, :]
                hi = x[:, ds(kt, 2), 0:T]
                step(cp(hi, src))
                tt(x[:, ds(kt, 2), T:2 * T], src, hi.bitcast(F32), SUB).then_inc(x_ready, 1)
                dve.wait_ge(x_ready, count)

            def take(st, p, par, dst):
                pair = st.pair0 + p
                dve.wait_ge(cross_ready, pair + 1)
                tt(dst, ps[:, banks(st, par), 0:T], cross[:, (st.pair0 + par) % 2, 0:st.nb, :],
                   ADD).then_inc(pair_out, 1)
                dve.wait_ge(pair_out, pair + 1)

            def store(name, buf, at, scale, first=0, count=None):
                st = ST[name]

                def pair(p, par):
                    dst = buf[:, ds(p * st.nb + at, st.nb), :]
                    take(st, p, par, dst)
                    tt(dst, dst, along(rs[:, scale, :], st.nb), MUL).then_inc(stored, 1)

                pairs_loop(dve, st.pairs if count is None else count, pair, first)
                dve.wait_ge(stored, STORED[name] + (st.pairs if count is None else count))

            def root(name, which, width):
                i, at, pairs = NORMS[name]
                dve.wait_ge(sq_used, at + pairs)
                ts(tb[:, 0, :], ps[:, 7, 0:T], 1.0 / width, EPS, MUL, ADD).then_inc(var_ready, 1)
                dve.wait_ge(std_ready, i + 1)
                inverse(rs[:, which, :], tb[:, 0, :], tb[:, 1, :])

            def inverse(r, v, t):
                step(nc.vector.reciprocal(r, r))
                step(tt(t, r, r, MUL))
                step(tt(t, t, v, MUL))
                step(ts(t, t, -0.5, 1.5, MUL, ADD))
                step(tt(r, r, t, MUL))

            def log1p(y, z, zz, p):
                step(ts(z, y, 2.0, None, ADD))
                step(nc.vector.reciprocal(z, z))
                step(tt(z, z, y, MUL))
                step(tt(zz, z, z, MUL))
                step(ts(p, zz, 1.0 / 21, None, MUL))
                for k in range(9, 0, -1):
                    step(stt(p, p, 1.0 / (2 * k + 1), zz, ADD, MUL))
                step(stt(p, p, 1.0, z, ADD, MUL))
                step(ts(p, p, 2.0, None, MUL))

            nc.vector.memset(ones[:, :], 1.0).then_inc(ones_set, 1)
            dve.wait_ge(consts_loaded, 16 * 6)
            step(cp(lvl[:, :, :].rearrange("p a b -> p (a b)"), ob[:, 36:40, :].rearrange("p a b -> p (a b)")))
            dve.wait_ge(cols_loaded, 16)
            l0, l1, lam = col("a_lb0"), col("a_lb1"), col("b_lambda")
            step(tt(small[:, 24:32], l0, l1, MAX))
            step(tt(small[:, 0:8], l0, small[:, 24:32], SUB))
            step(tt(small[:, 8:16], l1, small[:, 24:32], SUB))
            step(stt(small[:, 40:48], lam, -1.0, lam, MUL, MAX))
            ts(small[:, 16:24], small[:, 40:48], -1.0, None, MUL).then_inc(par_in, 1)
            dve.wait_ge(par_exp, 1)
            step(tt(small[:, 8:16], small[:, 0:8], small[:, 8:16], ADD))
            step(nc.vector.reciprocal(small[:, 8:16], small[:, 8:16]))
            step(tt(small[:, 24:32], small[:, 0:8], small[:, 8:16], MUL))
            step(ts(small[:, 32:40], small[:, 24:32], -1.0, 1.0, MUL, ADD))
            log1p(small[:, 16:24], small[:, 0:8], small[:, 8:16], small[:, 40:48])
            step(ts(small[:, 0:8], lam, -1.0, 0.0, MUL, MAX))
            step(tt(small[:, 40:48], small[:, 40:48], small[:, 0:8], ADD))
            step(ts(small[:, 40:48], small[:, 40:48], 8.0, None, MUL))
            ts(small[:, 48:56], small[:, 40:48], -1.0, None, MUL).then_inc(par_done, 1)
            lb, oml = small[:, 24:32], small[:, 32:40]
            dve.wait_ge(x_loaded, 16)
            for j in range(8):
                split(h[:, 2 * j:2 * j + 2, :], col("e_norm", 2, 2 * j), xa, 2 * j, XR["x"] + j + 1)
            root("x", RS_LAYER, D)
            dve.wait_ge(stream_loaded[0], 16)
            split(sm[:, 0, :, :], None, xs, 0, XR["p0"] + 1)
            cp(small[:, 63:64], ones[:, 0:1]).then_inc(stream_split, 1)
            store("ein", w, 0, RS_LAYER)
            store("ein_zb", ob, 0, RS_LAYER)
            if upto < 1:
                return
            dve.wait_ge(par_done, 1)
            dve.wait_ge(hg_sig, 1)
            q, kk = w[:, 0:8, :], ob[:, 8:16, :]
            tt(q, q, ob[:, 16:24, :], MUL).then_inc(hg_q, 1)
            dve.wait_ge(hg_sig, 2)
            tt(kk, kk, wide(oml, 8), MUL).then_inc(hg_qk, 1)
            for hd in range(8):
                dve.wait_ge(hg_logf, hd + 1)
                for c in range(4):
                    bc = w[:, 8 + hd, 64 * c:64 * c + 64]
                    step.post(nc.vector.tensor_tensor_scan(bc, ones[:, 0:64], bc, 0.0, MUL, ADD))
            cp(small[:, 62:63], ones[:, 0:1]).then_inc(hg_qk, 1)
            step.wait()
            dve.wait_ge(hg_q, 1)
            dve.wait_ge(hg_qk, 2)
            dve.wait_ge(hg_logf, 8)
            am = ob[:, 28:34, :].rearrange("p a b -> p (a b)")

            for g in range(2):
                qg, kg = w[:, 4 * g:4 * g + 4, :], ob[:, 8 + 4 * g:12 + 4 * g, :]
                b = w[:, 8 + 4 * g:12 + 4 * g, :].rearrange("p a b -> p (a b)")

                def differences(level):
                    e = (ob[:, 16:20, :] if level % 2 else ob[:, 34:38, :]).rearrange("p a b -> p (a b)")
                    size = 2 ** level
                    half = size // 2
                    ev = e.rearrange("p (n s) -> p n s", s=size)
                    bv = b.rearrange("p (n s) -> p n s", s=size)
                    n = 1024 // size
                    if level <= 6:
                        mid = bv[:, :, half - 1:half].to_broadcast([P, n, half])
                        step.post(tt(ev[:, :, half:size], bv[:, :, half:size], mid, SUB))
                        ins = tt(ev[:, :, 0:half], mid, bv[:, :, 0:half], SUB)
                    elif level == 7:
                        step.post(cp(ev[:, :, 64:128], bv[:, :, 64:128]))
                        ins = tt(ev[:, :, 0:64], bv[:, :, 63:64].to_broadcast([P, n, 64]), bv[:, :, 0:64], SUB)
                    else:
                        def last(c):
                            return bv[:, :, 64 * c + 63:64 * c + 64].to_broadcast([P, n, 64])

                        step.post(cp(ev[:, :, 128:192], bv[:, :, 128:192]))
                        step.post(tt(ev[:, :, 192:256], bv[:, :, 192:256], last(2), ADD))
                        step.post(tt(ev[:, :, 64:128], last(1), bv[:, :, 64:128], SUB))
                        step(tt(ev[:, :, 0:64], last(0), bv[:, :, 0:64], SUB))
                        ins = tt(ev[:, :, 0:64], ev[:, :, 0:64], last(1), ADD)
                    ins.then_inc(hg_diff, 1)

                def scaled(level):
                    e = ob[:, 16:20, :] if level % 2 else ob[:, 34:38, :]
                    dve.wait_ge(hg_exp, 8 * g + level)
                    if level > 1:
                        dve.wait_ge(hg_lv_out, 9 * g + level)
                    elif g:
                        dve.wait_ge(hg_lv_out, 9)
                    step.post(tt(ob[:, 20:24, :], qg, e, MUL))
                    tt(ob[:, 24:28, :], kg, e, MUL).then_inc(hg_lv_in, 1)
                    dve.wait_ge(hg_lv_in, 8 * g + level)

                def masked(level):
                    n = 9 * g + level
                    dve.wait_ge(hg_lv_out, n + 1)
                    if level < 8:
                        nc.vector.copy_predicated(
                            am[:, 0:1024].rearrange("p (n s) -> p n s", s=P),
                            lvl[:, level, :].unsqueeze(1).to_broadcast([P, 8, P]),
                            ps[:, 4:6, :].rearrange("p a b -> p (a b)").rearrange("p (n s) -> p n s", s=P),
                        ).then_inc(hg_masked, 1)
                    else:
                        cp(am[:, 1024:1536], ps[:, 4, :]).then_inc(hg_masked, 1)
                    dve.wait_ge(hg_masked, n + 1)

                if g:
                    dve.wait_ge(hg_o, 1)
                dve.wait_ge(consts_loaded, 16 * 6)
                step(nc.vector.memset(am[:, 0:1024], 0.0))
                differences(1)
                masked(0)
                for level in range(1, 9):
                    if level < 8:
                        differences(level + 1)
                    scaled(level)
                    masked(level)
            dve.wait_ge(hn_sums, 1)
            rh = ob[:, 32:40, :]
            ts(rh.rearrange("p a b -> p (a b)"), ps[:, 4:8, :].rearrange("p a b -> p (a b)"), 1.0 / P, EPS, MUL,
               ADD).then_inc(hn_var, 1)
            ya, z = w[:, 0:8, :], w[:, 24:32, :]
            dve.wait_ge(hn_gate, 5)
            step(tt(z, z, ob[:, 24:32, :], MUL))
            step(tt(z, z, wide(col("a_norm"), 8), MUL))
            dve.wait_ge(hg_ocopied, 4)
            step(tt(ya, ya, z, MUL))
            dve.wait_ge(hn_std, 1)
            inverse(ob[:, 16:24, :], rh, ob[:, 24:32, :])
            step(tt(ya, ya, ob[:, 16:24, :], MUL))
            cp(small[:, 61:62], ones[:, 0:1]).then_inc(hn_gate, 1)
            if upto < 2:
                return
            for n in range(8):
                xb_, xc = w[:, 32 + n, :], ob[:, 8 + n, :]

                def tap(k):
                    return col("b_conv_w", 1, 8 * k + n)

                step(ts(xc, xb_, tap(3), col("b_conv_b", 1, n), MUL, ADD))
                for k in (2, 1):
                    s = 3 - k
                    step(stt(xc[:, s:T], xb_[:, 0:T - s], tap(k), xc[:, s:T], MUL, ADD))
                stt(xc[:, 3:T], xb_[:, 0:T - 3], tap(0), xc[:, 3:T], MUL, ADD).then_inc(lr_conv, 1)
            dve.wait_ge(lr_conv, 8)
            th, t1, ig, xc = ob[:, 24:32, :], ob[:, 32:40, :], w[:, 16:24, :], ob[:, 8:16, :]
            dve.wait_ge(lr_act, 16)
            step(tt(ig, ig, xc, MUL))
            dve.wait_ge(lr_th, 8)
            step(ts(t1, th, 1.0, None, ADD))
            step(nc.vector.reciprocal(t1, t1))
            tt(th, th, t1, MUL).then_inc(lr_fix, 1)
            dve.wait_ge(lr_root, 1)
            step(tt(ig, ig, th, MUL))
            dve.wait_ge(lr_th, 16)
            for n in range(8):
                step.post(nc.vector.tensor_tensor_scan(ob[:, 8 + n, :], ob[:, 16 + n, :], w[:, 16 + n, :], 0.0, MUL, ADD))
            cp(small[:, 60:61], ones[:, 0:1]).then_inc(lr_fix, 1)
            step.wait()
            yb, zb = w[:, 8:16, :], ob[:, 0:8, :]
            dve.wait_ge(lr_root, 2)
            step(tt(zb, zb, t1, MUL))
            step(tt(yb, ob[:, 8:16, :], zb, MUL))
            for j in range(8):
                split(w[:, 2 * j:2 * j + 2, :], None, xb, 2 * j, XR["y0"] + j + 1)
            if upto < 3:
                return

            def tail(l, x_out, x_h, x_next, gain_next, x_next_buf):
                st = ST[f"ple{l}"]
                pairs_loop(dve, 8, lambda p, par: take(st, p, par, w[:, ds(p * 2 + 16, 2), :]))
                root(f"ple{l}", RS_PLE, D)
                pl = w[:, 16:32, :]
                step(tt(pl, pl, along(rs[:, RS_PLE, :], 16), MUL))
                step(tt(pl, pl, wide(col(f"ple_norm{l}"), 16), MUL))
                so, xo = ST["eout" if l == 0 else "oout"], X[ST[f"gate{l}"].x]

                def out_pair(p, par):
                    hp = h[:, ds(p * 2, 2), :]
                    take(so, p, par, tb[:, :, :])
                    step(tt(hp, hp, tb[:, :, :], ADD))
                    split(hp, None, xo, p * 2, p + (XR[x_h] + 1))

                pairs_loop(dve, 8, out_pair, steps=step, per=2)
                sg = ST[f"gate{l}"]

                def gate_pair(p, par):
                    hp = h[:, ds(p * 2, 2), :]
                    pair = sg.pair0 + p
                    dve.wait_ge(cross_ready, pair + 1)
                    step(tt(tb[:, :, :], ps[:, banks(sg, par), 0:T], cross[:, (sg.pair0 + par) % 2, :, :], ADD))
                    cp(small[:, 59:60], ones[:, 0:1]).then_inc(pair_out, 1)
                    dve.wait_ge(pair_out, pair + 1)
                    cp(small[:, 58:59], ones[:, 0:1]).then_inc(g_pre, 1)
                    dve.wait_ge(g_sig, p + (8 * l + 1))
                    step(tt(tb[:, :, :], tb[:, :, :], w[:, ds(p * 2 + 16, 2), :], MUL))
                    tt(hp, hp, tb[:, :, :], ADD).then_inc(h_ready, 1)
                    dve.wait_ge(h_ready, p + (HR[f"gate{l}"] + 1))
                    if x_next:
                        split(hp, col(gain_next, 2, p * 2), x_next_buf, p * 2, p + (XR[x_next] + 1))

                pairs_loop(dve, 8, gate_pair, steps=step, per=4 if x_next else 2)

            tail(0, "eout", "h0", "h1", "o_norm", xb)
            if upto < 4:
                return
            root("h1", RS_LAYER, D)
            store("ogate", w, 32, RS_LAYER)
            store("oqk", w, 0, RS_LAYER)
            store("ov", w, 16, RS_LAYER)
            store("oog", oa, 0, RS_LAYER)
            store("oz", oa, 16, RS_LAYER)
            if upto < 5:
                return
            gx, gb, gm, t0, t1, t2, t3 = (w[:, 32 + i, :] for i in range(7))
            step(ts(gx, gx, col("c_gate_b"), None, ADD))
            step(ts(t0, gx, 0.0, None, ALU.min))
            stt(t1, gx, -1.0, gx, MUL, MAX).then_inc(mg_in, 1)
            dve.wait_ge(mg_exp, 1)
            log1p(t1, t2, t3, gm)
            step(tt(t0, t0, gm, SUB))
            step(ts(t2, t1, 0.0, 1.0, MUL, ADD))
            nc.vector.tensor_tensor_scan(gb, t2, t0, 0.0, MUL, ADD).then_inc(mg_lf, 1)
            dve.wait_ge(mg_lf, 1)
            dve.wait_ge(mg_g, 1)
            nc.vector.tensor_tensor_scan(gm, t2, ps[:, 6, 0:T], 0.0, MUL, MAX).then_inc(mg_max, 1)
            dve.wait_ge(mg_max, 1)
            for n in range(16):
                src, acc = w[:, n, :], w[:, 38 + n % 2, :]

                def tap(k):
                    return col("c_conv_w", 1, 16 * k + n)

                step(ts(acc, src, tap(3), col("c_conv_b", 1, n), MUL, ADD))
                for k in (2, 1):
                    s = 3 - k
                    step(stt(acc[:, s:T], src[:, 0:T - s], tap(k), acc[:, s:T], MUL, ADD))
                stt(acc[:, 3:T], src[:, 0:T - 3], tap(0), acc[:, 3:T], MUL, ADD).then_inc(cv_pre, 1)
                dve.wait_ge(cv_pre, n + 1)
                dve.wait_ge(cv_sig, n + 1)
                tt(src, acc, sm[:, n % 2, 0, :], MUL).then_inc(cv_done, 1)
            dve.wait_ge(cv_done, 16)
            for hd in range(8):
                dve.wait_ge(ml_s, hd + 1)
                tt(sm[:, 0, :, :], masks[:, M_LSTM, :, :], along(ps[:, 5, 0:T], 2), ADD).then_inc(ml_mask, 1)
                dve.wait_ge(ml_e, 4 * hd + 2)
                if hd:
                    dve.wait_ge(ml_o, hd)
                stt(pt[:, 0, :, :].rearrange("p a b -> p (a b)"), ps[:, 4, :], float(P) ** -0.5,
                    sm[:, 0, :, :].rearrange("p a b -> p (a b)"), MUL, MUL).then_inc(ml_p, 1)
                dve.wait_ge(ml_p, hd + 1)
                dve.wait_ge(ml_e, 4 * hd + 4)
                tt(w[:, 43, :], w[:, 40, :], w[:, 41, :], MAX).then_inc(ml_den, 1)
                dve.wait_ge(ml_den, hd + 1)
                step(nc.vector.reciprocal(w[:, 43, :], w[:, 43, :]))
                hb = w[:, 16 + 2 * hd:18 + 2 * hd, :]
                tt(hb, ps[:, 6, :].rearrange("p (a b) -> p a b", b=T), along(w[:, 43, :], 2), MUL).then_inc(ml_h, 1)
                dve.wait_ge(ml_sums, hd + 1)
                ts(w[:, 42, :], ps[:, 7, T:2 * T], 1.0 / (2 * P), EPS, MUL, ADD).then_inc(ml_var, 1)
                dve.wait_ge(ml_std, hd + 1)
                inverse(w[:, 41, :], w[:, 42, :], w[:, 43, :])
                step(tt(hb, hb, along(w[:, 41, :], 2), MUL))
            yc = w[:, 16:32, :]
            step(tt(yc, yc, wide(col("c_norm"), 16), MUL))
            dve.wait_ge(y_gate, 1)
            tt(yc, yc, w[:, 0:16, :], MUL).then_inc(y_done, 1)
            dve.wait_ge(y_done, 1)
            step(tt(yc, yc, oa[:, 16:32, :], MUL))
            dve.wait_ge(y_gate, 2)
            step(tt(yc, yc, w[:, 0:16, :], MUL))
            dve.wait_ge(stream_loaded[1], 16)
            split(sm[:, 1, :, :], None, xs, 0, XR["p1"] + 1)
            cp(small[:, 63:64], ones[:, 0:1]).then_inc(stream_split, 1)
            for j in range(8):
                split(w[:, 16 + 2 * j:18 + 2 * j, :], None, xa, 2 * j, XR["y1"] + j + 1)
            if upto < 6:
                return
            tail(1, "oout", "h2", None, None, None)
            if upto < 7:
                return
            root("first", RS_LAYER, D)
            step(tt(h[:, :, :], h[:, :, :], along(rs[:, RS_LAYER, :], 16), MUL))
            tt(h[:, :, :], h[:, :, :], wide(col("final_norm"), 16), MUL).then_inc(h_ready, 1)
            dve.wait_ge(h_ready, HR["x2"] + 1)

            def memory(first, name, gain):
                for j in range(8):
                    n = first + j
                    dve.wait_ge(stream_loaded[n % 2], 16 * (n // 2 + 1))
                    split(sm[:, n % 2, :, :], col(gain, 2, 2 * j), xb, 2 * j, XR[name] + j + 1)
                    cp(small[:, 63:64], ones[:, 0:1]).then_inc(stream_split, 1)

            memory(2, "mem2", "ev_mem_norm")
            root("mem", RS_MEM, D)
            for j in range(8):
                split(h[:, 2 * j:2 * j + 2, :], col("ev_norm", 2, 2 * j), xa, 2 * j, XR["x2"] + j + 1)
            root("x2", RS_LAYER, D)
            store("evkpe", w, 28, RS_LAYER)
            store("evc", w, 29, RS_LAYER)
            store("evmem", w, 35, RS_MEM)
            for j in range(2):
                split(w[:, 29 + 2 * j:31 + 2 * j, :], col("ev_q_norm", 2, 2 * j), xs, 2 * j, XR["cq"] + j + 1)
            split(w[:, 33:35, :], col("ev_kv_norm", 2, 0), xs, 4, XR["ckv"] + 1)
            root("cq", RS_Q, 512)
            root("ckv", RS_KV, 256)
            store("uq", w, 0, RS_Q)
            store("ukv", w, 12, RS_KV)
            if upto < 8:
                return

            rotated = [0]

            def rotate(blocks, kind):
                for k in range(0, len(blocks), 2):
                    n, two = rotated[0], blocks[k:k + 2]
                    dve.wait_ge(rp_sums, n + 1)
                    for j, bl in enumerate(two):
                        step.post(tt(tb[:, j, :], ps[:, 6 + n % 2, j * T:(j + 1) * T], rope[:, kind, 1, :], MUL))
                        step.post(tt(w[:, bl, :], w[:, bl, :], rope[:, kind, 0, :], MUL))
                    step.wait()
                    for j, bl in enumerate(two):
                        ins = tt(w[:, bl, :], w[:, bl, :], tb[:, j, :], ADD)
                        if j + 1 < len(two):
                            step.post(ins)
                    ins.then_inc(rp_taken, 1)
                    dve.wait_ge(rp_taken, n + 1)
                    rotated[0] += 1

            def softmax_in(heads, a):
                for i, hd in enumerate(heads):
                    s4 = small[:, 16 * i:16 * i + 16]
                    dve.wait_ge(at_s, a + i + 1)
                    if a + i >= 2:
                        dve.wait_ge(at_turned, a + i - 1)
                    dst, src = sm[:, i, :, :].rearrange("p a b -> p (a b)"), ps[:, 4 + i, :]
                    if hd["mask"] is None:
                        step(ts(dst, src, hd["scale"], None, MUL))
                    else:
                        step(stt(dst, src, hd["scale"], masks[:, hd["mask"], :, :].rearrange("p a b -> p (a b)"), MUL,
                                 ADD))
                    if hd["sink"] is None:
                        nc.vector.tensor_reduce(s4[:, 0:2], sm[:, i, :, :], AX, MAX, negate=True).then_inc(at_neg, 1)
                    else:
                        step(nc.vector.tensor_reduce(s4[:, 6:8], sm[:, i, :, :], AX, MAX))
                        ts(s4[:, 0:2], s4[:, 6:8], col("sinks", 1, hd["sink"]), -1.0, MAX, MUL).then_inc(at_neg, 1)

            def softmax_out(heads, a):
                for i, hd in enumerate(heads):
                    s4 = small[:, 16 * i:16 * i + 16]
                    dve.wait_ge(at_e, a + i + 1)
                    if hd["sink"] is not None:
                        step(tt(s4[:, 2:4], s4[:, 2:4], s4[:, 4:6], ADD))
                    step(nc.vector.reciprocal(s4[:, 2:4], s4[:, 2:4]))
                    tt(sm[:, i, :, :], sm[:, i, :, :], wide(s4[:, 2:4], 2), MUL).then_inc(at_p, 1)

            def keep(heads, a):
                for i, hd in enumerate(heads):
                    vb, v0, vn, p0 = hd["v"]
                    dve.wait_ge(at_o, a + i + 1)
                    cp(w[p0:p0 + vn, hd["o"], :], ps[p0:p0 + vn, 4 + i, 0:T]).then_inc(at_done, 1)

            gates = [16]

            def gated(st, p, blocks, x_at, x_count):
                pair = st.pair0 + p
                dve.wait_ge(cross_ready, pair + 1)
                cr = cross[:, (st.pair0 + p) % 2, :, :]
                step(tt(tb[:, :, :], ps[:, banks(st, p % 2), 0:T], cr, ADD))
                tt(tb[:, :, :], tb[:, :, :], along(rs[:, RS_LAYER, :], 2), MUL).then_inc(g_pre, 1)
                dve.wait_ge(g_sig, gates[0] + 1)
                gates[0] += 1
                tt(tb[:, :, :], tb[:, :, :], cr, MUL).then_inc(pair_out, 1)
                dve.wait_ge(pair_out, pair + 1)
                for j, bl in enumerate(blocks):
                    step.post(tt(tb[:, j, :], tb[:, j, :], w[:, bl, :], MUL))
                step.wait()
                split(tb[:, :, :], None, xb, x_at, x_count)

            def attend(couples, gate, a, x_at, x_count):
                p, due = 0, None
                for c, heads in enumerate(couples):
                    softmax_in(heads, a + 2 * c)
                    softmax_out(heads, a + 2 * c)
                    if due:
                        gated(ST[gate], p, due, x_at + 2 * p, x_count + p + 1)
                        p += 1
                    keep(heads, a + 2 * c)
                    due = heads[-1]["gate"]
                dve.wait_ge(at_done, a + 2 * len(couples))
                gated(ST[gate], p, due, x_at + 2 * p, x_count + p + 1)

            rotate(MLA_ROPE, 0)
            attend(MLA_COUPLES, "evgate_a", 0, 0, XR["y2"])
            store("evmoba", w, 0, RS_LAYER)
            rotate(MOBA_ROPE, 1)
            attend(MOBA_COUPLES, "evgate_b", 8, 8, XR["y2"] + 4)

            def add_out(name, x_next, gain):
                st = ST[name]

                def pair(p, par):
                    hp = h[:, ds(p * 2, 2), :]
                    take(st, p, par, tb[:, :, :])
                    tt(hp, hp, tb[:, :, :], ADD).then_inc(h_ready, 1)
                    dve.wait_ge(h_ready, p + (HR[name] + 1))
                    if x_next:
                        split(hp, col(gain, 2, p * 2), xa, p * 2, p + (XR[x_next] + 1))

                pairs_loop(dve, 8, pair, steps=step, per=2 if x_next else 0)

            add_out("evout", "x3", "od_norm")
            if upto < 9:
                return
            root("x3", RS_LAYER, D)
            memory(10, "mem3", "od_mem_norm")
            store("odin", w, 0, RS_LAYER)
            store("odmem", w, 32, RS_MEM)
            dve.wait_ge(rope_loaded, 32 * 2)
            rotate(SWA_ROPE, 0)
            rotate(DIL_ROPE, 1)
            attend(OD_COUPLES, "odgate", 20, 0, XR["y3"])
            add_out("odout", None, None)
            root("last", RS_LAYER, D)
            step(tt(h[:, :, :], h[:, :, :], along(rs[:, RS_LAYER, :], 16), MUL))
            tt(h[:, :, :], h[:, :, :], wide(col("final_norm_2"), 16), MUL).then_inc(h_ready, 1)


def _head(qk, v, o, mask, scale, gate=None, sink=None):
    return dict(qk=qk, v=v, o=o, mask=mask, scale=scale, gate=gate, sink=sink)


def _couples(heads):
    return [heads[i:i + 2] for i in range(0, len(heads), 2)]


MLA_ROPE, MLA_V = [8, 9, 10, 11, 28], list(range(20, 28))
MLA_COUPLES = _couples([
    _head([(i, 12 + i, 0, 128), (8 + i // 2, 28, 64 * (i % 2), 64)], (20 + i, 0, 128, 0), i, 1, 192.0 ** -0.5,
          gate=(i - 1, i) if i % 2 else None) for i in range(8)])
MOBA_ROPE, MOBA_V = list(range(16)), list(range(16, 24)) + list(range(39, 43))
MOBA_COUPLES = _couples([
    _head([(i, 8 + i, 0, 128)], (16 + i, 0, 128, 0), i, 1, 128.0 ** -0.5,
          gate=(i - 1, i) if i % 2 else None) for i in range(8)] + [
    _head([(24 + i, 35 + i, 0, 128)], (39 + i, 0, 128, 0), 24 + i, None, 128.0 ** -0.5,
          gate=(24 + i - 1, 24 + i) if i % 2 else None) for i in range(4)])
SWA_ROPE, DIL_ROPE = list(range(9)), list(range(10, 22))
OD_V = [9] + list(range(22, 28)) + list(range(36, 40))
OD_COUPLES = _couples([
    _head([(j, 8, 64 * g, 64)], (9, 64 * g, 64, 64 * g), j, 2, 64.0 ** -0.5, sink=j + 8 * g,
          gate=(j - 1, j) if j % 2 and g else None) for j in range(8) for g in range(2)] + [
    _head([(10 + i, 16 + i, 0, 128)], (22 + i, 0, 128, 0), 10 + i, 3, 128.0 ** -0.5,
          gate=(10 + i - 1, 10 + i) if i % 2 else None) for i in range(6)] + [
    _head([(28 + i, 32 + i, 0, 128)], (36 + i, 0, 128, 0), 28 + i, None, 128.0 ** -0.5,
          gate=(28 + i - 1, 28 + i) if i % 2 else None) for i in range(4)])


def constants():
    f = np.float32
    ident = np.eye(P, dtype=f)
    gsel = np.zeros((P, 2, P), f)
    for i in range(8):
        gsel[ROW_I + i, 0, i] = 1.0
        gsel[ROW_F + i, 1, i] = -1.0
    pos = np.arange(T)
    q, k = pos[:, None], pos[None, :]

    def rows(m):
        return m.reshape(2, P, T).transpose(1, 0, 2)

    causal = np.where(k <= q, 0.0, NEG)
    swa = np.where((q - k >= 0) & (q - k <= 127), 0.0, NEG)
    hits = ((q >= k) & (q - k <= 128)).astype(int)
    for dil in (4, 16):
        hits = hits + ((q >= k) & ((q - k) % dil == 0) & ((q - k) // dil <= 128))
    dil = np.where(hits > 0, np.log(np.maximum(hits, 1)), NEG)
    mlstm = np.where(q >= k, -NEG, 0.0) * (q != k)
    mlstm = np.where(k >= q, 0.0, -NEG)
    masks = np.stack([rows(mlstm), rows(causal), rows(swa), rows(dil)], 1).astype(f)
    s, t = np.arange(P)[:, None], np.arange(P)[None, :]
    lvl = np.zeros((P, 4, 2, P), f).reshape(P, 8, P)
    lvl[:, 0, :] = s == t
    for level in range(1, 8):
        size = 2 ** level
        lvl[:, level, :] = (s // size == t // size) & (s % size < size // 2) & (t % size >= size // 2)

    def rope(width, dim):
        inv = (f(1.0) / np.power(f(500000.0), np.arange(0, dim, 2, dtype=f) / f(dim))).astype(f)
        ang = (np.arange(T, dtype=f)[:, None] * inv[None, :]).astype(f)
        c, sn = np.cos(ang).astype(f).T, np.sin(ang).astype(f).T
        cos, sin, m = np.ones((P, T), f), np.zeros((P, T), f), np.zeros((P, P), f)
        for at in range(0, P, width):
            hf = dim // 2
            cos[at:at + hf] = c
            cos[at + hf:at + dim] = c
            sin[at:at + hf] = sn
            sin[at + hf:at + dim] = sn
            for i in range(hf):
                m[at + hf + i, at + i] = -1.0
                m[at + i, at + hf + i] = 1.0
        return np.stack([cos, sin], 1), m

    kinds = [rope(64, 64), rope(128, 32), rope(64, 16), rope(128, 32)]
    out = dict(ident=ident, gsel=gsel, masks=masks, lvl=lvl.reshape(P, 4, T))
    for name, a, b in (("ev", 0, 1), ("od", 2, 3)):
        out["rope_" + name] = np.stack([kinds[a][0], kinds[b][0]], 1)
        out["rot_" + name] = np.stack([kinds[a][1], kinds[b][1]], 1)
    return out


def channel_cols(v):
    v = np.asarray(v)
    return np.ascontiguousarray(v.reshape(-1, P).T)


def token_blocks(x):
    x = np.asarray(x)
    return np.ascontiguousarray(x.T.reshape(-1, P, T).transpose(1, 0, 2))


def weight_pairs(wt, st):
    wt = np.asarray(wt)
    cells = wt.reshape(st.blocks, P, st.pairs, st.nb, P)
    order = (2, 1, 3, 0, 4) if st.blocks == 2 else (2, 1, 0, 3, 4)
    return np.ascontiguousarray(cells.transpose(order)).reshape(st.pairs, P, -1)


def layout(i):
    ST = stages()
    i = {k: np.asarray(v) for k, v in i.items()}
    out = dict(constants())
    out["x"] = token_blocks(i["x"][0])
    out["p"] = np.stack([token_blocks(i["p"][l, 0]) for l in range(2)])
    out["mem"] = np.ascontiguousarray(token_blocks(i["mem_2"][0]).reshape(P, 8, 2, T).transpose(1, 0, 2, 3))
    for name in ("w_r", "w_i"):
        out[name] = np.ascontiguousarray(i["b_" + name][0].transpose(1, 0, 2)).reshape(P, 8 * P)
    gate_b = np.zeros((P, 1), np.float32)
    gate_b[ROW_I:ROW_I + 8, 0] = i["c_b_i"][0]
    gate_b[ROW_F:ROW_F + 8, 0] = i["c_b_f"][0]
    c = dict(
        e_norm=i["e_norm"][0], a_lb0=i["a_lb_logits"][0], a_lb1=i["a_lb_logits"][1], a_norm=i["a_norm"][0],
        b_conv_w=i["b_conv_w"][0], b_conv_b=i["b_conv_b"][0], b_b_r=i["b_b_r"][0], b_b_i=i["b_b_i"][0],
        b_lambda=i["b_lambda"][0], o_norm=i["o_norm"][0], c_conv_w=i["c_conv_w"][0], c_conv_b=i["c_conv_b"][0],
        c_norm=i["c_norm"][0], ple_norm0=i["ple_norm"][0], ple_norm1=i["ple_norm"][1], final_norm=i["final_norm"],
        ev_norm=i["ev_norm_g_2"][0], ev_q_norm=i["ev_q_norm_g_2"][0], ev_kv_norm=i["ev_kv_norm_g_2"][0],
        ev_mem_norm=i["ev_mem_norm_g_2"][0], od_norm=i["od_norm_g_2"][0], od_mem_norm=i["od_mem_norm_g_2"][0],
        final_norm_2=i["final_norm_g_2"])
    c = {k: channel_cols(v) for k, v in c.items()}
    c["c_gate_b"] = gate_b
    c["sinks"] = np.broadcast_to(i["od_sinks_2"][0], (P, 16))
    out["cols"] = np.ascontiguousarray(np.concatenate([c[n] for n, _ in COLS], 1))

    W = {}
    e = i["e_w_in"][0]
    W["ein"], W["ein_zb"] = e[:, :5120], e[:, 5120:]
    W["eout"], W["oout"] = i["e_w_out"][0], i["o_w_out"][0]
    for l in range(2):
        W[f"ple{l}"], W[f"gate{l}"] = i["ple_w"][l], i["ple_gate_w"][l]
    o = i["o_w_in"][0]
    W["oqk"], W["ov"], W["oog"], W["oz"] = (o[:, 2048 * j:2048 * j + 2048] for j in range(4))
    g = np.zeros((D, P), np.float32)
    g[:, ROW_I:ROW_I + 8] = o[:, 8192:8200]
    g[:, ROW_F:ROW_F + 8] = o[:, 8200:8208]
    W["ogate"] = g
    e = i["ev_w_in_2"][0]
    W["evc"] = e[:, 0:768]
    W["evkpe"] = np.concatenate([e[:, 768:832], e[:, 768:832]], 1)
    W["evmoba"] = e[:, 832:832 + 3584]
    W["evgate_a"], W["evgate_b"] = e[:, 4416:4416 + 1024], e[:, 5440:]
    W["evmem"], W["odmem"] = i["ev_w_mem_kv_2"][0], i["od_w_mem_kv_2"][0]
    uq = i["ev_w_uq_2"][0].reshape(512, 8, 192)
    W["uq"] = np.concatenate([uq[:, :, :128].reshape(512, 1024), uq[:, :, 128:].reshape(512, 512)], 1)
    ukv = i["ev_w_ukv_2"][0].reshape(256, 8, 2, 128)
    W["ukv"] = ukv.transpose(0, 2, 1, 3).reshape(256, 2048)
    W["evout"] = i["ev_w_out_2"][0]
    swa = np.arange(1024).reshape(2, 8, 64).transpose(1, 0, 2).reshape(-1)
    o = i["od_w_in_2"][0]
    W["odin"] = np.concatenate([o[:, swa], o[:, 1024:4096]], 1)
    W["odgate"] = np.concatenate([o[:, 4096 + swa], o[:, 5120:]], 1)
    W["odout"] = np.concatenate([i["od_w_out_2"][0][swa], i["od_w_out_2"][0][1024:]], 0)
    for name, st in ST.items():
        out["w_" + name] = weight_pairs(W[name], st)
    return out


def kernel(**inputs):
    import concourse.bacc as bacc
    from concourse import mybir
    from concourse.bass_utils import run_bass_kernel_spmd

    arrays = layout(inputs)
    nc = bacc.Bacc("TRN2", target_bir_lowering=False, num_devices=1)
    A = {n: nc.dram_tensor(n + "_dram", a.shape, mybir.dt.from_np(a.dtype), kind="ExternalInput").ap()
         for n, a in arrays.items()}
    out = nc.dram_tensor("out_dram", (P, KD, T), mybir.dt.float32, kind="ExternalOutput").ap()
    build(nc, A, out)
    r = run_bass_kernel_spmd(nc, [{n + "_dram": a for n, a in arrays.items()}], core_ids=[0])
    got = r.results[0]["out_dram"]
    return got.transpose(1, 0, 2).reshape(D, T).T.reshape(1, T, D)
```

```python
import numpy as np

T = 256
P = 128
D = 2048
KD = D // P
EPS = 1e-6
SLOTS = 4
CELLS_MAX = 4
POOL_ROUNDS = ("evgate_a", "evgate_b", "odgate")
NEG = -1.0e30


def stage_table():
    return [
        ("ein", "xa", 16, 20, 2),
        ("ein_zb", "xa", 16, 4, 2),
        ("ple0", "xs", 2, 8, 2),
        ("eout", "xb", 16, 8, 2),
        ("gate0", "xa", 16, 8, 2),
        ("ogate", "xb", 16, 1, 1),
        ("oqk", "xb", 16, 8, 2),
        ("ov", "xb", 16, 8, 2),
        ("oog", "xb", 16, 8, 2),
        ("oz", "xb", 16, 8, 2),
        ("ple1", "xs", 2, 8, 2),
        ("oout", "xa", 16, 8, 2),
        ("gate1", "xb", 16, 8, 2),
        ("evkpe", "xa", 16, 1, 1),
        ("evc", "xa", 16, 3, 2),
        ("evmem", "xb", 16, 4, 2),
        ("uq", "xs", 4, 6, 2),
        ("ukv", "xs", 2, 8, 2),
        ("evgate_a", "xa", 16, 4, 2),
        ("evmoba", "xa", 16, 14, 2),
        ("evgate_b", "xa", 16, 6, 2),
        ("evout", "xb", 20, 8, 2),
        ("odin", "xa", 16, 16, 2),
        ("odmem", "xb", 16, 4, 2),
        ("odgate", "xa", 16, 9, 2),
        ("odout", "xb", 18, 8, 2),
    ]


def unit_cells(blocks, nb):
    if blocks == 2:
        return [[(k, b)] for b in range(nb) for k in range(blocks)]
    n = 4 if blocks < 16 else 8 if blocks == 16 else 12
    small, more = divmod(blocks, n)
    out, k = [], 0
    for q in range(n):
        m = small + (q < more)
        out.append([(kk, b) for kk in range(k, k + m) for b in range(nb)])
        k += m
    return out


class Stage:

    def __init__(self, row, unit0, pair0):
        self.name, self.x, self.blocks, self.pairs, self.nb = row
        self.units = unit_cells(self.blocks, self.nb)
        self.upp = len(self.units)
        self.unit0, self.pair0 = unit0, pair0
        self.pool_rounds = self.name in POOL_ROUNDS


def stages():
    out, unit0, pair0 = {}, 0, 0
    rounded = {True: 0, False: 0}
    for row in stage_table():
        s = Stage(row, unit0, pair0)
        out[s.name] = s
        s.rounded0 = rounded[s.pool_rounds]
        rounded[s.pool_rounds] += s.pairs * s.upp
        unit0 += s.pairs * s.upp
        pair0 += s.pairs
    return out


COLS = [
    ("e_norm", 16), ("a_lb0", 8), ("a_lb1", 8), ("a_norm", 8), ("b_conv_w", 32), ("b_conv_b", 8),
    ("b_b_r", 8), ("b_b_i", 8), ("b_lambda", 8), ("o_norm", 16), ("c_conv_w", 64), ("c_conv_b", 16),
    ("c_gate_b", 1), ("c_norm", 16), ("ple_norm0", 16), ("ple_norm1", 16), ("final_norm", 16),
    ("ev_norm", 16), ("ev_q_norm", 4), ("ev_kv_norm", 2), ("ev_mem_norm", 16), ("od_norm", 16),
    ("sinks", 16), ("od_mem_norm", 16), ("final_norm_2", 16),
]
COL_AT, _n = {}, 0
for _name, _w in COLS:
    COL_AT[_name] = _n
    _n += _w
NCOLS = _n
ROW_I, ROW_F = 0, 32


def build(nc, A, out, upto=99):
    import concourse.bass as bass
    from concourse import mybir
    from contextlib import ExitStack

    F32, F32R, U8 = mybir.dt.float32, mybir.dt.float32r, mybir.dt.uint8
    ALU, ACT = mybir.AluOpType, mybir.ActivationFunctionType
    AX = mybir.AxisListType.X
    ADD, SUB, MUL, MAX = ALU.add, ALU.subtract, ALU.mult, ALU.max
    ds = bass.ds
    ST = stages()

    ctx = ExitStack()
    with ctx:
        def sb(name, shape, dt=F32):
            return ctx.enter_context(nc.sbuf_tensor(name, shape, dt))

        def sem(name):
            return ctx.enter_context(nc.semaphore(name))

        with nc.sbuf_tensor("oa", [P, 32, T], F32) as oa:
            pass
        xa = sb("xa", [P, 16, 2 * T], F32R)
        with nc.sbuf_tensor("ob", [P, 40, T], F32) as ob:
            pass
        xb = sb("xb", [P, 20, 2 * T], F32R)
        xs = sb("xs", [P, 6, 2 * T], F32R)
        h = sb("h", [P, KD, T])
        w = sb("w", [P, 44, T])
        raw = sb("raw", [P, SLOTS, CELLS_MAX * P])
        w_hi = sb("w_hi", [P, SLOTS, CELLS_MAX * P], F32R)
        w_lo = sb("w_lo", [P, SLOTS, CELLS_MAX * P], F32R)
        cross = sb("cross", [P, 2, 2, T])
        tb = sb("tb", [P, 2, T])
        sq = sb("sq", [P, 2, 2, T])
        rs = sb("rs", [P, 4, T])
        RS_LAYER, RS_PLE, RS_Q, RS_MEM = range(4)
        RS_KV = RS_PLE
        sm = sb("sm", [P, 2, 2, T])
        pt = sb("pt", [P, 2, 2, T])
        small = sb("small", [P, 64])
        cols = sb("cols", [P, NCOLS])
        ident = sb("ident", [P, P])
        ones = sb("ones", [P, P])
        gsel = sb("gsel", [P, 2, P])
        masks = sb("masks", [P, 4, 2, T])
        rope = sb("rope", [P, 2, 2, T])
        rot = sb("rot", [P, 2, P])
        lvl = sb("lvl", [P, 8, P], U8)
        ps = ctx.enter_context(nc.psum_tensor("ps", [P, 8, 512], F32))
        X = {"xa": xa, "xb": xb, "xs": xs}
        M_LSTM, M_CAUSAL, M_SWA, M_DIL = range(4)

        def col(name, n=None, at=0):
            c = COL_AT[name]
            return cols[:, c:c + dict(COLS)[name]] if n is None else cols[:, ds(c + at, n)]

        def wide(ap, n):
            return ap.unsqueeze(2).to_broadcast([P, n, T])

        def along(ap, n):
            return ap.unsqueeze(1).to_broadcast([P, n, T])

        x_loaded, cols_loaded, consts_loaded = sem("x_loaded"), sem("cols_loaded"), sem("consts_loaded")
        unit_loaded = [sem(f"unit_loaded{i}") for i in range(SLOTS)]
        act_rounded, pool_rounded = sem("act_rounded"), sem("pool_rounded")
        lo_ready, unit_used = sem("lo_ready"), sem("unit_used")
        cross_ready, pair_out, stored = sem("cross_ready"), sem("pair_out"), sem("stored")
        x_ready = sem("x_ready")
        sq_ready, sq_used, var_ready, std_ready = sem("sq_ready"), sem("sq_used"), sem("var_ready"), sem("std_ready")
        dve_step, act_step = sem("dve_step"), sem("act_step")
        ones_set = sem("ones_set")
        stream_loaded = [sem("stream_loaded0"), sem("stream_loaded1")]
        out_stored = sem("out_stored")
        h_ready = sem("h_ready")
        par_in, par_exp, par_done = sem("par_in"), sem("par_exp"), sem("par_done")
        hg_sig, hg_q, hg_logf, hg_qk = sem("hg_sig"), sem("hg_q"), sem("hg_logf"), sem("hg_qk")
        hg_diff, hg_exp, hg_lv_in, hg_lv_out, hg_masked = (
            sem("hg_diff"), sem("hg_exp"), sem("hg_lv_in"), sem("hg_lv_out"), sem("hg_masked"))
        v_turned, v_copied = sem("v_turned"), sem("v_copied")
        hg_o, hg_ocopied = sem("hg_o"), sem("hg_ocopied")
        hn_sums, hn_var, hn_std, hn_gate = sem("hn_sums"), sem("hn_var"), sem("hn_std"), sem("hn_gate")
        lr_conv, lr_w, lr_pre, lr_act, lr_th, lr_fix, lr_root = (
            sem("lr_conv"), sem("lr_w"), sem("lr_pre"), sem("lr_act"), sem("lr_th"), sem("lr_fix"), sem("lr_root"))
        y_gate, y_done = sem("y_gate"), sem("y_done")
        g_sig, g_pre = sem("g_sig"), sem("g_pre")
        cv_pre, cv_sig, cv_done = sem("cv_pre"), sem("cv_sig"), sem("cv_done")
        mg_in, mg_exp, mg_lf, mg_g, mg_gcols, mg_max = (
            sem("mg_in"), sem("mg_exp"), sem("mg_lf"), sem("mg_g"), sem("mg_gcols"), sem("mg_max"))
        ml_s, ml_mask, ml_e, ml_p, ml_o, ml_den, ml_h, ml_sums, ml_var, ml_std = (
            sem("ml_s"), sem("ml_mask"), sem("ml_e"), sem("ml_p"), sem("ml_o"), sem("ml_den"), sem("ml_h"),
            sem("ml_sums"), sem("ml_var"), sem("ml_std"))
        ml_sq = sem("ml_sq")
        rp_sums, rp_taken, rope_loaded = sem("rp_sums"), sem("rp_taken"), sem("rope_loaded")
        at_s, at_neg, at_e, at_p, at_turned, at_pt, at_o, at_done = (
            sem("at_s"), sem("at_neg"), sem("at_e"), sem("at_p"), sem("at_turned"), sem("at_pt"), sem("at_o"),
            sem("at_done"))

        XR, n = {}, 0
        for name, pairs in (("x", 8), ("p0", 1), ("y0", 8), ("h0", 8), ("h1", 8), ("p1", 1), ("y1", 8),
                            ("h2", 8), ("x2", 8), ("mem2", 8), ("cq", 2), ("ckv", 1), ("y2", 10),
                            ("x3", 8), ("mem3", 8), ("y3", 9)):
            XR[name] = n
            n += pairs
        NORMS, n = {}, 0
        for i, (name, pairs) in enumerate((("x", 8), ("mem", 8), ("ple0", 8), ("h1", 8), ("ple1", 8), ("first", 16),
                                           ("cq", 2), ("ckv", 1), ("x3", 8), ("last", 8))):
            NORMS[name] = (n, pairs)
            n += pairs
        STORED, n = {}, 0
        for name in ("ein", "ein_zb", "ogate", "oqk", "ov", "oog", "oz", "evkpe", "evc", "evmem", "uq", "ukv",
                     "evmoba", "odin", "odmem"):
            STORED[name] = n
            n += ST[name].pairs
        HR = {"gate0": 0, "gate1": 8, "evout": 16, "odout": 24, "last": 32}
        ROOTS = {"x": 0, "mem": 1, "ple0": 2, "h1": 3, "ple1": 4, "first": 5, "x2": 6, "cq": 7, "ckv": 8, "x3": 9,
                 "last": 10}
        STREAM = {"mem": 0, "p0": 8, "p1": 9, "mem2": 10, "mem3": 18}

        class Steps:

            def __init__(self, eng, s):
                self.eng, self.s, self.n = eng, s, 0

            def post(self, ins):
                self.n = self.n + 1
                ins.then_inc(self.s, 1)

            def wait(self):
                self.eng.wait_ge(self.s, self.n)

            def __call__(self, ins):
                self.post(ins)
                self.wait()

        def pairs_loop(eng, count, body, first=0, steps=None, per=0):
            trips = (count - first) // 2
            if trips >= 2:
                n0 = steps.n if steps else 0
                with eng.Fori(0, trips) as i:
                    for k in range(2):
                        if steps:
                            steps.n = n0 + i * (2 * per) + k * per
                        body(i * 2 + (first + k), (first + k) % 2)
                if steps:
                    steps.n = n0 + trips * 2 * per
                first += 2 * trips
            for p in range(first, count):
                body(p, p % 2)

        def banks(st, par, nb=None):
            at = 2 * ((st.pair0 + par) % 2)
            return slice(at, at + (nb or st.nb))

        def unit_of(st, p, q):
            turn = st.unit0 // SLOTS + p * (st.upp // SLOTS) + q // SLOTS + 1
            return q % SLOTS, len(st.units[q]) * P, st.unit0 + p * st.upp + q, turn

        block = ctx.enter_context(nc.Block())

        @block.sync
        def _(sp):
            def load(st):
                wd = A["w_" + st.name]

                def pair(p, par):
                    at = 0
                    for q in range(st.upp):
                        slot, n, unit, _ = unit_of(st, p, q)
                        if not (isinstance(p, int) and unit < SLOTS):
                            sp.wait_ge(lo_ready, unit - SLOTS + 1)
                        src = wd[p] if isinstance(p, int) else wd[ds(p, 1)].rearrange("o p c -> (o p) c")
                        sp.dma_start(raw[:, slot, 0:n], src[:, at:at + n]).then_inc(unit_loaded[slot], 16)
                        at += n

                if st.unit0 == 0:
                    pair(0, 0)
                pairs_loop(sp, st.pairs, pair, first=int(st.unit0 == 0))

            for name in [r[0] for r in stage_table()]:
                load(ST[name])
            for k in range(4):
                sp.wait_ge(h_ready, HR["last"] + k + 1)
                sp.dma_start(out[:, 4 * k:4 * k + 4, :], h[:, 4 * k:4 * k + 4, :]).then_inc(out_stored, 16)
            sp.wait_ge(out_stored, 64)

        @block.gpsimd
        def _(pool):
            pool.wait_ge(ones_set, 1)

            def split(st):
                def pair(p, par):
                    for q in range(st.upp):
                        slot, n, unit, turn = unit_of(st, p, q)
                        nth = st.rounded0 + p * st.upp + q + 1
                        if st.pool_rounds:
                            pool.wait_ge(unit_loaded[slot], turn * 16)
                            pool.wait_ge(unit_used, unit - SLOTS + 1)
                            nc.gpsimd.tensor_tensor(w_hi[:, slot, 0:n].rearrange("p (c s) -> p c s", s=P),
                                                    raw[:, slot, 0:n].rearrange("p (c s) -> p c s", s=P),
                                                    ones[:, :].unsqueeze(1).to_broadcast([P, n // P, P]),
                                                    MUL).then_inc(pool_rounded, 1)
                            pool.wait_ge(pool_rounded, nth)
                        else:
                            pool.wait_ge(act_rounded, nth)
                        nc.gpsimd.tensor_tensor(w_lo[:, slot, 0:n], raw[:, slot, 0:n],
                                                w_hi[:, slot, 0:n].bitcast(F32), SUB).then_inc(lo_ready, 1)

                pairs_loop(pool, st.pairs, pair)

            for name in [r[0] for r in stage_table()]:
                split(ST[name])

        @block.tensor
        def _(pe):
            mm = nc.tensor.matmul

            def product(st, p, par, new=None):
                x, x0 = X[st.x], 4 if st.name == "ukv" else 0
                pair = st.pair0 + p
                if not (isinstance(p, int) and pair < 2):
                    pe.wait_ge(pair_out, pair - 1)
                bank = banks(st, par).start
                for q, cells in enumerate(st.units):
                    if new:
                        pe.wait_ge(x_ready, XR[new] + cells[-1][0] // 2 + 1)
                    pe.wait_ge(lo_ready, st.unit0 + p * st.upp + q + 1)
                    for c, (k, b) in enumerate(cells):
                        at = slice(c * P, c * P + P)
                        mm(ps[:, bank + b, :], w_hi[:, q % SLOTS, at], x[:, x0 + k, :], start=(k == 0), stop=False)
                        ins = mm(ps[:, bank + b, 0:T], w_lo[:, q % SLOTS, at], x[:, x0 + k, 0:T],
                                 start=False, stop=(k == st.blocks - 1))
                    ins.then_inc(unit_used, 1)

            def products(name, first=0, count=None, new=None, behind=None, peel=1):
                st = ST[name]
                count = st.pairs if count is None else count

                def pair(p, par):
                    product(st, p, par, new if isinstance(p, int) and p == 0 else None)
                    if behind:
                        behind(p, par)

                for p in range(first, first + peel):
                    pair(p, p % 2)
                pairs_loop(pe, count, pair, first + peel)

            def sum_squares(name, j, par, half=None):
                at, pairs = NORMS[name]
                n, hf = (1, 0) if half is None else (2, half)
                first, last = (isinstance(j, int) and j == v for v in (0, pairs // n - 1))
                if first and ROOTS[name] and not hf:
                    pe.wait_ge(var_ready, ROOTS[name])
                pe.wait_ge(sq_ready, j * n + (at + hf + 1))
                slot = (at + par * n + hf) % 2
                for b in range(2):
                    ins = mm(ps[:, 7, hf * T:hf * T + T], ones[:, :], sq[:, slot, b, :],
                             start=(first and not hf and b == 0), stop=(last and hf == n - 1 and b == 1))
                ins.then_inc(sq_used, 1)

            def sums_behind(name):
                def behind(p, par):
                    if not (isinstance(p, int) and p == 0):
                        for half in ((0, 1) if name == "first" else (None,)):
                            sum_squares(name, p - 1, 1 - par, half)
                return behind

            turned = [0]

            def turn_values(name_blocks, buf, after_stored):
                pe.wait_ge(stored, after_stored)
                for k in range(0, len(name_blocks), 2):
                    n = turned[0]
                    if n >= 2:
                        pe.wait_ge(v_copied, n - 1)
                    for j, bl in enumerate(name_blocks[k:k + 2]):
                        for tt in range(2):
                            ins = nc.tensor.transpose(ps[:, 4 + n % 2, (2 * j + tt) * P:(2 * j + tt + 1) * P],
                                                      buf[:, bl, tt * P:(tt + 1) * P], ident[:, :])
                    ins.then_inc(v_turned, 1)
                    turned[0] += 1

            pe.wait_ge(consts_loaded, 16 * 6)
            pe.wait_ge(ones_set, 1)
            def x_sums(p, par):
                for j in range(8):
                    sum_squares("x", j, j % 2)

            products("ein", 0, 1, new="x", behind=x_sums)
            products("ein", 1, 2)
            products("ein", 2, 10, behind=lambda p, par: sum_squares("mem", p - 2, par))
            products("ein", 10, 20, peel=0)
            products("ein_zb")
            if upto < 1:
                return

            turn_values(range(16, 24), w, STORED["ein"] + 12)
            pe.wait_ge(v_copied, 4)
            for g in range(2):
                for level in range(9):
                    n = 9 * g + level
                    if level == 0:
                        pe.wait_ge(hg_q, 1)
                        pe.wait_ge(hg_qk, 1)
                        q_, k_ = w[:, 4 * g:4 * g + 4, :], ob[:, 8 + 4 * g:12 + 4 * g, :]
                    else:
                        pe.wait_ge(hg_lv_in, 8 * g + level)
                        q_, k_ = ob[:, 20:24, :], ob[:, 24:28, :]
                    if n:
                        pe.wait_ge(hg_masked, n)
                    for hd in range(4):
                        if level < 8:
                            for tt in range(2):
                                c = hd * T + tt * P
                                ins = mm(ps[:, 4 + c // 512, c % 512:c % 512 + P], k_[:, hd, tt * P:(tt + 1) * P],
                                         q_[:, hd, tt * P:(tt + 1) * P], start=True, stop=True)
                        else:
                            ins = mm(ps[:, 4, hd * P:(hd + 1) * P], k_[:, hd, 0:P], q_[:, hd, P:T],
                                     start=True, stop=True)
                    ins.then_inc(hg_lv_out, 1)
                pe.wait_ge(hg_masked, 9 * g + 9)
                a = ob[:, 28:34, :].rearrange("p a b -> p (a b)")
                if g:
                    pe.wait_ge(hg_ocopied, 2)
                for hd in range(4):
                    v = w[:, 16 + 4 * g + hd, :]
                    o = ps[:, 6 + hd // 2, (hd % 2) * T:(hd % 2 + 1) * T]
                    mm(o[:, 0:P], v[:, 0:P], a[:, hd * T:hd * T + P], start=True, stop=True)
                    mm(o[:, P:T], v[:, 0:P], a[:, 1024 + hd * P:1024 + hd * P + P], start=True, stop=False)
                    ins = mm(o[:, P:T], v[:, P:T], a[:, hd * T + P:hd * T + T], start=False, stop=True)
                ins.then_inc(hg_o, 1)
            for hd in range(8):
                if hd % 2 == 0:
                    pe.wait_ge(hg_ocopied, 4)
                    pe.wait_ge(hn_gate, hd // 2 + 1)
                ins = mm(ps[:, 4 + hd // 2, (hd % 2) * T:(hd % 2 + 1) * T], ones[:, :], ob[:, 16 + hd, :],
                         start=True, stop=True)
            ins.then_inc(hn_sums, 1)
            if upto < 2:
                return
            pe.wait_ge(lr_w, 32)
            pe.wait_ge(hn_var, 1)
            for n in range(8):
                pe.wait_ge(lr_conv, n + 1)
                if n >= 2:
                    pe.wait_ge(lr_act, 2 * n - 2)
                for j in range(2):
                    wt = ob[:, 16 + 4 * j:20 + 4 * j, :].rearrange("p a b -> p (a b)")
                    ins = mm(ps[:, 4 + n % 2, j * T:(j + 1) * T], wt[:, n * P:(n + 1) * P], ob[:, 8 + n, :],
                             start=True, stop=True)
                ins.then_inc(lr_pre, 1)
            if upto < 3:
                return

            def tail(l, norm):
                products(f"ple{l}", new=f"p{l}")
                products("eout" if l == 0 else "oout", new=f"y{l}",
                         behind=lambda p, par: sum_squares(f"ple{l}", p, par))
                products(f"gate{l}", new=f"h{2 * l}", behind=sums_behind(norm), peel=2)

            tail(0, "h1")
            if upto < 4:
                return
            products("ogate", new="h1")
            sum_squares("h1", 7, 1)
            products("oqk")
            products("ov")
            products("oog")
            products("oz")
            if upto < 5:
                return
            pe.wait_ge(mg_lf, 1)
            gx, gb, gm = w[:, 32, :], w[:, 33, :], w[:, 34, :]
            mm(ps[:, 6, 0:T], gsel[:, 0, :], gx, start=True, stop=False)
            mm(ps[:, 6, 0:T], gsel[:, 1, :], gb, start=False, stop=True).then_inc(mg_g, 1)
            for st_ in range(2):
                c = slice(8 * st_, 8 * st_ + 8)
                mm(ps[:, 7, c], gx[:, st_ * P:(st_ + 1) * P], gsel[:, 0, 0:8], start=True, stop=False)
                ins = mm(ps[:, 7, c], gb[:, st_ * P:(st_ + 1) * P], gsel[:, 1, 0:8], start=False, stop=True)
            ins.then_inc(mg_g, 1)
            turn_values(range(16, 32), w, STORED["ov"] + 8)
            pe.wait_ge(v_copied, 12)
            pe.wait_ge(cv_done, 16)
            pe.wait_ge(mg_max, 1)
            pe.wait_ge(mg_gcols, 1)

            def ml_scores(hd):
                if hd:
                    pe.wait_ge(ml_p, hd)
                    pe.wait_ge(ml_den, hd)
                for kt in range(2):
                    mm(ps[:, 4, kt * T:(kt + 1) * T], w[:, 8 + hd, kt * P:(kt + 1) * P], w[:, hd, :],
                       start=True, stop=True)
                one_m = ident[:, hd:hd + 1].to_broadcast([P, P])
                one_b = ident[:, ROW_F + hd:ROW_F + hd + 1].to_broadcast([P, P])
                mm(ps[:, 5, 0:T], one_m, gm, start=True, stop=True)
                mm(ps[:, 5, T:2 * T], one_m, gm, start=True, stop=False)
                mm(ps[:, 5, T:2 * T], one_b, gb, start=False, stop=True).then_inc(ml_s, 1)

            for hd in range(8):
                ml_scores(hd)
                pe.wait_ge(ml_p, hd + 1)
                if hd:
                    pe.wait_ge(ml_h, hd)
                for eb in range(2):
                    for kt in range(2):
                        mm(ps[:, 6, eb * T:(eb + 1) * T], w[:, 16 + 2 * hd + eb, kt * P:(kt + 1) * P],
                           pt[:, 0, kt, :], start=(kt == 0), stop=(kt == 1))
                if hd:
                    pe.wait_ge(ml_var, hd)
                for kt in range(2):
                    ins = mm(ps[:, 7, 0:T], ones[:, :], pt[:, 0, kt, :], start=(kt == 0), stop=(kt == 1))
                ins.then_inc(ml_o, 1)
                pe.wait_ge(ml_sq, hd + 1)
                for eb in range(2):
                    ins = mm(ps[:, 7, T:2 * T], ones[:, :], pt[:, 1, eb, :], start=(eb == 0), stop=(eb == 1))
                ins.then_inc(ml_sums, 1)
            if upto < 6:
                return
            tail(1, "first")
            if upto < 7:
                return
            products("evkpe", new="x2")
            for half in range(2):
                sum_squares("first", 7, 1, half)
            products("evc")
            products("evmem", 0, 2, new="mem2", peel=2)
            for j in range(2):
                sum_squares("cq", j, j)
            products("evmem", 2, 3)
            sum_squares("ckv", 0, 0)
            products("evmem", 3, 4)
            products("uq", new="cq")
            products("ukv", new="ckv")
            if upto < 8:
                return

            rotated = [0]

            def rotate(blocks, kind, after_stored):
                pe.wait_ge(stored, after_stored)
                for k in range(0, len(blocks), 2):
                    n = rotated[0]
                    if n >= 2:
                        pe.wait_ge(rp_taken, n - 1)
                    for j, bl in enumerate(blocks[k:k + 2]):
                        ins = mm(ps[:, 6 + n % 2, j * T:(j + 1) * T], rot[:, kind, :], w[:, bl, :],
                                 start=True, stop=True)
                    ins.then_inc(rp_sums, 1)
                    rotated[0] += 1

            def scores(heads, a):
                for i, hd in enumerate(heads):
                    if a + i >= 2:
                        pe.wait_ge(at_done, a + i - 1)
                    for qt in range(2):
                        qs = slice(qt * P, (qt + 1) * P)
                        parts = hd["qk"]
                        for j, (qb_, kb_, p0, pn) in enumerate(parts):
                            ins = mm(ps[:, 4 + i, qt * T:(qt + 1) * T], w[p0:p0 + pn, qb_, qs], w[p0:p0 + pn, kb_, :],
                                     start=(j == 0), stop=(j == len(parts) - 1))
                    ins.then_inc(at_s, 1)

            def outputs(heads, a):
                for i in range(len(heads)):
                    pe.wait_ge(at_p, a + i + 1)
                    if a + i >= 2:
                        pe.wait_ge(at_pt, a + i - 1)
                    for qt in range(2):
                        for kt in range(2):
                            ins = nc.tensor.transpose(ps[:, 6 + i, kt * T + qt * P:kt * T + (qt + 1) * P],
                                                      sm[:, i, qt, kt * P:(kt + 1) * P], ident[:, :])
                    ins.then_inc(at_turned, 1)
                for i, hd in enumerate(heads):
                    pe.wait_ge(at_pt, a + i + 1)
                    vb, v0, vn, p0 = hd["v"]
                    for kt in range(2):
                        ins = mm(ps[p0:p0 + vn, 4 + i, 0:T], w[:, vb, kt * P + v0:kt * P + v0 + vn], pt[:, i, kt, :],
                                 start=(kt == 0), stop=(kt == 1))
                    ins.then_inc(at_o, 1)

            def attend(couples, gate, a):
                scores(couples[0], a)
                p = 0
                for c, heads in enumerate(couples):
                    outputs(heads, a + 2 * c)
                    if c + 1 < len(couples):
                        scores(couples[c + 1], a + 2 * c + 2)
                    if heads[-1]["gate"] is not None:
                        product(ST[gate], p, p % 2)
                        p += 1

            rotate(MLA_ROPE, 0, STORED["uq"] + 6)
            turn_values(MLA_V, w, STORED["ukv"] + 8)
            pe.wait_ge(rp_taken, rotated[0])
            pe.wait_ge(v_copied, turned[0])
            attend(MLA_COUPLES, "evgate_a", 0)
            products("evmoba")
            rotate(MOBA_ROPE, 1, STORED["evmoba"] + 14)
            turn_values(MOBA_V, w, STORED["evmoba"] + 14)
            pe.wait_ge(rp_taken, rotated[0])
            pe.wait_ge(v_copied, turned[0])
            attend(MOBA_COUPLES, "evgate_b", 8)
            products("evout", new="y2", behind=sums_behind("x3"), peel=2)
            if upto < 9:
                return
            products("odin", 0, 1, new="x3")
            sum_squares("x3", 7, 1)
            products("odin", 1)
            products("odmem", new="mem3")
            pe.wait_ge(rope_loaded, 32 * 2)
            rotate(SWA_ROPE, 0, STORED["odin"] + 16)
            rotate(DIL_ROPE, 1, STORED["odin"] + 16)
            turn_values(OD_V, w, STORED["odmem"] + 4)
            pe.wait_ge(rp_taken, rotated[0])
            pe.wait_ge(v_copied, turned[0])
            attend(OD_COUPLES, "odgate", 20)
            products("odout", new="y3", behind=sums_behind("last"), peel=2)
            sum_squares("last", 7, 1)

        @block.scalar
        def _(act):
            step = Steps(act, act_step)
            af = nc.scalar.activation

            def start_of(p, q, at):
                return isinstance(p, int) and p == 0 and q == at

            for buf, name, s in ((cols, "cols", cols_loaded), (h, "x", x_loaded)):
                act.dma_start(buf[:], A[name]).then_inc(s, 16)
            for buf, name in ((ident, "ident"), (gsel, "gsel"), (masks, "masks"), (ob[:, 36:40, :], "lvl"),
                              (rope, "rope_ev"), (rot, "rot_ev")):
                act.dma_start(buf if name == "lvl" else buf[:], A[name]).then_inc(consts_loaded, 16)

            def stream(name, j, par):
                n = STREAM[name] + par
                src = A["p"][int(name[1])] if name[0] == "p" else A["mem"][j] if isinstance(j, int) else (
                    A["mem"][ds(j, 1)].rearrange("o p a b -> (o p) a b"))
                act.dma_start(sm[:, n % 2, :, :], src).then_inc(stream_loaded[n % 2], 16)

            def rounded(st, p, q):
                slot, n, unit, turn = unit_of(st, p, q)
                act.wait_ge(unit_loaded[slot], turn * 16)
                if not (isinstance(p, int) and unit < SLOTS):
                    act.wait_ge(unit_used, unit - SLOTS + 1)
                af(w_hi[:, slot, 0:n], raw[:, slot, 0:n], ACT.Copy).then_inc(act_rounded, 1)

            def crossed(st, p, par):
                pair = st.pair0 + p
                act.wait_ge(unit_used, st.unit0 + p * st.upp + st.upp)
                if not (isinstance(p, int) and pair < 2):
                    act.wait_ge(pair_out, pair - 1)
                af(cross[:, (st.pair0 + par) % 2, 0:st.nb, :], ps[:, banks(st, par), T:2 * T],
                   ACT.Copy).then_inc(cross_ready, 1)

            def last_crossed(name):
                st = ST[name]
                crossed(st, st.pairs - 1, (st.pairs - 1) % 2)

            def stage(name, before=None, first=0, count=None, peel=1, behind=None):
                st = ST[name]
                count = st.pairs if count is None else count

                def pair(p, par):
                    start = isinstance(p, int) and p == 0
                    for q in range(st.upp):
                        rounded(st, p, q)
                        if q == (1 if st.upp == 4 else 2):
                            if not start:
                                crossed(st, p - 1, 1 - par)
                            elif before:
                                last_crossed(before)
                        if behind:
                            behind(p, par, q)

                for p in range(first, first + peel):
                    pair(p, p % 2)
                pairs_loop(act, count, pair, first + peel)

            def square(name, j, par, src, half=None, gain=None):
                at, pairs = NORMS[name]
                n, hf = (1, 0) if half is None else (2, half)
                nth = j * n + (at + hf)
                if not (isinstance(j, int) and nth < 2):
                    act.wait_ge(sq_used, nth - 1)
                slot = (at + par * n + hf) % 2
                if gain is None:
                    af(sq[:, slot, :, :], src, ACT.Square).then_inc(sq_ready, 1)
                else:
                    for b in range(2):
                        ins = af(sq[:, slot, b, :], src[:, b, :], ACT.Square, scale=gain[:, b:b + 1])
                        if b == 0:
                            step.post(ins)
                    ins.then_inc(sq_ready, 1)

            def square_h(name, update, j, par):
                act.wait_ge(h_ready, j + (HR[update] + 1))
                hp = h[:, 2 * j:2 * j + 2, :] if isinstance(j, int) else h[:, ds(j * 2, 2), :]
                if name == "first":
                    square(name, j, par, hp, 0)
                    c = COL_AT["final_norm"]
                    square(name, j, par, hp, 1, cols[:, ds(j * 2 + c, 2)])
                else:
                    square(name, j, par, hp)

            def root(name, which):
                act.wait_ge(var_ready, ROOTS[name] + 1)
                af(rs[:, which, :], tb[:, 0, :], ACT.Sqrt).then_inc(std_ready, 1)

            copied = [0]

            def copy_values(blocks, buf):
                for k in range(0, len(blocks), 2):
                    n = copied[0]
                    act.wait_ge(v_turned, n + 1)
                    nb = len(blocks[k:k + 2])
                    if nb == 2 and blocks[k + 1] != blocks[k] + 1:
                        for j in range(2):
                            ins = af(buf[:, blocks[k + j], :], ps[:, 4 + n % 2, j * T:(j + 1) * T], ACT.Copy)
                            if j == 0:
                                step.post(ins)
                    else:
                        ins = af(buf[:, blocks[k]:blocks[k] + nb, :].rearrange("p a b -> p (a b)"),
                                 ps[:, 4 + n % 2, 0:nb * T], ACT.Copy)
                    ins.then_inc(v_copied, 1)
                    copied[0] += 1

            act.wait_ge(par_in, 1)
            af(small[:, 0:24], small[:, 0:24], ACT.Exp).then_inc(par_exp, 1)
            act.wait_ge(x_loaded, 16)
            for j in range(2):
                stream("mem", j, j)

            def x_norm(p, par, q):
                if p == 1 and q == 1:
                    for j in range(8):
                        square("x", j, j % 2, h[:, 2 * j:2 * j + 2, :])
                if p == 1 and q == 6:
                    root("x", RS_LAYER)

            def mem_norm(p, par, q):
                if q == 5:
                    j = p - 2
                    m = p * 8
                    act.wait_ge(stream_loaded[par], m if par == 0 else m - 8)
                    square("mem", j, par, sm[:, par, :, :])
                    act.wait_ge(sq_ready, j + (NORMS["mem"][0] + 1))
                    if not (isinstance(p, int) and j >= 6):
                        stream("mem", j + 2, par)

            stage("ein", first=0, count=2, peel=2, behind=x_norm)
            stage("ein", first=2, count=8, behind=mem_norm)
            stage("ein", first=8, count=10, peel=2, behind=mem_norm)
            stage("ein", first=10, behind=lambda p, par, q: (
                root("mem", RS_MEM) if isinstance(p, int) and p == 10 and q == 5 else None))
            stream("p0", 0, 0)
            stage("ein_zb", "ein")
            last_crossed("ein_zb")
            if upto < 1:
                return
            act.wait_ge(stored, STORED["ein"] + 12)
            act.wait_ge(par_done, 1)
            sg = ob[:, 16:24, :]
            af(sg, w[:, 0:8, :], ACT.Sigmoid).then_inc(hg_sig, 1)
            af(ob[:, 8:16, :], w[:, 8:16, :], ACT.Sigmoid, scale=-1.0).then_inc(hg_sig, 1)
            act.wait_ge(hg_q, 1)
            af(sg, w[:, 8:16, :], ACT.Sigmoid).then_inc(hg_sig, 1)
            act.wait_ge(hg_sig, 3)
            for hd in range(8):
                af(w[:, 8 + hd, :], ob[:, 16 + hd, :], ACT.Ln, bias=small[:, 24 + hd:25 + hd],
                   scale=small[:, 32 + hd:33 + hd]).then_inc(hg_logf, 1)
            copy_values(range(16, 24), w)
            for g in range(2):
                for level in range(1, 9):
                    n = 8 * g + level
                    e = ob[:, 16:20, :] if level % 2 else ob[:, 34:38, :]
                    act.wait_ge(hg_diff, n)
                    af(e, e, ACT.Exp).then_inc(hg_exp, 1)
                act.wait_ge(hg_o, g + 1)
                for k in range(2):
                    af(w[:, 4 * g + 2 * k:4 * g + 2 * k + 2, :].rearrange("p a b -> p (a b)"), ps[:, 6 + k, :],
                       ACT.Copy).then_inc(hg_ocopied, 1)
            act.wait_ge(hg_ocopied, 4)
            for k in range(4):
                af(ob[:, 16 + 2 * k:18 + 2 * k, :], w[:, 2 * k:2 * k + 2, :], ACT.Square).then_inc(hn_gate, 1)
            act.wait_ge(stored, STORED["ein_zb"] + 4)
            af(ob[:, 24:32, :], w[:, 24:32, :], ACT.Sigmoid).then_inc(hn_gate, 1)
            act.wait_ge(hn_var, 1)
            af(ob[:, 16:24, :], ob[:, 32:40, :], ACT.Sqrt).then_inc(hn_std, 1)
            if upto < 2:
                return
            act.wait_ge(hn_gate, 6)
            for j, name in enumerate(("w_r", "w_i")):
                act.dma_start(ob[:, 16 + 4 * j:20 + 4 * j, :].rearrange("p a b -> p (a b)"), A[name]).then_inc(lr_w, 16)
            for n in range(8):
                act.wait_ge(lr_pre, n + 1)
                for j, b in enumerate(("b_b_r", "b_b_i")):
                    af(w[:, 8 + 8 * j + n, :], ps[:, 4 + n % 2, j * T:(j + 1) * T], ACT.Sigmoid,
                       bias=col(b, 1, n)).then_inc(lr_act, 1)
            act.wait_ge(lr_act, 16)
            for n in range(8):
                af(ob[:, 24 + n, :], w[:, 8 + n, :], ACT.Tanh, scale=small[:, 40 + n:41 + n]).then_inc(lr_th, 1)
            for n in range(8):
                af(ob[:, 16 + n, :], w[:, 8 + n, :], ACT.Exp, scale=small[:, 48 + n:49 + n]).then_inc(lr_th, 1)
            act.wait_ge(lr_fix, 1)
            af(ob[:, 24:32, :], ob[:, 24:32, :], ACT.Sqrt, scale=2.0).then_inc(lr_root, 1)
            af(ob[:, 32:40, :], ob[:, 0:8, :], ACT.Sigmoid).then_inc(lr_root, 1)
            if upto < 3:
                return

            def tail(l, norm):
                ple, so, sg = ST[f"ple{l}"], ST["eout" if l == 0 else "oout"], ST[f"gate{l}"]

                def ple_norm(p, par, q):
                    if q == 6:
                        act.wait_ge(pair_out, p + (ple.pair0 + 1))
                        square(ple.name, p, par, w[:, ds(p * 2 + 16, 2), :])

                def gate_norm(p, par, q):
                    if q == 4 and isinstance(p, int) and p == 0:
                        root(ple.name, RS_PLE)
                    elif q == 4:
                        gate_sigmoid(sg, p - 1)
                    elif q == 7 and not (isinstance(p, int) and p == 0):
                        square_h(norm, sg.name, p - 1, 1 - par)

                stage(ple.name)
                stage(so.name, ple.name, behind=ple_norm)
                stage(sg.name, so.name, behind=gate_norm, peel=2)

            def gate_sigmoid(sg, p):
                act.wait_ge(pair_out, p + (sg.pair0 + 1))
                af(tb[:, :, :], tb[:, :, :], ACT.Sigmoid).then_inc(g_sig, 1)

            tail(0, "h1")
            if upto < 4:
                return

            def end_of_gate(sg, norm):
                def behind(p, par, q):
                    if q == 4:
                        gate_sigmoid(sg, 7)
                    if q == 7:
                        square_h(norm, sg.name, 7, 1)
                return behind

            stage("ogate", "gate0", behind=end_of_gate(ST["gate0"], "h1"))
            stage("oqk", "ogate", behind=lambda p, par, q: root("h1", RS_LAYER) if start_of(p, q, 5) else None)
            stage("ov", "oqk")
            stage("oog", "ov")
            stage("oz", "oog")
            last_crossed("oz")
            if upto < 5:
                return
            act.wait_ge(mg_in, 1)
            af(w[:, 36, :], w[:, 36, :], ACT.Exp, scale=-1.0).then_inc(mg_exp, 1)
            for n in range(16):
                act.wait_ge(cv_pre, n + 1)
                if n >= 2:
                    act.wait_ge(cv_done, n - 1)
                af(sm[:, n % 2, 0, :], w[:, 38 + n % 2, :], ACT.Sigmoid).then_inc(cv_sig, 1)
            act.wait_ge(mg_g, 2)
            af(small[:, 0:16], ps[:, 7, 0:16], ACT.Copy).then_inc(mg_gcols, 1)
            copy_values(range(16, 32), w)
            act.wait_ge(mg_gcols, 1)
            act.wait_ge(cv_done, 16)
            for hd in range(8):
                act.wait_ge(ml_mask, hd + 1)
                for kt in range(2):
                    af(sm[:, 0, kt, :], sm[:, 0, kt, :], ACT.Exp, scale=-1.0,
                       bias=small[:, 8 * kt + hd:8 * kt + hd + 1]).then_inc(ml_e, 1)
                act.wait_ge(ml_s, hd + 1)
                if hd:
                    act.wait_ge(ml_den, hd)
                af(w[:, 40, :], ps[:, 5, T:2 * T], ACT.Exp, scale=-1.0).then_inc(ml_e, 1)
                act.wait_ge(ml_o, hd + 1)
                af(w[:, 41, :], ps[:, 7, 0:T], ACT.Abs).then_inc(ml_e, 1)
                act.wait_ge(ml_h, hd + 1)
                if hd:
                    act.wait_ge(ml_sums, hd)
                af(pt[:, 1, :, :], w[:, 16 + 2 * hd:18 + 2 * hd, :], ACT.Square).then_inc(ml_sq, 1)
                act.wait_ge(ml_var, hd + 1)
                af(w[:, 41, :], w[:, 42, :], ACT.Sqrt).then_inc(ml_std, 1)
            act.wait_ge(stored, STORED["oz"] + 8)
            af(w[:, 0:16, :], oa[:, 0:16, :], ACT.Sigmoid).then_inc(y_gate, 1)
            act.wait_ge(y_done, 1)
            af(w[:, 0:16, :], oa[:, 16:32, :], ACT.Sigmoid).then_inc(y_gate, 1)
            act.wait_ge(ml_std, 8)
            stream("p1", 0, 0)
            if upto < 6:
                return
            tail(1, "first")
            if upto < 7:
                return
            act.wait_ge(x_ready, XR["p1"] + 1)
            for j in range(2):
                stream("mem2", j, j)

            def first_norm(p, par, q):
                if p == 0 and q == 5:
                    root("first", RS_Q)
                if p == 1 and q == 1:
                    root("x2", RS_LAYER)
                if q in (3, 6):
                    j = 2 * p + q // 6
                    act.wait_ge(x_ready, XR["mem2"] + j + 1)
                    stream("mem2", j + 2, j % 2)

            def rank_norms(p, par, q):
                if p == 1 and q in (4, 6):
                    j = q // 6
                    act.wait_ge(stored, STORED["evc"] + j + 1)
                    square("cq", j, j, w[:, 29 + 2 * j:31 + 2 * j, :])
                if p == 2 and q == 3:
                    root("cq", RS_Q)
                if p == 2 and q == 4:
                    act.wait_ge(stored, STORED["evc"] + 3)
                    square("ckv", 0, 0, w[:, 33:35, :])
                if p == 3 and q == 4:
                    root("ckv", RS_KV)

            stage("evkpe", "gate1", behind=end_of_gate(ST["gate1"], "first"))
            stage("evc", "evkpe", peel=3, behind=first_norm)
            stage("evmem", "evc", peel=4, behind=rank_norms)
            stage("uq", "evmem")
            stage("ukv", "uq")
            last_crossed("ukv")
            if upto < 8:
                return

            def exps(heads, a):
                for i, hd in enumerate(heads):
                    act.wait_ge(at_neg, a + i + 1)
                    s4 = small[:, 16 * i:16 * i + 16]
                    for qt in range(2):
                        ins = af(sm[:, i, qt, :], sm[:, i, qt, :], ACT.Exp, bias=s4[:, qt:qt + 1],
                                 accum_out=s4[:, 2 + qt:3 + qt])
                        if qt == 0 or hd["sink"] is not None:
                            step.post(ins)
                    if hd["sink"] is not None:
                        ins = af(s4[:, 4:6], s4[:, 0:2], ACT.Exp, bias=col("sinks", 1, hd["sink"]))
                    ins.then_inc(at_e, 1)

            def turned_copy(heads, a):
                for i in range(len(heads)):
                    act.wait_ge(at_turned, a + i + 1)
                    af(pt[:, i, :, :].rearrange("p a b -> p (a b)"), ps[:, 6 + i, :], ACT.Copy).then_inc(at_pt, 1)

            gates = [16]

            def gated(st, p):
                crossed(st, p, p % 2)
                act.wait_ge(g_pre, gates[0] - 15)
                af(cross[:, (st.pair0 + p) % 2, :, :], tb[:, :, :], ACT.Sigmoid).then_inc(g_sig, 1)
                gates[0] += 1

            def attend(couples, gate, a):
                p, due = 0, False
                for c, heads in enumerate(couples):
                    exps(heads, a + 2 * c)
                    if due:
                        gated(ST[gate], p)
                        p += 1
                    turned_copy(heads, a + 2 * c)
                    due = heads[-1]["gate"] is not None
                gated(ST[gate], p)

            copy_values(MLA_V, w)
            attend(MLA_COUPLES, "evgate_a", 0)
            stage("evmoba")
            last_crossed("evmoba")
            copy_values(MOBA_V, w)
            attend(MOBA_COUPLES, "evgate_b", 8)
            act.wait_ge(at_done, 20)
            for buf, name in ((rope, "rope_od"), (rot, "rot_od")):
                act.dma_start(buf[:], A[name]).then_inc(rope_loaded, 32)
            for j in range(2):
                stream("mem3", j, j)

            def out_norm(st, norm):
                def behind(p, par, q):
                    if q == 8 and not (isinstance(p, int) and p == 0):
                        square_h(norm, st.name, p - 1, 1 - par)
                return behind

            def x3_norm(p, par, q):
                if isinstance(p, int) and p == 0 and q == 5:
                    square_h("x3", "evout", 7, 1)
                if isinstance(p, int) and p == 1 and q == 4:
                    root("x3", RS_LAYER)
                if q == 7:
                    act.wait_ge(x_ready, p + (XR["mem3"] + 1))
                    stream("mem3", p + 2, par)

            stage("evout", behind=out_norm(ST["evout"], "x3"), peel=2)
            if upto < 9:
                return
            stage("odin", "evout", count=6, peel=2, behind=x3_norm)
            stage("odin", first=6, peel=0)
            stage("odmem", "odin")
            last_crossed("odmem")
            copy_values(OD_V, w)
            attend(OD_COUPLES, "odgate", 20)
            stage("odout", behind=out_norm(ST["odout"], "last"), peel=2)
            last_crossed("odout")
            square_h("last", "odout", 7, 1)
            root("last", RS_LAYER)

        @block.vector
        def _(dve):
            step = Steps(dve, dve_step)
            tt, ts, stt, cp = (nc.vector.tensor_tensor, nc.vector.tensor_scalar, nc.vector.scalar_tensor_tensor,
                               nc.vector.tensor_copy)

            def split(src, gain, x, kt, count):
                if gain is not None:
                    step(tt(tb[:, :, :], src, wide(gain, 2), MUL))
                    src = tb[:, :, :]
                hi = x[:, ds(kt, 2), 0:T]
                step(cp(hi, src))
                tt(x[:, ds(kt, 2), T:2 * T], src, hi.bitcast(F32), SUB).then_inc(x_ready, 1)
                dve.wait_ge(x_ready, count)

            def take(st, p, par, dst):
                pair = st.pair0 + p
                dve.wait_ge(cross_ready, pair + 1)
                tt(dst, ps[:, banks(st, par), 0:T], cross[:, (st.pair0 + par) % 2, 0:st.nb, :],
                   ADD).then_inc(pair_out, 1)
                dve.wait_ge(pair_out, pair + 1)

            def store(name, buf, at, scale, first=0, count=None):
                st = ST[name]

                def pair(p, par):
                    dst = buf[:, ds(p * st.nb + at, st.nb), :]
                    take(st, p, par, dst)
                    tt(dst, dst, along(rs[:, scale, :], st.nb), MUL).then_inc(stored, 1)

                pairs_loop(dve, st.pairs if count is None else count, pair, first)
                dve.wait_ge(stored, STORED[name] + (st.pairs if count is None else count))

            def root(name, which, width):
                at, pairs = NORMS[name]
                dve.wait_ge(sq_used, at + pairs)
                ts(tb[:, 0, :], ps[:, 7, 0:T], 1.0 / width, EPS, MUL, ADD).then_inc(var_ready, 1)
                dve.wait_ge(std_ready, ROOTS[name] + 1)
                inverse(rs[:, which, :], tb[:, 0, :], tb[:, 1, :])

            def inverse(r, v, t):
                step(nc.vector.reciprocal(r, r))
                step(tt(t, r, r, MUL))
                step(tt(t, t, v, MUL))
                step(ts(t, t, -0.5, 1.5, MUL, ADD))
                step(tt(r, r, t, MUL))

            def streamed(name, j, par, gain, x, kt):
                n = STREAM[name] + par
                loads = 16 * (n // 2 + 1) if isinstance(j, int) and j == par else (j - par) * 8 + 16 * (n // 2 + 1)
                dve.wait_ge(stream_loaded[n % 2], loads)
                split(sm[:, n % 2, :, :], gain, x, kt, j + (XR[name] + 1))

            def log1p(y, z, zz, p):
                step(ts(z, y, 2.0, None, ADD))
                step(nc.vector.reciprocal(z, z))
                step(tt(z, z, y, MUL))
                step(tt(zz, z, z, MUL))
                step(ts(p, zz, 1.0 / 21, None, MUL))
                for k in range(9, 0, -1):
                    step(stt(p, p, 1.0 / (2 * k + 1), zz, ADD, MUL))
                step(stt(p, p, 1.0, z, ADD, MUL))
                step(ts(p, p, 2.0, None, MUL))

            nc.vector.memset(ones[:, :], 1.0).then_inc(ones_set, 1)
            dve.wait_ge(consts_loaded, 16 * 6)
            step(cp(lvl[:, :, :].rearrange("p a b -> p (a b)"), ob[:, 36:40, :].rearrange("p a b -> p (a b)")))
            dve.wait_ge(cols_loaded, 16)
            l0, l1, lam = col("a_lb0"), col("a_lb1"), col("b_lambda")
            step(tt(small[:, 24:32], l0, l1, MAX))
            step(tt(small[:, 0:8], l0, small[:, 24:32], SUB))
            step(tt(small[:, 8:16], l1, small[:, 24:32], SUB))
            step(stt(small[:, 40:48], lam, -1.0, lam, MUL, MAX))
            ts(small[:, 16:24], small[:, 40:48], -1.0, None, MUL).then_inc(par_in, 1)
            dve.wait_ge(par_exp, 1)
            step(tt(small[:, 8:16], small[:, 0:8], small[:, 8:16], ADD))
            step(nc.vector.reciprocal(small[:, 8:16], small[:, 8:16]))
            step(tt(small[:, 24:32], small[:, 0:8], small[:, 8:16], MUL))
            step(ts(small[:, 32:40], small[:, 24:32], -1.0, 1.0, MUL, ADD))
            log1p(small[:, 16:24], small[:, 0:8], small[:, 8:16], small[:, 40:48])
            step(ts(small[:, 0:8], lam, -1.0, 0.0, MUL, MAX))
            step(tt(small[:, 40:48], small[:, 40:48], small[:, 0:8], ADD))
            step(ts(small[:, 40:48], small[:, 40:48], 8.0, None, MUL))
            ts(small[:, 48:56], small[:, 40:48], -1.0, None, MUL).then_inc(par_done, 1)
            lb, oml = small[:, 24:32], small[:, 32:40]
            step(tt(col("ev_norm"), col("ev_norm"), col("final_norm"), MUL))
            dve.wait_ge(x_loaded, 16)
            for j in range(8):
                split(h[:, 2 * j:2 * j + 2, :], col("e_norm", 2, 2 * j), xa, 2 * j, XR["x"] + j + 1)
            root("x", RS_LAYER, D)
            store("ein", w, 0, RS_LAYER, 0, 10)
            root("mem", RS_MEM, D)
            store("ein", w, 0, RS_LAYER, 10)
            streamed("p0", 0, 0, None, xs, 0)
            store("ein_zb", ob, 0, RS_LAYER)
            if upto < 1:
                return
            dve.wait_ge(par_done, 1)
            dve.wait_ge(hg_sig, 1)
            q, kk = w[:, 0:8, :], ob[:, 8:16, :]
            tt(q, q, ob[:, 16:24, :], MUL).then_inc(hg_q, 1)
            dve.wait_ge(hg_sig, 2)
            tt(kk, kk, wide(oml, 8), MUL).then_inc(hg_qk, 1)
            for hd in range(8):
                dve.wait_ge(hg_logf, hd + 1)
                for c in range(4):
                    bc = w[:, 8 + hd, 64 * c:64 * c + 64]
                    step.post(nc.vector.tensor_tensor_scan(bc, ones[:, 0:64], bc, 0.0, MUL, ADD))
            step.wait()
            dve.wait_ge(hg_q, 1)
            dve.wait_ge(hg_qk, 1)
            dve.wait_ge(hg_logf, 8)
            am = ob[:, 28:34, :].rearrange("p a b -> p (a b)")

            for g in range(2):
                qg, kg = w[:, 4 * g:4 * g + 4, :], ob[:, 8 + 4 * g:12 + 4 * g, :]
                b = w[:, 8 + 4 * g:12 + 4 * g, :].rearrange("p a b -> p (a b)")

                def differences(level):
                    e = (ob[:, 16:20, :] if level % 2 else ob[:, 34:38, :]).rearrange("p a b -> p (a b)")
                    size = 2 ** level
                    half = size // 2
                    ev = e.rearrange("p (n s) -> p n s", s=size)
                    bv = b.rearrange("p (n s) -> p n s", s=size)
                    n = 1024 // size
                    if level <= 6:
                        mid = bv[:, :, half - 1:half].to_broadcast([P, n, half])
                        step.post(tt(ev[:, :, half:size], bv[:, :, half:size], mid, SUB))
                        ins = tt(ev[:, :, 0:half], mid, bv[:, :, 0:half], SUB)
                    elif level == 7:
                        step.post(cp(ev[:, :, 64:128], bv[:, :, 64:128]))
                        ins = tt(ev[:, :, 0:64], bv[:, :, 63:64].to_broadcast([P, n, 64]), bv[:, :, 0:64], SUB)
                    else:
                        def last(c):
                            return bv[:, :, 64 * c + 63:64 * c + 64].to_broadcast([P, n, 64])

                        step.post(cp(ev[:, :, 128:192], bv[:, :, 128:192]))
                        step.post(tt(ev[:, :, 192:256], bv[:, :, 192:256], last(2), ADD))
                        step.post(tt(ev[:, :, 64:128], last(1), bv[:, :, 64:128], SUB))
                        step(tt(ev[:, :, 0:64], last(0), bv[:, :, 0:64], SUB))
                        ins = tt(ev[:, :, 0:64], ev[:, :, 0:64], last(1), ADD)
                    ins.then_inc(hg_diff, 1)

                def scaled(level):
                    e = ob[:, 16:20, :] if level % 2 else ob[:, 34:38, :]
                    dve.wait_ge(hg_exp, 8 * g + level)
                    if level > 1:
                        dve.wait_ge(hg_lv_out, 9 * g + level)
                    elif g:
                        dve.wait_ge(hg_lv_out, 9)
                    step.post(tt(ob[:, 20:24, :], qg, e, MUL))
                    tt(ob[:, 24:28, :], kg, e, MUL).then_inc(hg_lv_in, 1)
                    dve.wait_ge(hg_lv_in, 8 * g + level)

                def masked(level):
                    n = 9 * g + level
                    dve.wait_ge(hg_lv_out, n + 1)
                    if level < 8:
                        nc.vector.copy_predicated(
                            am[:, 0:1024].rearrange("p (n s) -> p n s", s=P),
                            lvl[:, level, :].unsqueeze(1).to_broadcast([P, 8, P]),
                            ps[:, 4:6, :].rearrange("p a b -> p (a b)").rearrange("p (n s) -> p n s", s=P),
                        ).then_inc(hg_masked, 1)
                    else:
                        cp(am[:, 1024:1536], ps[:, 4, :]).then_inc(hg_masked, 1)
                    dve.wait_ge(hg_masked, n + 1)

                if g:
                    dve.wait_ge(hg_o, 1)
                dve.wait_ge(consts_loaded, 16 * 6)
                step(nc.vector.memset(am[:, 0:1024], 0.0))
                differences(1)
                masked(0)
                for level in range(1, 9):
                    if level < 8:
                        differences(level + 1)
                    scaled(level)
                    masked(level)
            dve.wait_ge(hn_sums, 1)
            rh = ob[:, 32:40, :]
            ts(rh.rearrange("p a b -> p (a b)"), ps[:, 4:8, :].rearrange("p a b -> p (a b)"), 1.0 / P, EPS, MUL,
               ADD).then_inc(hn_var, 1)
            ya, z = w[:, 0:8, :], w[:, 24:32, :]
            dve.wait_ge(hn_gate, 5)
            step(tt(z, z, ob[:, 24:32, :], MUL))
            step(tt(z, z, wide(col("a_norm"), 8), MUL))
            dve.wait_ge(hg_ocopied, 4)
            step(tt(ya, ya, z, MUL))
            dve.wait_ge(hn_std, 1)
            inverse(ob[:, 16:24, :], rh, ob[:, 24:32, :])
            tt(ya, ya, ob[:, 16:24, :], MUL).then_inc(hn_gate, 1)
            dve.wait_ge(hn_gate, 6)
            if upto < 2:
                return
            for n in range(8):
                xb_, xc = w[:, 32 + n, :], ob[:, 8 + n, :]

                def tap(k):
                    return col("b_conv_w", 1, 8 * k + n)

                step(ts(xc, xb_, tap(3), col("b_conv_b", 1, n), MUL, ADD))
                for k in (2, 1):
                    s = 3 - k
                    step(stt(xc[:, s:T], xb_[:, 0:T - s], tap(k), xc[:, s:T], MUL, ADD))
                stt(xc[:, 3:T], xb_[:, 0:T - 3], tap(0), xc[:, 3:T], MUL, ADD).then_inc(lr_conv, 1)
            dve.wait_ge(lr_conv, 8)
            th, t1, ig, xc = ob[:, 24:32, :], ob[:, 32:40, :], w[:, 16:24, :], ob[:, 8:16, :]
            dve.wait_ge(lr_act, 16)
            step(tt(ig, ig, xc, MUL))
            dve.wait_ge(lr_th, 8)
            step(ts(t1, th, 1.0, None, ADD))
            step(nc.vector.reciprocal(t1, t1))
            tt(th, th, t1, MUL).then_inc(lr_fix, 1)
            dve.wait_ge(lr_root, 1)
            step(tt(ig, ig, th, MUL))
            dve.wait_ge(lr_th, 16)
            for n in range(8):
                step.post(nc.vector.tensor_tensor_scan(ob[:, 8 + n, :], ob[:, 16 + n, :], w[:, 16 + n, :], 0.0, MUL, ADD))
            step.wait()
            yb, zb = w[:, 8:16, :], ob[:, 0:8, :]
            dve.wait_ge(lr_root, 2)
            step(tt(zb, zb, t1, MUL))
            step(tt(yb, ob[:, 8:16, :], zb, MUL))
            for j in range(8):
                split(w[:, 2 * j:2 * j + 2, :], None, xb, 2 * j, XR["y0"] + j + 1)
            if upto < 3:
                return

            def tail(l, x_out, x_h, x_next, gain_next, x_next_buf):
                st = ST[f"ple{l}"]
                pairs_loop(dve, 8, lambda p, par: take(st, p, par, w[:, ds(p * 2 + 16, 2), :]))
                so, xo = ST["eout" if l == 0 else "oout"], X[ST[f"gate{l}"].x]

                def out_pair(p, par):
                    hp = h[:, ds(p * 2, 2), :]
                    take(so, p, par, tb[:, :, :])
                    step(tt(hp, hp, tb[:, :, :], ADD))
                    split(hp, None, xo, p * 2, p + (XR[x_h] + 1))

                pairs_loop(dve, 8, out_pair, steps=step, per=2)
                root(f"ple{l}", RS_PLE, D)
                sg = ST[f"gate{l}"]

                def gate_pair(p, par):
                    hp, pl = h[:, ds(p * 2, 2), :], w[:, ds(p * 2 + 16, 2), :]
                    pair = sg.pair0 + p
                    step(tt(pl, pl, along(rs[:, RS_PLE, :], 2), MUL))
                    step(tt(pl, pl, wide(col(f"ple_norm{l}", 2, p * 2), 2), MUL))
                    dve.wait_ge(cross_ready, pair + 1)
                    tt(tb[:, :, :], ps[:, banks(sg, par), 0:T], cross[:, (sg.pair0 + par) % 2, :, :],
                       ADD).then_inc(pair_out, 1)
                    dve.wait_ge(g_sig, p + (8 * l + 1))
                    step(tt(tb[:, :, :], tb[:, :, :], pl, MUL))
                    tt(hp, hp, tb[:, :, :], ADD).then_inc(h_ready, 1)
                    dve.wait_ge(h_ready, p + (HR[f"gate{l}"] + 1))
                    split(hp, col(gain_next, 2, p * 2), x_next_buf, p * 2, p + (XR[x_next] + 1))

                pairs_loop(dve, 8, gate_pair, steps=step, per=5)

            tail(0, "eout", "h0", "h1", "o_norm", xb)
            if upto < 4:
                return
            root("h1", RS_LAYER, D)
            store("ogate", w, 32, RS_LAYER)
            store("oqk", w, 0, RS_LAYER)
            store("ov", w, 16, RS_LAYER)
            store("oog", oa, 0, RS_LAYER)
            store("oz", oa, 16, RS_LAYER)
            if upto < 5:
                return
            gx, gb, gm, t0, t1, t2, t3 = (w[:, 32 + i, :] for i in range(7))
            step(ts(gx, gx, col("c_gate_b"), None, ADD))
            step(ts(t0, gx, 0.0, None, ALU.min))
            stt(t1, gx, -1.0, gx, MUL, MAX).then_inc(mg_in, 1)
            dve.wait_ge(mg_exp, 1)
            log1p(t1, t2, t3, gm)
            step(tt(t0, t0, gm, SUB))
            step(ts(t2, t1, 0.0, 1.0, MUL, ADD))
            nc.vector.tensor_tensor_scan(gb, t2, t0, 0.0, MUL, ADD).then_inc(mg_lf, 1)
            dve.wait_ge(mg_lf, 1)
            dve.wait_ge(mg_g, 1)
            nc.vector.tensor_tensor_scan(gm, t2, ps[:, 6, 0:T], 0.0, MUL, MAX).then_inc(mg_max, 1)
            dve.wait_ge(mg_max, 1)
            for n in range(16):
                src, acc = w[:, n, :], w[:, 38 + n % 2, :]

                def tap(k):
                    return col("c_conv_w", 1, 16 * k + n)

                step(ts(acc, src, tap(3), col("c_conv_b", 1, n), MUL, ADD))
                for k in (2, 1):
                    s = 3 - k
                    step(stt(acc[:, s:T], src[:, 0:T - s], tap(k), acc[:, s:T], MUL, ADD))
                stt(acc[:, 3:T], src[:, 0:T - 3], tap(0), acc[:, 3:T], MUL, ADD).then_inc(cv_pre, 1)
                dve.wait_ge(cv_pre, n + 1)
                dve.wait_ge(cv_sig, n + 1)
                tt(src, acc, sm[:, n % 2, 0, :], MUL).then_inc(cv_done, 1)
            dve.wait_ge(cv_done, 16)
            for hd in range(8):
                dve.wait_ge(ml_s, hd + 1)
                tt(sm[:, 0, :, :], masks[:, M_LSTM, :, :], along(ps[:, 5, 0:T], 2), ADD).then_inc(ml_mask, 1)
                dve.wait_ge(ml_e, 4 * hd + 2)
                if hd:
                    dve.wait_ge(ml_o, hd)
                stt(pt[:, 0, :, :].rearrange("p a b -> p (a b)"), ps[:, 4, :], float(P) ** -0.5,
                    sm[:, 0, :, :].rearrange("p a b -> p (a b)"), MUL, MUL).then_inc(ml_p, 1)
                dve.wait_ge(ml_p, hd + 1)
                dve.wait_ge(ml_e, 4 * hd + 4)
                tt(w[:, 43, :], w[:, 40, :], w[:, 41, :], MAX).then_inc(ml_den, 1)
                dve.wait_ge(ml_den, hd + 1)
                step(nc.vector.reciprocal(w[:, 43, :], w[:, 43, :]))
                hb = w[:, 16 + 2 * hd:18 + 2 * hd, :]
                tt(hb, ps[:, 6, :].rearrange("p (a b) -> p a b", b=T), along(w[:, 43, :], 2), MUL).then_inc(ml_h, 1)
                dve.wait_ge(ml_sums, hd + 1)
                ts(w[:, 42, :], ps[:, 7, T:2 * T], 1.0 / (2 * P), EPS, MUL, ADD).then_inc(ml_var, 1)
                dve.wait_ge(ml_std, hd + 1)
                inverse(w[:, 41, :], w[:, 42, :], w[:, 43, :])
                step(tt(hb, hb, along(w[:, 41, :], 2), MUL))
            yc = w[:, 16:32, :]
            step(tt(yc, yc, wide(col("c_norm"), 16), MUL))
            dve.wait_ge(y_gate, 1)
            tt(yc, yc, w[:, 0:16, :], MUL).then_inc(y_done, 1)
            dve.wait_ge(y_done, 1)
            step(tt(yc, yc, oa[:, 16:32, :], MUL))
            dve.wait_ge(y_gate, 2)
            step(tt(yc, yc, w[:, 0:16, :], MUL))
            streamed("p1", 0, 0, None, xs, 0)
            for j in range(8):
                split(w[:, 16 + 2 * j:18 + 2 * j, :], None, xa, 2 * j, XR["y1"] + j + 1)
            if upto < 6:
                return
            tail(1, "oout", "h2", "x2", "ev_norm", xa)
            if upto < 7:
                return
            def memory(name, j, par, gain):
                streamed(name, j, par, col(gain, 2, j * 2), xb, j * 2)

            for j in range(2):
                memory("mem2", j, j, "ev_mem_norm")
            root("first", RS_Q, D)
            rf, rl, v = rs[:, RS_Q, :], rs[:, RS_LAYER, :], tb[:, 0, :]
            step(tt(rl, rf, rf, MUL))
            step(stt(v, ps[:, 7, T:2 * T], 1.0 / D, rl, MUL, MUL))
            ts(v, v, EPS, None, ADD).then_inc(var_ready, 1)
            dve.wait_ge(std_ready, ROOTS["x2"] + 1)
            inverse(rl, v, tb[:, 1, :])
            step(tt(rl, rl, rf, MUL))
            store("evkpe", w, 28, RS_LAYER)
            for p in range(3):
                for j in (2 * p + 2, 2 * p + 3):
                    memory("mem2", j, j % 2, "ev_mem_norm")
                store("evc", w, 29, RS_LAYER, p, p + 1)
            for j in range(2):
                split(w[:, 29 + 2 * j:31 + 2 * j, :], col("ev_q_norm", 2, 2 * j), xs, 2 * j, XR["cq"] + j + 1)
            split(w[:, 33:35, :], col("ev_kv_norm", 2, 0), xs, 4, XR["ckv"] + 1)
            step(tt(h[:, :, :], h[:, :, :], along(rf, 16), MUL))
            step(tt(h[:, :, :], h[:, :, :], wide(col("final_norm"), 16), MUL))
            store("evmem", w, 35, RS_MEM, 0, 2)
            root("cq", RS_Q, 512)
            store("evmem", w, 35, RS_MEM, 2, 3)
            root("ckv", RS_KV, 256)
            store("evmem", w, 35, RS_MEM, 3, 4)
            store("uq", w, 0, RS_Q)
            store("ukv", w, 12, RS_KV)
            if upto < 8:
                return

            rotated = [0]

            def rotate(blocks, kind):
                for k in range(0, len(blocks), 2):
                    n, two = rotated[0], blocks[k:k + 2]
                    dve.wait_ge(rp_sums, n + 1)
                    for j, bl in enumerate(two):
                        step.post(tt(tb[:, j, :], ps[:, 6 + n % 2, j * T:(j + 1) * T], rope[:, kind, 1, :], MUL))
                        step.post(tt(w[:, bl, :], w[:, bl, :], rope[:, kind, 0, :], MUL))
                    step.wait()
                    for j, bl in enumerate(two):
                        ins = tt(w[:, bl, :], w[:, bl, :], tb[:, j, :], ADD)
                        if j + 1 < len(two):
                            step.post(ins)
                    ins.then_inc(rp_taken, 1)
                    dve.wait_ge(rp_taken, n + 1)
                    rotated[0] += 1

            def softmax_in(heads, a):
                for i, hd in enumerate(heads):
                    s4 = small[:, 16 * i:16 * i + 16]
                    dve.wait_ge(at_s, a + i + 1)
                    if a + i >= 2:
                        dve.wait_ge(at_turned, a + i - 1)
                    dst, src = sm[:, i, :, :].rearrange("p a b -> p (a b)"), ps[:, 4 + i, :]
                    if hd["mask"] is None:
                        step(ts(dst, src, hd["scale"], None, MUL))
                    else:
                        step(stt(dst, src, hd["scale"], masks[:, hd["mask"], :, :].rearrange("p a b -> p (a b)"), MUL,
                                 ADD))
                    if hd["sink"] is None:
                        nc.vector.tensor_reduce(s4[:, 0:2], sm[:, i, :, :], AX, MAX, negate=True).then_inc(at_neg, 1)
                    else:
                        step(nc.vector.tensor_reduce(s4[:, 6:8], sm[:, i, :, :], AX, MAX))
                        ts(s4[:, 0:2], s4[:, 6:8], col("sinks", 1, hd["sink"]), -1.0, MAX, MUL).then_inc(at_neg, 1)

            def softmax_out(heads, a):
                for i, hd in enumerate(heads):
                    s4 = small[:, 16 * i:16 * i + 16]
                    dve.wait_ge(at_e, a + i + 1)
                    if hd["sink"] is not None:
                        step(tt(s4[:, 2:4], s4[:, 2:4], s4[:, 4:6], ADD))
                    step(nc.vector.reciprocal(s4[:, 2:4], s4[:, 2:4]))
                    tt(sm[:, i, :, :], sm[:, i, :, :], wide(s4[:, 2:4], 2), MUL).then_inc(at_p, 1)

            def keep(heads, a):
                for i, hd in enumerate(heads):
                    vb, v0, vn, p0 = hd["v"]
                    dve.wait_ge(at_o, a + i + 1)
                    cp(w[p0:p0 + vn, hd["o"], :], ps[p0:p0 + vn, 4 + i, 0:T]).then_inc(at_done, 1)

            gates = [16]

            def gated(st, p, blocks, x_at, x_count):
                pair = st.pair0 + p
                dve.wait_ge(cross_ready, pair + 1)
                cr = cross[:, (st.pair0 + p) % 2, :, :]
                step(tt(tb[:, :, :], ps[:, banks(st, p % 2), 0:T], cr, ADD))
                tt(tb[:, :, :], tb[:, :, :], along(rs[:, RS_LAYER, :], 2), MUL).then_inc(g_pre, 1)
                dve.wait_ge(g_sig, gates[0] + 1)
                gates[0] += 1
                tt(tb[:, :, :], tb[:, :, :], cr, MUL).then_inc(pair_out, 1)
                dve.wait_ge(pair_out, pair + 1)
                for j, bl in enumerate(blocks):
                    step.post(tt(tb[:, j, :], tb[:, j, :], w[:, bl, :], MUL))
                step.wait()
                split(tb[:, :, :], None, xb, x_at, x_count)

            def attend(couples, gate, a, x_at, x_count):
                p, due = 0, None
                for c, heads in enumerate(couples):
                    softmax_in(heads, a + 2 * c)
                    softmax_out(heads, a + 2 * c)
                    if due:
                        gated(ST[gate], p, due, x_at + 2 * p, x_count + p + 1)
                        p += 1
                    keep(heads, a + 2 * c)
                    due = heads[-1]["gate"]
                dve.wait_ge(at_done, a + 2 * len(couples))
                gated(ST[gate], p, due, x_at + 2 * p, x_count + p + 1)

            rotate(MLA_ROPE, 0)
            attend(MLA_COUPLES, "evgate_a", 0, 0, XR["y2"])
            store("evmoba", w, 0, RS_LAYER)
            rotate(MOBA_ROPE, 1)
            attend(MOBA_COUPLES, "evgate_b", 8, 8, XR["y2"] + 4)

            def add_out(name, x_next, gain):
                st = ST[name]

                def pair(p, par):
                    hp = h[:, ds(p * 2, 2), :]
                    take(st, p, par, tb[:, :, :])
                    tt(hp, hp, tb[:, :, :], ADD).then_inc(h_ready, 1)
                    dve.wait_ge(h_ready, p + (HR[name] + 1))
                    if x_next:
                        split(hp, col(gain, 2, p * 2), xa, p * 2, p + (XR[x_next] + 1))

                pairs_loop(dve, 8, pair, steps=step, per=2 if x_next else 0)

            add_out("evout", "x3", "od_norm")
            if upto < 9:
                return
            for j in range(2):
                memory("mem3", j, j, "od_mem_norm")
            root("x3", RS_LAYER, D)
            st = ST["odin"]

            def odin_pair(p, par):
                dst = w[:, ds(p * 2, 2), :]
                take(st, p, par, dst)
                tt(dst, dst, along(rs[:, RS_LAYER, :], 2), MUL).then_inc(stored, 1)
                memory("mem3", p + 2, par, "od_mem_norm")

            pairs_loop(dve, 6, odin_pair, steps=step, per=2)
            store("odin", w, 0, RS_LAYER, 6)
            store("odmem", w, 32, RS_MEM)
            dve.wait_ge(rope_loaded, 32 * 2)
            rotate(SWA_ROPE, 0)
            rotate(DIL_ROPE, 1)
            attend(OD_COUPLES, "odgate", 20, 0, XR["y3"])
            add_out("odout", None, None)
            root("last", RS_LAYER, D)
            for k in range(4):
                hk = h[:, 4 * k:4 * k + 4, :]
                step(tt(hk, hk, along(rs[:, RS_LAYER, :], 4), MUL))
                tt(hk, hk, wide(col("final_norm_2", 4, 4 * k), 4), MUL).then_inc(h_ready, 1)


def _head(qk, v, o, mask, scale, gate=None, sink=None):
    return dict(qk=qk, v=v, o=o, mask=mask, scale=scale, gate=gate, sink=sink)


def _couples(heads):
    return [heads[i:i + 2] for i in range(0, len(heads), 2)]


MLA_ROPE, MLA_V = [8, 9, 10, 11, 28], list(range(20, 28))
MLA_COUPLES = _couples([
    _head([(i, 12 + i, 0, 128), (8 + i // 2, 28, 64 * (i % 2), 64)], (20 + i, 0, 128, 0), i, 1, 192.0 ** -0.5,
          gate=(i - 1, i) if i % 2 else None) for i in range(8)])
MOBA_ROPE, MOBA_V = list(range(16)), list(range(16, 24)) + list(range(39, 43))
MOBA_COUPLES = _couples([
    _head([(i, 8 + i, 0, 128)], (16 + i, 0, 128, 0), i, 1, 128.0 ** -0.5,
          gate=(i - 1, i) if i % 2 else None) for i in range(8)] + [
    _head([(24 + i, 35 + i, 0, 128)], (39 + i, 0, 128, 0), 24 + i, None, 128.0 ** -0.5,
          gate=(24 + i - 1, 24 + i) if i % 2 else None) for i in range(4)])
SWA_ROPE, DIL_ROPE = list(range(9)), list(range(10, 22))
OD_V = [9] + list(range(22, 28)) + list(range(36, 40))
OD_COUPLES = _couples([
    _head([(j, 8, 64 * g, 64)], (9, 64 * g, 64, 64 * g), j, 2, 64.0 ** -0.5, sink=j + 8 * g,
          gate=(j - 1, j) if j % 2 and g else None) for j in range(8) for g in range(2)] + [
    _head([(10 + i, 16 + i, 0, 128)], (22 + i, 0, 128, 0), 10 + i, 3, 128.0 ** -0.5,
          gate=(10 + i - 1, 10 + i) if i % 2 else None) for i in range(6)] + [
    _head([(28 + i, 32 + i, 0, 128)], (36 + i, 0, 128, 0), 28 + i, None, 128.0 ** -0.5,
          gate=(28 + i - 1, 28 + i) if i % 2 else None) for i in range(4)])


def constants():
    f = np.float32
    ident = np.eye(P, dtype=f)
    gsel = np.zeros((P, 2, P), f)
    for i in range(8):
        gsel[ROW_I + i, 0, i] = 1.0
        gsel[ROW_F + i, 1, i] = -1.0
    pos = np.arange(T)
    q, k = pos[:, None], pos[None, :]

    def rows(m):
        return m.reshape(2, P, T).transpose(1, 0, 2)

    causal = np.where(k <= q, 0.0, NEG)
    swa = np.where((q - k >= 0) & (q - k <= 127), 0.0, NEG)
    hits = ((q >= k) & (q - k <= 128)).astype(int)
    for dil in (4, 16):
        hits = hits + ((q >= k) & ((q - k) % dil == 0) & ((q - k) // dil <= 128))
    dil = np.where(hits > 0, np.log(np.maximum(hits, 1)), NEG)
    mlstm = np.where(q >= k, -NEG, 0.0) * (q != k)
    mlstm = np.where(k >= q, 0.0, -NEG)
    masks = np.stack([rows(mlstm), rows(causal), rows(swa), rows(dil)], 1).astype(f)
    s, t = np.arange(P)[:, None], np.arange(P)[None, :]
    lvl = np.zeros((P, 4, 2, P), f).reshape(P, 8, P)
    lvl[:, 0, :] = s == t
    for level in range(1, 8):
        size = 2 ** level
        lvl[:, level, :] = (s // size == t // size) & (s % size < size // 2) & (t % size >= size // 2)

    def rope(width, dim):
        inv = (f(1.0) / np.power(f(500000.0), np.arange(0, dim, 2, dtype=f) / f(dim))).astype(f)
        ang = (np.arange(T, dtype=f)[:, None] * inv[None, :]).astype(f)
        c, sn = np.cos(ang).astype(f).T, np.sin(ang).astype(f).T
        cos, sin, m = np.ones((P, T), f), np.zeros((P, T), f), np.zeros((P, P), f)
        for at in range(0, P, width):
            hf = dim // 2
            cos[at:at + hf] = c
            cos[at + hf:at + dim] = c
            sin[at:at + hf] = sn
            sin[at + hf:at + dim] = sn
            for i in range(hf):
                m[at + hf + i, at + i] = -1.0
                m[at + i, at + hf + i] = 1.0
        return np.stack([cos, sin], 1), m

    kinds = [rope(64, 64), rope(128, 32), rope(64, 16), rope(128, 32)]
    out = dict(ident=ident, gsel=gsel, masks=masks, lvl=lvl.reshape(P, 4, T))
    for name, a, b in (("ev", 0, 1), ("od", 2, 3)):
        out["rope_" + name] = np.stack([kinds[a][0], kinds[b][0]], 1)
        out["rot_" + name] = np.stack([kinds[a][1], kinds[b][1]], 1)
    return out


def channel_cols(v):
    v = np.asarray(v)
    return np.ascontiguousarray(v.reshape(-1, P).T)


def token_blocks(x):
    x = np.asarray(x)
    return np.ascontiguousarray(x.T.reshape(-1, P, T).transpose(1, 0, 2))


def weight_pairs(wt, st):
    wt = np.asarray(wt)
    cells = wt.reshape(st.blocks, P, st.pairs, st.nb, P)
    order = (2, 1, 3, 0, 4) if st.blocks == 2 else (2, 1, 0, 3, 4)
    return np.ascontiguousarray(cells.transpose(order)).reshape(st.pairs, P, -1)


def layout(i):
    ST = stages()
    i = {k: np.asarray(v) for k, v in i.items()}
    out = dict(constants())
    out["x"] = token_blocks(i["x"][0])
    out["p"] = np.stack([token_blocks(i["p"][l, 0]) for l in range(2)])
    out["mem"] = np.ascontiguousarray(token_blocks(i["mem_2"][0]).reshape(P, 8, 2, T).transpose(1, 0, 2, 3))
    for name in ("w_r", "w_i"):
        out[name] = np.ascontiguousarray(i["b_" + name][0].transpose(1, 0, 2)).reshape(P, 8 * P)
    gate_b = np.zeros((P, 1), np.float32)
    gate_b[ROW_I:ROW_I + 8, 0] = i["c_b_i"][0]
    gate_b[ROW_F:ROW_F + 8, 0] = i["c_b_f"][0]
    c = dict(
        e_norm=i["e_norm"][0], a_lb0=i["a_lb_logits"][0], a_lb1=i["a_lb_logits"][1], a_norm=i["a_norm"][0],
        b_conv_w=i["b_conv_w"][0], b_conv_b=i["b_conv_b"][0], b_b_r=i["b_b_r"][0], b_b_i=i["b_b_i"][0],
        b_lambda=i["b_lambda"][0], o_norm=i["o_norm"][0], c_conv_w=i["c_conv_w"][0], c_conv_b=i["c_conv_b"][0],
        c_norm=i["c_norm"][0], ple_norm0=i["ple_norm"][0], ple_norm1=i["ple_norm"][1], final_norm=i["final_norm"],
        ev_norm=i["ev_norm_g_2"][0], ev_q_norm=i["ev_q_norm_g_2"][0], ev_kv_norm=i["ev_kv_norm_g_2"][0],
        ev_mem_norm=i["ev_mem_norm_g_2"][0], od_norm=i["od_norm_g_2"][0], od_mem_norm=i["od_mem_norm_g_2"][0],
        final_norm_2=i["final_norm_g_2"])
    c = {k: channel_cols(v) for k, v in c.items()}
    c["c_gate_b"] = gate_b
    c["sinks"] = np.broadcast_to(i["od_sinks_2"][0], (P, 16))
    out["cols"] = np.ascontiguousarray(np.concatenate([c[n] for n, _ in COLS], 1))

    W = {}
    e = i["e_w_in"][0]
    W["ein"], W["ein_zb"] = e[:, :5120], e[:, 5120:]
    W["eout"], W["oout"] = i["e_w_out"][0], i["o_w_out"][0]
    for l in range(2):
        W[f"ple{l}"], W[f"gate{l}"] = i["ple_w"][l], i["ple_gate_w"][l]
    o = i["o_w_in"][0]
    W["oqk"], W["ov"], W["oog"], W["oz"] = (o[:, 2048 * j:2048 * j + 2048] for j in range(4))
    g = np.zeros((D, P), np.float32)
    g[:, ROW_I:ROW_I + 8] = o[:, 8192:8200]
    g[:, ROW_F:ROW_F + 8] = o[:, 8200:8208]
    W["ogate"] = g
    e = i["ev_w_in_2"][0]
    W["evc"] = e[:, 0:768]
    W["evkpe"] = np.concatenate([e[:, 768:832], e[:, 768:832]], 1)
    W["evmoba"] = e[:, 832:832 + 3584]
    W["evgate_a"], W["evgate_b"] = e[:, 4416:4416 + 1024], e[:, 5440:]
    W["evmem"], W["odmem"] = i["ev_w_mem_kv_2"][0], i["od_w_mem_kv_2"][0]
    uq = i["ev_w_uq_2"][0].reshape(512, 8, 192)
    W["uq"] = np.concatenate([uq[:, :, :128].reshape(512, 1024), uq[:, :, 128:].reshape(512, 512)], 1)
    ukv = i["ev_w_ukv_2"][0].reshape(256, 8, 2, 128)
    W["ukv"] = ukv.transpose(0, 2, 1, 3).reshape(256, 2048)
    W["evout"] = i["ev_w_out_2"][0]
    swa = np.arange(1024).reshape(2, 8, 64).transpose(1, 0, 2).reshape(-1)
    o = i["od_w_in_2"][0]
    W["odin"] = np.concatenate([o[:, swa], o[:, 1024:4096]], 1)
    W["odgate"] = np.concatenate([o[:, 4096 + swa], o[:, 5120:]], 1)
    W["odout"] = np.concatenate([i["od_w_out_2"][0][swa], i["od_w_out_2"][0][1024:]], 0)
    for name, st in ST.items():
        out["w_" + name] = weight_pairs(W[name], st)
    return out


def kernel(**inputs):
    import concourse.bacc as bacc
    from concourse import mybir
    from concourse.bass_utils import run_bass_kernel_spmd

    arrays = layout(inputs)
    nc = bacc.Bacc("TRN2", target_bir_lowering=False, num_devices=1)
    A = {n: nc.dram_tensor(n + "_dram", a.shape, mybir.dt.from_np(a.dtype), kind="ExternalInput").ap()
         for n, a in arrays.items()}
    out = nc.dram_tensor("out_dram", (P, KD, T), mybir.dt.float32, kind="ExternalOutput").ap()
    build(nc, A, out)
    r = run_bass_kernel_spmd(nc, [{n + "_dram": a for n, a in arrays.items()}], core_ids=[0])
    got = r.results[0]["out_dram"]
    return got.transpose(1, 0, 2).reshape(D, T).T.reshape(1, T, D)
```

```python
import numpy as np

T = 256
P = 128
D = 2048
KD = D // P
EPS = 1e-6
SLOTS = 4
CELLS_MAX = 4
NEG = -1.0e30


def stage_table():
    return [
        ("ein", "xa", 16, 12, 2),
        ("ein_zx", "xa", 16, 8, 2),
        ("ein_zb", "xa", 16, 4, 2),
        ("ple0", "xs", 2, 8, 2),
        ("eout", "xb", 16, 8, 2),
        ("gate0", "xa", 16, 8, 2),
        ("oqk", "xb", 16, 8, 2),
        ("ogate", "xb", 16, 1, 1),
        ("ov", "xb", 16, 8, 2),
        ("ogz", "xb", 16, 16, 2),
        ("ple1", "xs", 2, 8, 2),
        ("oout", "xa", 16, 8, 2),
        ("gate1", "xb", 16, 8, 2),
        ("evc", "xa", 16, 3, 2),
        ("evkpe", "xa", 16, 1, 1),
        ("evmem", "xb", 16, 4, 2),
        ("uq", "xs", 4, 6, 2),
        ("ukv", "xs", 2, 8, 2),
        ("evgate_a", "xa", 16, 4, 2),
        ("evmoba", "xa", 16, 14, 2),
        ("evgate_b", "xa", 16, 6, 2),
        ("evout", "xb", 20, 8, 2),
        ("odin", "xa", 16, 16, 2),
        ("odmem", "xb", 16, 4, 2),
        ("odgate", "xa", 16, 9, 2),
        ("odout", "xb", 18, 8, 2),
    ]


def unit_cells(blocks, nb):
    n = 2 if blocks < 16 else 8 if blocks == 16 else 10
    small, more = divmod(blocks, n)
    out, k = [], 0
    for q in range(n):
        m = small + (q < more)
        out.append([(kk, b) for kk in range(k, k + m) for b in range(nb)])
        k += m
    return out


class Stage:

    def __init__(self, row, unit0, pair0):
        self.name, self.x, self.blocks, self.pairs, self.nb = row
        self.units = unit_cells(self.blocks, self.nb)
        self.upp = len(self.units)
        self.unit0, self.pair0 = unit0, pair0

def stages():
    out, unit0, pair0 = {}, 0, 0
    for row in stage_table():
        s = Stage(row, unit0, pair0)
        out[s.name] = s
        unit0 += s.pairs * s.upp
        pair0 += s.pairs
    return out


COLS = [
    ("e_norm", 16), ("a_lb0", 8), ("a_lb1", 8), ("a_norm", 8), ("b_conv_w", 32), ("b_conv_b", 8),
    ("b_b_r", 8), ("b_b_i", 8), ("b_lambda", 8), ("o_norm", 16), ("c_conv_w", 64), ("c_conv_b", 16),
    ("c_gate_b", 1), ("c_norm", 16), ("ple_norm0", 16), ("ple_norm1", 16), ("final_norm", 16),
    ("ev_norm", 16), ("ev_q_norm", 4), ("ev_kv_norm", 2), ("ev_mem_norm", 16), ("od_norm", 16),
    ("sinks", 16), ("od_mem_norm", 16), ("final_norm_2", 16),
]
COL_AT, _n = {}, 0
for _name, _w in COLS:
    COL_AT[_name] = _n
    _n += _w
NCOLS = _n
ROW_I, ROW_F = 0, 32


def build(nc, A, out, upto=99):
    import concourse.bass as bass
    from concourse import mybir
    from contextlib import ExitStack

    F32, F32R, U8 = mybir.dt.float32, mybir.dt.float32r, mybir.dt.uint8
    ALU, ACT = mybir.AluOpType, mybir.ActivationFunctionType
    AX = mybir.AxisListType.X
    ADD, SUB, MUL, MAX = ALU.add, ALU.subtract, ALU.mult, ALU.max
    ds = bass.ds
    ST = stages()

    ctx = ExitStack()
    with ctx:
        def sb(name, shape, dt=F32):
            return ctx.enter_context(nc.sbuf_tensor(name, shape, dt))

        def sem(name):
            return ctx.enter_context(nc.semaphore(name))

        with nc.sbuf_tensor("oa", [P, 32, T], F32) as oa:
            pass
        xa = sb("xa", [P, 16, 2 * T], F32R)
        with nc.sbuf_tensor("ob", [P, 40, T], F32) as ob:
            pass
        xb = sb("xb", [P, 20, 2 * T], F32R)
        xs = sb("xs", [P, 6, 2 * T], F32R)
        h = sb("h", [P, KD, T])
        w = sb("w", [P, 44, T])
        raw = sb("raw", [P, SLOTS, CELLS_MAX * P])
        w_hi = sb("w_hi", [P, SLOTS, CELLS_MAX * P], F32R)
        w_lo = sb("w_lo", [P, SLOTS, CELLS_MAX * P], F32R)
        cross = sb("cross", [P, 2, 2, T])
        tb = sb("tb", [P, 2, T])
        sq = sb("sq", [P, 2, 2, T])
        sq_sum, sq_next = sq[:, 0, :, :], sq[:, 1, :, :]
        rs = sb("rs", [P, 4, T])
        RS_LAYER, RS_PLE, RS_Q, RS_MEM = range(4)
        RS_KV = RS_PLE
        sm = sb("sm", [P, 2, 2, T])
        pt = sb("pt", [P, 2, 2, T])
        small = sb("small", [P, 64])
        cols = sb("cols", [P, NCOLS])
        ident = sb("ident", [P, P])
        ones = sb("ones", [P, P])
        gsel = sb("gsel", [P, 2, P])
        masks = sb("masks", [P, 4, 2, T])
        rope = sb("rope", [P, 2, 2, T])
        rot = sb("rot", [P, 2, P])
        lvl = sb("lvl", [P, 8, P], U8)
        ps = ctx.enter_context(nc.psum_tensor("ps", [P, 8, 512], F32))
        X = {"xa": xa, "xb": xb, "xs": xs}
        M_LSTM, M_CAUSAL, M_SWA, M_DIL = range(4)

        def col(name, n=None, at=0):
            c = COL_AT[name]
            return cols[:, c:c + dict(COLS)[name]] if n is None else cols[:, ds(c + at, n)]

        def wide(ap, n):
            return ap.unsqueeze(2).to_broadcast([P, n, T])

        def along(ap, n):
            return ap.unsqueeze(1).to_broadcast([P, n, T])

        x_loaded = [sem(f"x_loaded{i}") for i in range(4)]
        cols_loaded, consts_loaded = sem("cols_loaded"), sem("consts_loaded")
        unit_loaded = [sem(f"unit_loaded{i}") for i in range(SLOTS)]
        act_rounded, lo_ready, unit_used = sem("act_rounded"), sem("lo_ready"), sem("unit_used")
        cross_ready, pair_out, stored = sem("cross_ready"), sem("pair_out"), sem("stored")
        x_ready = sem("x_ready")
        sq_ready, sq_added, sums_ready = sem("sq_ready"), sem("sq_added"), sem("sums_ready")
        var_ready, std_ready = sem("var_ready"), sem("std_ready")
        dve_step, act_step = sem("dve_step"), sem("act_step")
        ones_set = sem("ones_set")
        stream_loaded = [sem("stream_loaded0"), sem("stream_loaded1")]
        out_stored = sem("out_stored")
        h_ready = sem("h_ready")
        par_in, par_exp, par_done = sem("par_in"), sem("par_exp"), sem("par_done")
        hg_sig, hg_q, hg_logf, hg_qk = sem("hg_sig"), sem("hg_q"), sem("hg_logf"), sem("hg_qk")
        hg_diff, hg_exp, hg_lv_in, hg_lv_out, hg_masked = (
            sem("hg_diff"), sem("hg_exp"), sem("hg_lv_in"), sem("hg_lv_out"), sem("hg_masked"))
        v_turned, v_copied = sem("v_turned"), sem("v_copied")
        hg_o, hg_ocopied = sem("hg_o"), sem("hg_ocopied")
        hn_sums, hn_var, hn_std, hn_gate = sem("hn_sums"), sem("hn_var"), sem("hn_std"), sem("hn_gate")
        lr_conv, lr_w, lr_pre, lr_act, lr_th, lr_fix, lr_root = (
            sem("lr_conv"), sem("lr_w"), sem("lr_pre"), sem("lr_act"), sem("lr_th"), sem("lr_fix"), sem("lr_root"))
        y_gate, y_done = sem("y_gate"), sem("y_done")
        g_sig, g_pre = sem("g_sig"), sem("g_pre")
        cv_pre, cv_sig, cv_done = sem("cv_pre"), sem("cv_sig"), sem("cv_done")
        mg_in, mg_exp, mg_lf, mg_g, mg_gcols, mg_max = (
            sem("mg_in"), sem("mg_exp"), sem("mg_lf"), sem("mg_g"), sem("mg_gcols"), sem("mg_max"))
        ml_s, ml_mask, ml_e, ml_p, ml_o, ml_den, ml_h, ml_sums, ml_var, ml_std = (
            sem("ml_s"), sem("ml_mask"), sem("ml_e"), sem("ml_p"), sem("ml_o"), sem("ml_den"), sem("ml_h"),
            sem("ml_sums"), sem("ml_var"), sem("ml_std"))
        ml_sq = sem("ml_sq")
        rp_sums, rp_taken, rope_loaded = sem("rp_sums"), sem("rp_taken"), sem("rope_loaded")
        at_s, at_neg, at_e, at_p, at_turned, at_pt, at_o, at_done = (
            sem("at_s"), sem("at_neg"), sem("at_e"), sem("at_p"), sem("at_turned"), sem("at_pt"), sem("at_o"),
            sem("at_done"))

        XR, n = {}, 0
        for name, pairs in (("x", 8), ("p0", 1), ("y0", 8), ("h0", 8), ("h1", 8), ("p1", 1), ("y1", 8),
                            ("h2", 8), ("x2", 8), ("mem2", 8), ("cq", 2), ("ckv", 1), ("y2", 10),
                            ("x3", 8), ("mem3", 8), ("y3", 9)):
            XR[name] = n
            n += pairs
        NORMS, n, m = {}, 0, 0
        for name, squares, additions in (("x", 8, 1), ("mem", 8, 7), ("ple0", 2, 1), ("h1", 8, 7), ("ple1", 2, 1),
                                         ("first", 16, 14), ("cq", 2, 1), ("ckv", 1, 0), ("x3", 8, 7), ("last", 8, 7)):
            NORMS[name] = (n, m, n + squares, m + additions)
            n, m = n + squares, m + additions
        NORMS["x2"] = NORMS["first"]
        STORED, n = {}, 0
        for name in ("ein", "ein_zx", "ein_zb", "oqk", "ogate", "ov", "ogz", "evc", "evkpe", "evmem", "uq", "ukv",
                     "evmoba", "odin", "odmem"):
            STORED[name] = n
            n += ST[name].pairs
        ZX_AT, ZX_END, n = {}, {}, 2 * ST["ein_zx"].upp
        for slot in range(18):
            units = [2, 3, 3, 3, 3, 3, 3, 2, 2][slot % 9]
            ZX_AT[slot] = [divmod(n + k, ST["ein_zx"].upp) for k in range(units)]
            for p, q in ZX_AT[slot]:
                if q == ST["ein_zx"].upp - 1:
                    ZX_END[slot] = p
            n += units
        HR = {"gate0": 0, "gate1": 8, "evout": 16, "odout": 24, "last": 32}
        ROOTS = {"x": 0, "mem": 1, "ple0": 2, "h1": 3, "ple1": 4, "first": 5, "x2": 6, "cq": 7, "ckv": 8, "x3": 9,
                 "last": 10}
        STREAM = {"mem": 0, "p0": 8, "p1": 9, "mem2": 10, "mem3": 18}

        class Steps:

            def __init__(self, eng, s):
                self.eng, self.s, self.n = eng, s, 0

            def post(self, ins):
                self.n = self.n + 1
                ins.then_inc(self.s, 1)

            def wait(self):
                self.eng.wait_ge(self.s, self.n)

            def __call__(self, ins):
                self.post(ins)
                self.wait()

        def pairs_loop(eng, count, body, first=0, steps=None, per=0):
            trips = (count - first) // 2
            if trips >= 2:
                n0 = steps.n if steps else 0
                with eng.Fori(0, trips) as i:
                    for k in range(2):
                        if steps:
                            steps.n = n0 + i * (2 * per) + k * per
                        body(i * 2 + (first + k), (first + k) % 2)
                if steps:
                    steps.n = n0 + trips * 2 * per
                first += 2 * trips
            for p in range(first, count):
                body(p, p % 2)

        def banks(st, par, nb=None):
            at = 2 * ((st.pair0 + par) % 2)
            return slice(at, at + (nb or st.nb))

        def square_sums(name):
            if name == "x" or name[:3] == "ple":
                return w[:, 0:2, :], 0
            return {"x2": (w[:, 40:42, :], 1), "ckv": (sq_next, 1)}.get(name, (sq_sum, 0))

        def unit_of(st, p, par, q):
            turn, slot = divmod(par * st.upp + q, SLOTS)
            loads = (p - par) * (st.upp * 16 // SLOTS) + (st.unit0 // SLOTS + turn + 1) * 16
            return slot, len(st.units[q]) * P, st.unit0 + p * st.upp + q, loads

        block = ctx.enter_context(nc.Block())

        @block.sync
        def _(sp):
            def load(st):
                wd = A["w_" + st.name]

                def pair(p, par):
                    at = 0
                    for q in range(st.upp):
                        slot, n, unit, _ = unit_of(st, p, par, q)
                        if not (isinstance(p, int) and unit < SLOTS):
                            sp.wait_ge(lo_ready, unit - SLOTS + 1)
                        src = wd[p] if isinstance(p, int) else wd[ds(p, 1)].rearrange("o p c -> (o p) c")
                        sp.dma_start(raw[:, slot, 0:n], src[:, at:at + n]).then_inc(unit_loaded[slot], 16)
                        at += n

                if st.unit0 == 0:
                    pair(0, 0)
                pairs_loop(sp, st.pairs, pair, first=int(st.unit0 == 0))

            for name in [r[0] for r in stage_table()]:
                load(ST[name])
            for k in range(4):
                sp.wait_ge(h_ready, HR["last"] + k + 1)
                sp.dma_start(out[:, 4 * k:4 * k + 4, :], h[:, 4 * k:4 * k + 4, :]).then_inc(out_stored, 16)
            sp.wait_ge(out_stored, 64)

        @block.gpsimd
        def _(pool):
            def split(st):
                def pair(p, par):
                    for q in range(st.upp):
                        slot, n, unit, _ = unit_of(st, p, par, q)
                        pool.wait_ge(act_rounded, unit + 1)
                        nc.gpsimd.tensor_tensor(w_lo[:, slot, 0:n], raw[:, slot, 0:n],
                                                w_hi[:, slot, 0:n].bitcast(F32), SUB).then_inc(lo_ready, 1)

                pairs_loop(pool, st.pairs, pair)

            for name in [r[0] for r in stage_table()]:
                split(ST[name])

        @block.tensor
        def _(pe):
            mm = nc.tensor.matmul

            def product(st, p, par, new=None, units=None):
                x, x0 = X[st.x], 4 if st.name == "ukv" else 0
                pair = st.pair0 + p
                units = range(st.upp) if units is None else units
                if units[0] == 0 and not (isinstance(p, int) and pair < 2):
                    pe.wait_ge(pair_out, pair - 1)
                bank = banks(st, par).start
                for q in units:
                    cells, slot = st.units[q], (par * st.upp + q) % SLOTS
                    if new:
                        pe.wait_ge(x_ready, XR[new] + cells[-1][0] // 2 + 1)
                    pe.wait_ge(lo_ready, st.unit0 + p * st.upp + q + 1)
                    for c, (k, b) in enumerate(cells):
                        at = slice(c * P, c * P + P)
                        mm(ps[:, bank + b, :], w_hi[:, slot, at], x[:, x0 + k, :], start=(k == 0), stop=False)
                        ins = mm(ps[:, bank + b, 0:T], w_lo[:, slot, at], x[:, x0 + k, 0:T],
                                 start=False, stop=(k == st.blocks - 1))
                    ins.then_inc(unit_used, 1)

            def products(name, first=0, count=None, new=None, behind=None, peel=1):
                st = ST[name]
                count = st.pairs if count is None else count

                def pair(p, par):
                    product(st, p, par, new if isinstance(p, int) and p == 0 else None)
                    if behind:
                        behind(p, par)

                for p in range(first, first + peel):
                    pair(p, p % 2)
                pairs_loop(pe, count, pair, first + peel)

            def sums(name):
                acc, half = square_sums(name)
                _, _, squares, additions = NORMS[name]
                if ROOTS[name] and not half:
                    pe.wait_ge(var_ready, ROOTS[name])
                pe.wait_ge(sq_ready, squares)
                pe.wait_ge(sq_added, additions)
                for b in range(2):
                    ins = mm(ps[:, 7, half * T:half * T + T], ones[:, :], acc[:, b, :], start=(b == 0), stop=(b == 1))
                ins.then_inc(sums_ready, 1)

            turned = [0]

            def turn_values(name_blocks, buf, after_stored):
                pe.wait_ge(stored, after_stored)
                for k in range(0, len(name_blocks), 2):
                    n = turned[0]
                    if n >= 2:
                        pe.wait_ge(v_copied, n - 1)
                    for j, bl in enumerate(name_blocks[k:k + 2]):
                        for tt in range(2):
                            ins = nc.tensor.transpose(ps[:, 4 + n % 2, (2 * j + tt) * P:(2 * j + tt + 1) * P],
                                                      buf[:, bl, tt * P:(tt + 1) * P], ident[:, :])
                    ins.then_inc(v_turned, 1)
                    turned[0] += 1

            pe.wait_ge(ones_set, 1)
            products("ein", 0, 1, new="x")
            sums("x")
            products("ein", 1, 11)
            sums("mem")
            products("ein", 11)
            pe.wait_ge(consts_loaded, 16 * 6)

            zx, zb = ST["ein_zx"], ST["ein_zb"]
            product(zx, 0, 0)
            product(zx, 1, 1)
            turn_values(range(16, 24), w, STORED["ein"] + 12)
            pe.wait_ge(v_copied, 4)
            for g in range(2):
                for level in range(9):
                    n = 9 * g + level
                    if level == 0:
                        pe.wait_ge(hg_q, 1)
                        pe.wait_ge(hg_qk, 1)
                        q_, k_ = w[:, 4 * g:4 * g + 4, :], ob[:, 8 + 4 * g:12 + 4 * g, :]
                    else:
                        pe.wait_ge(hg_lv_in, 8 * g + level)
                        q_, k_ = ob[:, 20:24, :], ob[:, 24:28, :]
                    if n:
                        pe.wait_ge(hg_masked, n)
                    for hd in range(4):
                        if level < 8:
                            for tt in range(2):
                                c = hd * T + tt * P
                                ins = mm(ps[:, 4 + c // 512, c % 512:c % 512 + P], k_[:, hd, tt * P:(tt + 1) * P],
                                         q_[:, hd, tt * P:(tt + 1) * P], start=True, stop=True)
                        else:
                            ins = mm(ps[:, 4, hd * P:(hd + 1) * P], k_[:, hd, 0:P], q_[:, hd, P:T],
                                     start=True, stop=True)
                    ins.then_inc(hg_lv_out, 1)
                    for p, q in ZX_AT[n]:
                        product(zx, p, p % 2, units=(q,))
                pe.wait_ge(hg_masked, 9 * g + 9)
                a = ob[:, 28:34, :].rearrange("p a b -> p (a b)")
                if g:
                    pe.wait_ge(hg_ocopied, 2)
                for hd in range(4):
                    v = w[:, 16 + 4 * g + hd, :]
                    o = ps[:, 6 + hd // 2, (hd % 2) * T:(hd % 2 + 1) * T]
                    mm(o[:, 0:P], v[:, 0:P], a[:, hd * T:hd * T + P], start=True, stop=True)
                    mm(o[:, P:T], v[:, 0:P], a[:, 1024 + hd * P:1024 + hd * P + P], start=True, stop=False)
                    ins = mm(o[:, P:T], v[:, P:T], a[:, hd * T + P:hd * T + T], start=False, stop=True)
                ins.then_inc(hg_o, 1)
            product(zb, 0, 0, units=range(4))
            for hd in range(8):
                if hd % 2 == 0:
                    pe.wait_ge(hg_ocopied, 4)
                    pe.wait_ge(hn_gate, hd // 2 + 1)
                ins = mm(ps[:, 4 + hd // 2, (hd % 2) * T:(hd % 2 + 1) * T], ones[:, :], ob[:, 16 + hd, :],
                         start=True, stop=True)
            ins.then_inc(hn_sums, 1)
            if upto < 2:
                return
            product(zb, 0, 0, units=range(4, 8))
            pe.wait_ge(lr_w, 32)
            pe.wait_ge(hn_var, 1)
            for n in range(8):
                pe.wait_ge(lr_conv, n + 1)
                if n >= 2:
                    pe.wait_ge(lr_act, 2 * n - 2)
                for j in range(2):
                    wt = (sm, pt)[j][:, :, :, :].rearrange("p a b c -> p (a b c)")
                    ins = mm(ps[:, 4 + n % 2, j * T:(j + 1) * T], wt[:, n * P:(n + 1) * P], ob[:, 8 + n, :],
                             start=True, stop=True)
                ins.then_inc(lr_pre, 1)
                product(zb, 1, 1, units=range(n, n + 1))
            product(zb, 2, 0)
            product(zb, 3, 1)
            if upto < 3:
                return

            def tail(l):
                products(f"ple{l}", new=f"p{l}")
                products("eout" if l == 0 else "oout", 0, 2, new=f"y{l}", peel=2)
                sums(f"ple{l}")
                products("eout" if l == 0 else "oout", 2, peel=0)
                products(f"gate{l}", new=f"h{2 * l}")

            tail(0)
            if upto < 4:
                return
            products("oqk", 0, 1, new="h1")
            sums("h1")
            products("oqk", 1)
            products("ogate")
            products("ov", 0, 2, peel=2)
            pe.wait_ge(mg_lf, 1)
            gx, gb, gm = w[:, 32, :], w[:, 33, :], w[:, 34, :]
            mm(ps[:, 6, 0:T], gsel[:, 0, :], gx, start=True, stop=False)
            mm(ps[:, 6, 0:T], gsel[:, 1, :], gb, start=False, stop=True).then_inc(mg_g, 1)
            pe.wait_ge(var_ready, ROOTS["h1"] + 1)
            for st_ in range(2):
                c = slice(8 * st_, 8 * st_ + 8)
                mm(ps[:, 7, c], gx[:, st_ * P:(st_ + 1) * P], gsel[:, 0, 0:8], start=True, stop=False)
                ins = mm(ps[:, 7, c], gb[:, st_ * P:(st_ + 1) * P], gsel[:, 1, 0:8], start=False, stop=True)
            ins.then_inc(mg_g, 1)
            products("ov", 2, peel=0)
            if upto < 5:
                return
            ogz = ST["ogz"]
            for p in range(4):
                product(ogz, p, p % 2)
                if p in (1, 2):
                    turn_values(range(8 * p + 8, 8 * p + 16), w, STORED["ov"] + 8)

            def gates_chunk(c):
                product(ogz, 4 + c // 2, (c // 2) % 2, units=range(4 * (c % 2), 4 * (c % 2) + 4))

            pe.wait_ge(v_copied, 12)
            pe.wait_ge(cv_done, 8)
            pe.wait_ge(mg_max, 1)
            pe.wait_ge(mg_gcols, 1)

            def ml_scores(hd):
                if hd:
                    pe.wait_ge(ml_p, hd)
                    pe.wait_ge(ml_den, hd)
                for kt in range(2):
                    mm(ps[:, 4, kt * T:(kt + 1) * T], w[:, 8 + hd, kt * P:(kt + 1) * P], w[:, hd, :],
                       start=True, stop=True)
                one_m = ident[:, hd:hd + 1].to_broadcast([P, P])
                one_b = ident[:, ROW_F + hd:ROW_F + hd + 1].to_broadcast([P, P])
                mm(ps[:, 5, 0:T], one_m, gm, start=True, stop=True)
                mm(ps[:, 5, T:2 * T], one_m, gm, start=True, stop=False)
                mm(ps[:, 5, T:2 * T], one_b, gb, start=False, stop=True).then_inc(ml_s, 1)

            for hd in range(8):
                ml_scores(hd)
                gates_chunk(3 * hd)
                pe.wait_ge(ml_p, hd + 1)
                if hd:
                    pe.wait_ge(ml_h, hd)
                for eb in range(2):
                    for kt in range(2):
                        mm(ps[:, 6, eb * T:(eb + 1) * T], w[:, 16 + 2 * hd + eb, kt * P:(kt + 1) * P],
                           pt[:, 0, kt, :], start=(kt == 0), stop=(kt == 1))
                if hd:
                    pe.wait_ge(ml_var, hd)
                for kt in range(2):
                    ins = mm(ps[:, 7, 0:T], ones[:, :], pt[:, 0, kt, :], start=(kt == 0), stop=(kt == 1))
                ins.then_inc(ml_o, 1)
                gates_chunk(3 * hd + 1)
                pe.wait_ge(ml_sq, hd + 1)
                for eb in range(2):
                    ins = mm(ps[:, 7, T:2 * T], ones[:, :], pt[:, 1, eb, :], start=(eb == 0), stop=(eb == 1))
                ins.then_inc(ml_sums, 1)
                gates_chunk(3 * hd + 2)
            if upto < 6:
                return
            tail(1)
            if upto < 7:
                return
            products("evc", 0, 1, new="x2")
            sums("first")
            sums("x2")
            products("evc", 1, 3, peel=2)
            products("evkpe")
            products("evmem", 0, 3, new="mem2", peel=3)
            sums("cq")
            sums("ckv")
            products("evmem", 3, 4)
            products("uq", new="cq")

            def rotate(n, par, kind, at, nb, after):
                pe.wait_ge(stored, after)
                if not (isinstance(n, int) and n < 2):
                    pe.wait_ge(rp_taken, n - 1)
                for b in range(nb):
                    ins = mm(ps[:, 6 + par, b * T:(b + 1) * T], rot[:, kind, :],
                             w[:, ds(at + b, 1), :].rearrange("p o t -> p (o t)"), start=True, stop=True)
                ins.then_inc(rp_sums, 1)

            def mla_behind(p, par):
                if p == 0:
                    pe.wait_ge(var_ready, ROOTS["ckv"] + 1)
                if p < 3:
                    rotate(p, p % 2, 0, *MLA_ROPE[p], STORED["uq"] + 6)
                if p == 6:
                    turn_values(MLA_V, w, STORED["ukv"] + 4)

            products("ukv", 0, 7, new="ckv", behind=mla_behind, peel=7)
            products("ukv", 7, 8)
            if upto < 8:
                return

            def scores(heads, memory_ready):
                for i, hd in enumerate(heads):
                    if hd["mask"] is None:
                        pe.wait_ge(stored, memory_ready)
                    for qt in range(2):
                        qs = slice(qt * P, (qt + 1) * P)
                        parts = hd["qk"]
                        for j, (qb_, kb_, p0, pn) in enumerate(parts):
                            ins = mm(ps[:, 4 + i, qt * T:(qt + 1) * T], w[p0:p0 + pn, qb_, qs], w[p0:p0 + pn, kb_, :],
                                     start=(j == 0), stop=(j == len(parts) - 1))
                    ins.then_inc(at_s, 1)

            def turn_probs(heads, a):
                for i in range(len(heads)):
                    pe.wait_ge(at_p, a + i + 1)
                    if a + i >= 2:
                        pe.wait_ge(at_done, a + i - 1)
                    for qt in range(2):
                        for kt in range(2):
                            ins = nc.tensor.transpose(ps[:, 6 + i, kt * T + qt * P:kt * T + (qt + 1) * P],
                                                      sm[:, i, qt, kt * P:(kt + 1) * P], ident[:, :])
                    ins.then_inc(at_turned, 1)

            def outputs(heads, a):
                for i, hd in enumerate(heads):
                    pe.wait_ge(at_pt, a + i + 1)
                    vb, v0, vn, p0 = hd["v"]
                    for kt in range(2):
                        ins = mm(ps[p0:p0 + vn, 6 + i, 0:T], w[:, vb, kt * P + v0:kt * P + v0 + vn], pt[:, i, kt, :],
                                 start=(kt == 0), stop=(kt == 1))
                    ins.then_inc(at_o, 1)

            def attend(couples, gate, a, memory_ready=None):
                def chunk(c):
                    p, first, last = gate_chunk(couples, c)
                    product(ST[gate], p, p % 2, units=range(first, last))

                scores(couples[0], memory_ready)
                chunk(0)
                for c, heads in enumerate(couples):
                    turn_probs(heads, a + 2 * c)
                    if c + 1 < len(couples):
                        scores(couples[c + 1], memory_ready)
                    outputs(heads, a + 2 * c)
                    if c + 1 < len(couples):
                        chunk(c + 1)

            def moba_behind(p, par):
                rotate(p + (MOBA_ROT - 1), (MOBA_ROT + 1 + par) % 2, 1, p * 2 - 2, 2, p + STORED["evmoba"])

            pe.wait_ge(rp_taken, MOBA_ROT)
            pe.wait_ge(v_copied, turned[0])
            pe.wait_ge(stored, STORED["ukv"] + 8)
            attend(MLA_COUPLES, "evgate_a", 0)
            products("evmoba", 0, 1)
            pe.wait_ge(at_done, 8)
            products("evmoba", 1, 9, behind=moba_behind, peel=0)
            products("evmoba", 9, 13, peel=0)
            turn_values(MOBA_V, w, STORED["evmoba"] + 12)
            products("evmoba", 13)
            pe.wait_ge(rp_taken, OD_ROT)
            pe.wait_ge(v_copied, turned[0])
            attend(MOBA_COUPLES, "evgate_b", 8, STORED["evmoba"] + 14)
            products("evout", new="y2")
            if upto < 9:
                return
            products("odin", 0, 1, new="x3")
            sums("x3")
            pe.wait_ge(rope_loaded, 32 * 2)
            pe.wait_ge(var_ready, ROOTS["x3"] + 1)
            pe.wait_ge(at_done, 20)

            def od_behind(kind, nb):
                return lambda p, par: rotate(p + (OD_ROT - 1), (OD_ROT + 1 + par) % 2, kind, p * 2 - 2, nb,
                                             p + STORED["odin"])

            products("odin", 1, 5, behind=od_behind(0, 2), peel=0)
            products("odin", 5, 6, behind=od_behind(0, 1))
            products("odin", 6, 12, behind=od_behind(1, 2), peel=0)
            products("odin", 12, peel=0)
            products("odmem", 0, 3, new="mem3", peel=3)
            turn_values(OD_V, w, STORED["odmem"] + 2)
            products("odmem", 3)
            pe.wait_ge(rp_taken, OD_ROT + 11)
            pe.wait_ge(v_copied, turned[0])
            attend(OD_COUPLES, "odgate", 20, STORED["odmem"] + 4)
            products("odout", new="y3")
            sums("last")

        @block.scalar
        def _(act):
            step = Steps(act, act_step)
            af = nc.scalar.activation

            def start_of(p, q, at):
                return isinstance(p, int) and p == 0 and q == at

            act.dma_start(cols[:], A["cols"]).then_inc(cols_loaded, 16)
            for k in range(4):
                act.dma_start(h[:, 4 * k:4 * k + 4, :], A["x"][:, 4 * k:4 * k + 4, :]).then_inc(x_loaded[k], 16)

            def stream(name, j, par):
                n = STREAM[name] + par
                src = A["p"][int(name[1])] if name[0] == "p" else A["mem"][j] if isinstance(j, int) else (
                    A["mem"][ds(j, 1)].rearrange("o p a b -> (o p) a b"))
                act.dma_start(sm[:, n % 2, :, :], src).then_inc(stream_loaded[n % 2], 16)

            def rounded(st, p, q, par=None):
                slot, n, unit, loads = unit_of(st, p, p % 2 if par is None else par, q)
                act.wait_ge(unit_loaded[slot], loads)
                if not (isinstance(p, int) and unit < SLOTS):
                    act.wait_ge(unit_used, unit - SLOTS + 1)
                af(w_hi[:, slot, 0:n], raw[:, slot, 0:n], ACT.Copy).then_inc(act_rounded, 1)

            def crossed(st, p, par):
                pair = st.pair0 + p
                act.wait_ge(unit_used, st.unit0 + p * st.upp + st.upp)
                if not (isinstance(p, int) and pair < 2):
                    act.wait_ge(pair_out, pair - 1)
                af(cross[:, (st.pair0 + par) % 2, 0:st.nb, :], ps[:, banks(st, par), T:2 * T],
                   ACT.Copy).then_inc(cross_ready, 1)

            def last_crossed(name):
                st = ST[name]
                crossed(st, st.pairs - 1, (st.pairs - 1) % 2)

            def stage(name, before=None, first=0, count=None, peel=1, behind=None, done=0):
                st = ST[name]
                count = st.pairs if count is None else count

                def pair(p, par):
                    start = isinstance(p, int) and p == 0
                    for q in range(st.upp):
                        if not (isinstance(p, int) and p * st.upp + q < done):
                            rounded(st, p, q, par)
                        if q == (1 if st.upp < 8 else 2):
                            if not start:
                                crossed(st, p - 1, 1 - par)
                            elif before:
                                last_crossed(before)
                        if behind:
                            behind(p, par, q)

                for p in range(first, first + peel):
                    pair(p, p % 2)
                pairs_loop(act, count, pair, first + peel)

            def square(name, j, src, gain=None):
                added = NORMS[name][1]
                static = isinstance(j, int)
                if name == "ckv":
                    dst = sq_next
                    act.wait_ge(sq_added, added)
                elif static and j == 0:
                    dst = square_sums(name)[0]
                    if name != "x2":
                        act.wait_ge(var_ready, ROOTS[name])
                else:
                    dst = w[:, 42:44, :] if name == "x2" else sq_next
                    if name not in ("first", "x2"):
                        before = j + (added - 1)
                    else:
                        before = added if static and j == 1 else j * 2 + (added - (2 if name == "x2" else 3))
                    act.wait_ge(sq_added, before)
                if gain is None:
                    af(dst, src, ACT.Square).then_inc(sq_ready, 1)
                else:
                    for b in range(2):
                        ins = af(dst[:, b, :], src[:, b, :], ACT.Square, scale=gain[:, b:b + 1])
                        if b == 0:
                            step.post(ins)
                    ins.then_inc(sq_ready, 1)

            def square_h(name, update, j):
                act.wait_ge(h_ready, j + (HR[update] + 1))
                hp = h[:, 2 * j:2 * j + 2, :] if isinstance(j, int) else h[:, ds(j * 2, 2), :]
                square(name, j, hp)
                if name == "first":
                    square("x2", j, hp, cols[:, ds(j * 2 + COL_AT["final_norm"], 2)])

            def root(name, which):
                act.wait_ge(var_ready, ROOTS[name] + 1)
                af(rs[:, which, :], tb[:, 0, :], ACT.Sqrt).then_inc(std_ready, 1)

            copied = [0]

            def copy_values(blocks, buf):
                for k in range(0, len(blocks), 2):
                    n = copied[0]
                    act.wait_ge(v_turned, n + 1)
                    nb = len(blocks[k:k + 2])
                    if nb == 2 and blocks[k + 1] != blocks[k] + 1:
                        for j in range(2):
                            ins = af(buf[:, blocks[k + j], :], ps[:, 4 + n % 2, j * T:(j + 1) * T], ACT.Copy)
                            if j == 0:
                                step.post(ins)
                    else:
                        ins = af(buf[:, blocks[k]:blocks[k] + nb, :].rearrange("p a b -> p (a b)"),
                                 ps[:, 4 + n % 2, 0:nb * T], ACT.Copy)
                    ins.then_inc(v_copied, 1)
                    copied[0] += 1

            def x_norm(p, par, q):
                if p == 0:
                    act.wait_ge(x_loaded[q // 2], 16)
                    af(w[:, 2 * q:2 * q + 2, :], h[:, 2 * q:2 * q + 2, :], ACT.Square).then_inc(sq_ready, 1)
                if p == 1 and q == 0:
                    for j in range(2):
                        stream("mem", j, j)
                    for buf, name in ((ident, "ident"), (gsel, "gsel"), (masks, "masks"), (ob[:, 36:40, :], "lvl"),
                                      (rope, "rope_ev"), (rot, "rot_ev")):
                        act.dma_start(buf if name == "lvl" else buf[:], A[name]).then_inc(consts_loaded, 16)
                if p == 1 and q == 4:
                    root("x", RS_LAYER)
                if p == 1 and q == 6:
                    act.wait_ge(par_in, 1)
                    af(small[:, 0:24], small[:, 0:24], ACT.Exp).then_inc(par_exp, 1)

            def mem_norm(p, par, q):
                if q == 5:
                    j = p - 2
                    act.wait_ge(stream_loaded[par], p * 8 - 8 * par)
                    square("mem", j, sm[:, par, :, :])
                    act.wait_ge(sq_ready, j + (NORMS["mem"][0] + 1))
                    if not (isinstance(p, int) and j >= 6):
                        stream("mem", j + 2, par)

            stage("ein", first=0, count=2, peel=2, behind=x_norm)
            stage("ein", first=2, count=8, peel=2, behind=mem_norm)
            stage("ein", first=8, count=10, peel=2, behind=mem_norm)
            stage("ein", first=10, peel=2, behind=lambda p, par, q: (
                root("mem", RS_MEM) if p == 11 and q == 5 else None))
            stream("p0", 0, 0)
            if upto < 1:
                return
            zx, zb = ST["ein_zx"], ST["ein_zb"]
            for q in range(4):
                rounded(zx, 0, q)
                if q == 2:
                    last_crossed("ein")
            act.wait_ge(stored, STORED["ein"] + 12)
            act.wait_ge(par_done, 1)
            sg = ob[:, 16:24, :]
            af(sg, w[:, 0:8, :], ACT.Sigmoid).then_inc(hg_sig, 1)
            rounded(zx, 0, 4)
            rounded(zx, 0, 5)
            af(ob[:, 8:16, :], w[:, 8:16, :], ACT.Sigmoid, scale=-1.0).then_inc(hg_sig, 1)
            rounded(zx, 0, 6)
            rounded(zx, 0, 7)
            act.wait_ge(hg_q, 1)
            af(sg, w[:, 8:16, :], ACT.Sigmoid).then_inc(hg_sig, 1)
            act.wait_ge(hg_sig, 3)
            for hd in range(8):
                af(w[:, 8 + hd, :], ob[:, 16 + hd, :], ACT.Ln, bias=small[:, 24 + hd:25 + hd],
                   scale=small[:, 32 + hd:33 + hd]).then_inc(hg_logf, 1)
                if hd == 3:
                    crossed(zx, 0, 0)
                rounded(zx, 1, hd)
            copy_values(range(16, 24), w)
            crossed(zx, 1, 1)
            act.wait_ge(x_ready, XR["p0"] + 1)
            for name, buf in (("w_r", sm), ("w_i", pt)):
                act.dma_start(buf[:, :, :, :].rearrange("p a b c -> p (a b c)"), A[name]).then_inc(lr_w, 16)

            def decay(g, level):
                e = ob[:, 16:20, :] if level % 2 else ob[:, 34:38, :]
                act.wait_ge(hg_diff, 8 * g + level)
                af(e, e, ACT.Exp).then_inc(hg_exp, 1)

            for slot in range(18):
                g, level = divmod(slot, 9)
                if level < 8:
                    decay(g, level + 1)
                for p, q in ZX_AT[slot]:
                    rounded(zx, p, q)
                if slot - 1 in ZX_END:
                    p = ZX_END[slot - 1]
                    crossed(zx, p, p % 2)
                if level == 8:
                    act.wait_ge(hg_o, g + 1)
                    for k in range(2):
                        af(w[:, 4 * g + 2 * k:4 * g + 2 * k + 2, :].rearrange("p a b -> p (a b)"), ps[:, 6 + k, :],
                           ACT.Copy).then_inc(hg_ocopied, 1)
            crossed(zx, 7, 1)
            act.wait_ge(hg_ocopied, 4)
            for k in range(4):
                af(ob[:, 16 + 2 * k:18 + 2 * k, :], w[:, 2 * k:2 * k + 2, :], ACT.Square).then_inc(hn_gate, 1)
            for q in range(4):
                rounded(zb, 0, q)
            act.wait_ge(stored, STORED["ein_zx"] + 8)
            act.wait_ge(hg_lv_out, 18)
            af(ob[:, 24:32, :], w[:, 24:32, :], ACT.Sigmoid).then_inc(hn_gate, 1)
            for q in range(4, 8):
                rounded(zb, 0, q)
            act.wait_ge(hn_var, 1)
            af(ob[:, 16:24, :], ob[:, 32:40, :], ACT.Ln).then_inc(hn_std, 1)
            act.wait_ge(hn_std, 1)
            af(ob[:, 16:24, :], ob[:, 16:24, :], ACT.Exp, scale=-0.5).then_inc(hn_std, 1)
            for q in range(2):
                rounded(zb, 1, q)
            for n in range(8):
                if n < 6:
                    rounded(zb, 1, n + 2)
                if n == 2:
                    crossed(zb, 0, 0)
                act.wait_ge(lr_pre, n + 1)
                for j, b in enumerate(("b_b_r", "b_b_i")):
                    af(w[:, 8 + 8 * j + n, :], ps[:, 4 + n % 2, j * T:(j + 1) * T], ACT.Sigmoid,
                       bias=col(b, 1, n)).then_inc(lr_act, 1)
            for q in range(4):
                rounded(zb, 2, q)
                if q == 2:
                    crossed(zb, 1, 1)
            act.wait_ge(lr_act, 16)
            act.wait_ge(hn_gate, 6)
            for n in range(8):
                af(ob[:, 24 + n, :], w[:, 8 + n, :], ACT.Tanh, scale=small[:, 40 + n:41 + n]).then_inc(lr_th, 1)
            for n in range(8):
                af(ob[:, 16 + n, :], w[:, 8 + n, :], ACT.Exp, scale=small[:, 48 + n:49 + n]).then_inc(lr_th, 1)
            for q in range(4, 8):
                rounded(zb, 2, q)
            act.wait_ge(lr_fix, 1)
            af(ob[:, 24:32, :], ob[:, 24:32, :], ACT.Sqrt).then_inc(lr_root, 1)
            for q in range(8):
                rounded(zb, 3, q)
                if q == 2:
                    crossed(zb, 2, 0)

            def zb_behind(p, par, q):
                if p == 1 and q == 1:
                    act.wait_ge(stored, STORED["ein_zb"] + 4)
                    af(ob[:, 32:40, :], w[:, 24:32, :], ACT.Sigmoid).then_inc(lr_root, 1)

            if upto < 3:
                return

            def tail(l, norm, before=None, ple_behind=None):
                ple, so, sg = ST[f"ple{l}"], ST["eout" if l == 0 else "oout"], ST[f"gate{l}"]

                def ple_norm(p, par, q):
                    static = isinstance(p, int)
                    if static and p == 0 and q in (4, 6):
                        act.wait_ge(pair_out, ple.pair0 + ple.pairs)
                        k = 8 * (q // 6)
                        af(w[:, k:k + 8, :], w[:, 16 + k:24 + k, :], ACT.Square).then_inc(sq_ready, 1)
                    if static and p == 2 and q == 4:
                        root(ple.name, RS_PLE)

                def gate_norm(p, par, q):
                    if not (isinstance(p, int) and p == 0):
                        if q == 4:
                            gate_sigmoid(sg, p - 1)
                        if q == 7:
                            square_h(norm, sg.name, p - 1)

                stage(ple.name, before, peel=2, behind=lambda p, par, q: (
                    ple_behind(p, par, q) if ple_behind and isinstance(p, int) else None))
                stage(so.name, ple.name, behind=ple_norm, peel=3)
                stage(sg.name, so.name, behind=gate_norm, peel=3)

            def gate_sigmoid(sg, p):
                act.wait_ge(pair_out, p + (sg.pair0 + 1))
                af(tb[:, :, :], tb[:, :, :], ACT.Sigmoid).then_inc(g_sig, 1)

            tail(0, "h1", "ein_zb", zb_behind)
            if upto < 4:
                return

            def end_of_gate(p, q, sg, norm):
                if p == 0 and q == 4:
                    gate_sigmoid(sg, 7)
                if p == 0 and q == 7:
                    square_h(norm, sg.name, 7)

            def oqk_behind(p, par, q):
                if isinstance(p, int):
                    end_of_gate(p, q, ST["gate0"], "h1")
                    if p == 1 and q == 4:
                        root("h1", RS_LAYER)

            def conv_sigmoid(p, par):
                act.wait_ge(cv_pre, p * 2 + 2)
                if not (isinstance(p, int) and p < 2):
                    act.wait_ge(cv_done, p - 1)
                af(sm[:, par, :, :], w[:, 38 + 2 * par:40 + 2 * par, :], ACT.Sigmoid).then_inc(cv_sig, 1)

            def conv_behind(p, par, q):
                static = isinstance(p, int)
                if q == 1 and not (static and p < 2):
                    conv_sigmoid(p - 2, par)
                if static and p == 0 and q == 7:
                    act.wait_ge(mg_in, 1)
                    af(w[:, 36, :], w[:, 36, :], ACT.Exp, scale=-1.0).then_inc(mg_exp, 1)
                if static and p == 3 and q == 5:
                    act.wait_ge(mg_g, 2)
                    af(small[:, 0:16], ps[:, 7, 0:16], ACT.Copy).then_inc(mg_gcols, 1)

            def values_behind(p, par, q):
                if p < 2 and q == 1:
                    conv_sigmoid(6 + p, p)
                if p in (2, 3) and q == 3:
                    copy_values(range(8 * p, 8 * p + 8), w)

            stage("oqk", "gate0", peel=2, behind=oqk_behind)
            stage("ogate", "oqk")
            stage("ov", "ogate", behind=conv_behind, peel=4)
            stage("ogz", "ov", count=4, peel=4, behind=values_behind)
            ogz = ST["ogz"]

            def gates_chunk(c, start=0, end=4):
                p = 4 + c // 2
                for q in range(4 * (c % 2) + start, 4 * (c % 2) + end):
                    rounded(ogz, p, q)
                if c % 2 == 0 and end == 4:
                    crossed(ogz, p - 1, 1 - p % 2)

            def head_gates(hd):
                act.wait_ge(stored, STORED["ogz"] + 2 * hd + 2)
                if hd:
                    act.wait_ge(x_ready, XR["y1"] + hd)
                af(w[:, 36:40, :], oa[:, 4 * hd:4 * hd + 4, :], ACT.Sigmoid).then_inc(y_gate, 1)

            act.wait_ge(cv_done, 8)
            stream("p1", 0, 0)
            act.wait_ge(mg_gcols, 1)
            for hd in range(8):
                gates_chunk(3 * hd)
                act.wait_ge(ml_mask, hd + 1)
                for kt in range(2):
                    af(sm[:, 0, kt, :], sm[:, 0, kt, :], ACT.Exp, scale=-1.0,
                       bias=small[:, 8 * kt + hd:8 * kt + hd + 1]).then_inc(ml_e, 1)
                act.wait_ge(ml_s, hd + 1)
                if hd:
                    act.wait_ge(ml_den, hd)
                af(w[:, 40, :], ps[:, 5, T:2 * T], ACT.Exp, scale=-1.0).then_inc(ml_e, 1)
                gates_chunk(3 * hd + 1)
                act.wait_ge(ml_o, hd + 1)
                af(w[:, 41, :], ps[:, 7, 0:T], ACT.Abs).then_inc(ml_e, 1)
                gates_chunk(3 * hd + 2, 0, 2)
                act.wait_ge(ml_h, hd + 1)
                if hd:
                    act.wait_ge(ml_sums, hd)
                af(pt[:, 1, :, :], w[:, 16 + 2 * hd:18 + 2 * hd, :], ACT.Square).then_inc(ml_sq, 1)
                gates_chunk(3 * hd + 2, 2, 4)
                if hd:
                    head_gates(hd - 1)
                act.wait_ge(ml_var, hd + 1)
                af(w[:, 41, :], w[:, 42, :], ACT.Sqrt).then_inc(ml_std, 1)
            last_crossed("ogz")

            def head7_behind(p, par, q):
                if p == 1 and q == 1:
                    head_gates(7)

            if upto < 6:
                return
            tail(1, "first", None, head7_behind)
            if upto < 7:
                return
            act.wait_ge(x_ready, XR["p1"] + 1)
            for j in range(2):
                stream("mem2", j, j)

            def memory_stream(j):
                act.wait_ge(x_ready, XR["mem2"] + j + 1)
                stream("mem2", j + 2, j % 2)

            def evc_behind(p, par, q):
                end_of_gate(p, q, ST["gate1"], "first")
                if (p, q) == (1, 3):
                    root("first", RS_Q)
                if (p, q) == (1, 6):
                    root("x2", RS_LAYER)
                if (p, q) in ((1, 5), (1, 7), (2, 3), (2, 6)):
                    memory_stream(2 * p - 2 + int(q > 5))

            def rank_norms(p, par, q):
                if p == 1 and q in (4, 6):
                    j = q // 6
                    act.wait_ge(stored, STORED["evc"] + j + 1)
                    square("cq", j, w[:, 29 + 2 * j:31 + 2 * j, :])
                if p == 2 and q == 4:
                    act.wait_ge(stored, STORED["evc"] + 3)
                    square("ckv", 0, w[:, 33:35, :])
                if p == 3 and q == 3:
                    root("cq", RS_Q)
                if p == 3 and q == 6:
                    root("ckv", RS_KV)

            stage("evc", "gate1", peel=3, behind=evc_behind)
            stage("evkpe", "evc", behind=lambda p, par, q: memory_stream(4 + q // 6) if q in (3, 6) else None)
            stage("evmem", "evkpe", peel=4, behind=rank_norms)
            stage("uq", "evmem")
            stage("ukv", "uq", count=7)
            stage("ukv", first=7, behind=lambda p, par, q: copy_values(MLA_V, w) if q == 1 else None)
            last_crossed("ukv")
            if upto < 8:
                return

            def exps(heads, a, which=(0, 1)):
                for i in which:
                    hd = heads[i]
                    act.wait_ge(at_neg, a + i + 1)
                    s4 = small[:, 16 * i:16 * i + 16]
                    for qt in range(2):
                        ins = af(sm[:, i, qt, :], sm[:, i, qt, :], ACT.Exp, bias=s4[:, qt:qt + 1],
                                 accum_out=s4[:, 2 + qt:3 + qt])
                        if qt == 0 or hd["sink"] is not None:
                            step.post(ins)
                    if hd["sink"] is not None:
                        ins = af(s4[:, 4:6], s4[:, 0:2], ACT.Exp, bias=col("sinks", 1, hd["sink"]))
                    ins.then_inc(at_e, 1)

            def turned_copy(heads, a):
                for i in range(len(heads)):
                    act.wait_ge(at_turned, a + i + 1)
                    af(pt[:, i, :, :].rearrange("p a b -> p (a b)"), ps[:, 6 + i, :], ACT.Copy).then_inc(at_pt, 1)

            gates = [16]

            def attend(couples, gate, a, then):
                st = ST[gate]

                def chunk(c, start, end):
                    p, first, last = gate_chunk(couples, c)
                    for q in range(first, last)[start:end]:
                        rounded(st, p, q)

                chunk(0, 0, 4)
                exps(couples[0], a)
                chunk(0, 4, 8)
                for c, heads in enumerate(couples):
                    p, _, last = gate_chunk(couples, c)
                    if last == st.upp:
                        crossed(st, p, p % 2)
                    turned_copy(heads, a + 2 * c)
                    if c + 1 < len(couples):
                        chunk(c + 1, 0, 4)
                    else:
                        for q in range(4):
                            rounded(ST[then], 0, q)
                    if last == st.upp:
                        act.wait_ge(g_pre, gates[0] - 15)
                        af(cross[:, (st.pair0 + p) % 2, :, :], tb[:, :, :], ACT.Sigmoid).then_inc(g_sig, 1)
                        gates[0] += 1
                    if c + 1 < len(couples):
                        for i in range(2):
                            chunk(c + 1, 4 + i, 5 + i)
                            exps(couples[c + 1], a + 2 * c + 2, (i,))
                        chunk(c + 1, 6, 8)

            attend(MLA_COUPLES, "evgate_a", 0, "evmoba")
            stage("evmoba", count=9, done=4)
            stage("evmoba", first=9, count=13, peel=0)
            stage("evmoba", first=13, behind=lambda p, par, q: copy_values(MOBA_V, w) if q == 3 else None)
            last_crossed("evmoba")
            attend(MOBA_COUPLES, "evgate_b", 8, "evout")

            def out_norm(st, norm):
                def behind(p, par, q):
                    if q == 8 and not (isinstance(p, int) and p == 0):
                        square_h(norm, st.name, p - 1)
                    if start_of(p, q, 8) and norm == "x3":
                        act.wait_ge(at_done, 20)
                        for buf, name in ((rope, "rope_od"), (rot, "rot_od")):
                            act.dma_start(buf[:], A[name]).then_inc(rope_loaded, 32)
                        for j in range(2):
                            stream("mem3", j, j)
                return behind

            def x3_norm(p, par, q):
                if isinstance(p, int) and p == 0 and q == 5:
                    square_h("x3", "evout", 7)
                if isinstance(p, int) and p == 1 and q == 4:
                    root("x3", RS_LAYER)
                if q == 7:
                    act.wait_ge(x_ready, p + (XR["mem3"] + 1))
                    stream("mem3", p + 2, par)

            stage("evout", done=4, behind=out_norm(ST["evout"], "x3"), peel=3)
            if upto < 9:
                return
            stage("odin", "evout", count=6, peel=2, behind=x3_norm)
            stage("odin", first=6, peel=0)
            stage("odmem", "odin", count=3, peel=3)
            stage("odmem", first=3, behind=lambda p, par, q: copy_values(OD_V, w) if q == 3 else None)
            last_crossed("odmem")
            attend(OD_COUPLES, "odgate", 20, "odout")
            stage("odout", done=4, behind=out_norm(ST["odout"], "last"), peel=3)
            last_crossed("odout")
            square_h("last", "odout", 7)
            root("last", RS_LAYER)

        @block.vector
        def _(dve):
            step = Steps(dve, dve_step)
            tt, ts, stt, cp = (nc.vector.tensor_tensor, nc.vector.tensor_scalar, nc.vector.scalar_tensor_tensor,
                               nc.vector.tensor_copy)

            def split(src, gain, x, kt, count):
                if gain is not None:
                    step(tt(tb[:, :, :], src, wide(gain, 2), MUL))
                    src = tb[:, :, :]
                hi = x[:, ds(kt, 2), 0:T]
                step(cp(hi, src))
                tt(x[:, ds(kt, 2), T:2 * T], src, hi.bitcast(F32), SUB).then_inc(x_ready, 1)
                dve.wait_ge(x_ready, count)

            def take(st, p, par, dst):
                pair = st.pair0 + p
                dve.wait_ge(cross_ready, pair + 1)
                tt(dst, ps[:, banks(st, par), 0:T], cross[:, (st.pair0 + par) % 2, 0:st.nb, :],
                   ADD).then_inc(pair_out, 1)
                dve.wait_ge(pair_out, pair + 1)

            def store(name, buf, at, scale, first=0, count=None, adding=None, behind=0):
                st = ST[name]

                def pair(p, par):
                    dst = buf[:, ds(p * st.nb + at, st.nb), :]
                    take(st, p, par, dst)
                    tt(dst, dst, along(rs[:, scale, :], st.nb), MUL).then_inc(stored, 1)
                    if adding:
                        add_squares(adding, p - behind)

                pairs_loop(dve, st.pairs if count is None else count, pair, first)
                dve.wait_ge(stored, STORED[name] + (st.pairs if count is None else count))

            def take_ple(l, p):
                take(ST[f"ple{l}"], p, p % 2, w[:, 16 + 2 * p:18 + 2 * p, :])

            def root(name, which, width):
                half = square_sums(name)[1]
                dve.wait_ge(sums_ready, ROOTS[name] + (2 if name in ("first", "cq") else 1))
                ts(tb[:, 0, :], ps[:, 7, half * T:half * T + T], 1.0 / width, EPS, MUL, ADD).then_inc(var_ready, 1)
                dve.wait_ge(std_ready, ROOTS[name] + 1)
                inverse(rs[:, which, :], tb[:, 0, :], tb[:, 1, :])

            def add_squares(name, j):
                at, added, _, _ = NORMS[name]
                n, second = (2, int(name == "x2")) if name in ("first", "x2") else (1, 0)
                acc = square_sums(name)[0]
                dve.wait_ge(sq_ready, j * n + (at + second + 1))
                tt(acc, acc, w[:, 42:44, :] if second else sq_next, ADD).then_inc(sq_added, 1)
                dve.wait_ge(sq_added, j * n + (added + second + 1 - n))

            def fold_squares(name):
                dve.wait_ge(sq_ready, NORMS[name][2])
                step(tt(w[:, 0:8, :], w[:, 0:8, :], w[:, 8:16, :], ADD))
                step(tt(w[:, 0:4, :], w[:, 0:4, :], w[:, 4:8, :], ADD))
                tt(w[:, 0:2, :], w[:, 0:2, :], w[:, 2:4, :], ADD).then_inc(sq_added, 1)
                dve.wait_ge(sq_added, NORMS[name][3])

            def inverse(r, v, t):
                step(nc.vector.reciprocal(r, r))
                newton(r, v, t)

            def newton(r, v, t):
                step(tt(t, r, r, MUL))
                step(tt(t, t, v, MUL))
                step(ts(t, t, -0.5, 1.5, MUL, ADD))
                step(tt(r, r, t, MUL))

            def streamed(name, j, par, gain, x, kt):
                n = STREAM[name] + par
                loads = 16 * (n // 2 + 1) if isinstance(j, int) and j == par else (j - par) * 8 + 16 * (n // 2 + 1)
                dve.wait_ge(stream_loaded[n % 2], loads)
                split(sm[:, n % 2, :, :], gain, x, kt, j + (XR[name] + 1))

            def log1p(y, z, zz, p):
                step(ts(z, y, 2.0, None, ADD))
                step(nc.vector.reciprocal(z, z))
                step(tt(z, z, y, MUL))
                step(tt(zz, z, z, MUL))
                step(ts(p, zz, 1.0 / 21, None, MUL))
                for k in range(9, 0, -1):
                    step(stt(p, p, 1.0 / (2 * k + 1), zz, ADD, MUL))
                step(stt(p, p, 1.0, z, ADD, MUL))
                step(ts(p, p, 2.0, None, MUL))

            nc.vector.memset(ones[:, :], 1.0).then_inc(ones_set, 1)
            dve.wait_ge(cols_loaded, 16)
            for j in range(8):
                dve.wait_ge(x_loaded[j // 2], 16)
                split(h[:, 2 * j:2 * j + 2, :], col("e_norm", 2, 2 * j), xa, 2 * j, XR["x"] + j + 1)
            fold_squares("x")
            l0, l1, lam = col("a_lb0"), col("a_lb1"), col("b_lambda")
            step(tt(small[:, 24:32], l0, l1, MAX))
            step(tt(small[:, 0:8], l0, small[:, 24:32], SUB))
            step(tt(small[:, 8:16], l1, small[:, 24:32], SUB))
            step(stt(small[:, 40:48], lam, -1.0, lam, MUL, MAX))
            ts(small[:, 16:24], small[:, 40:48], -1.0, None, MUL).then_inc(par_in, 1)
            root("x", RS_LAYER, D)
            store("ein", w, 0, RS_LAYER, 0, 3)
            dve.wait_ge(par_exp, 1)
            step(tt(small[:, 8:16], small[:, 0:8], small[:, 8:16], ADD))
            step(nc.vector.reciprocal(small[:, 8:16], small[:, 8:16]))
            step(tt(small[:, 24:32], small[:, 0:8], small[:, 8:16], MUL))
            step(ts(small[:, 32:40], small[:, 24:32], -1.0, 1.0, MUL, ADD))
            log1p(small[:, 16:24], small[:, 0:8], small[:, 8:16], small[:, 40:48])
            step(ts(small[:, 0:8], lam, -1.0, 0.0, MUL, MAX))
            step(tt(small[:, 40:48], small[:, 40:48], small[:, 0:8], ADD))
            step(ts(small[:, 40:48], small[:, 40:48], 8.0, None, MUL))
            ts(small[:, 48:56], small[:, 40:48], -1.0, None, MUL).then_inc(par_done, 1)
            oml = small[:, 32:40]
            step(tt(col("ev_norm"), col("ev_norm"), col("final_norm"), MUL))
            store("ein", w, 0, RS_LAYER, 3, 10, adding="mem", behind=2)
            store("ein", w, 0, RS_LAYER, 10, 11)
            root("mem", RS_MEM, D)
            store("ein", w, 0, RS_LAYER, 11)
            streamed("p0", 0, 0, None, xs, 0)
            dve.wait_ge(consts_loaded, 16 * 6)
            step(cp(lvl[:, :, :].rearrange("p a b -> p (a b)"), ob[:, 36:40, :].rearrange("p a b -> p (a b)")))
            if upto < 1:
                return
            dve.wait_ge(par_done, 1)
            dve.wait_ge(hg_sig, 1)
            q, kk = w[:, 0:8, :], ob[:, 8:16, :]
            tt(q, q, ob[:, 16:24, :], MUL).then_inc(hg_q, 1)
            dve.wait_ge(hg_sig, 2)
            tt(kk, kk, wide(oml, 8), MUL).then_inc(hg_qk, 1)
            for hd in range(8):
                dve.wait_ge(hg_logf, hd + 1)
                for c in range(4):
                    bc = w[:, 8 + hd, 64 * c:64 * c + 64]
                    step.post(nc.vector.tensor_tensor_scan(bc, ones[:, 0:64], bc, 0.0, MUL, ADD))
            step.post(nc.vector.memset(ob[:, 20:28, :], 0.0))
            step.wait()
            dve.wait_ge(hg_q, 1)
            dve.wait_ge(hg_qk, 1)
            store("ein_zx", w, 24, RS_LAYER, 0, 1)
            dve.wait_ge(hg_logf, 8)
            am = ob[:, 28:34, :].rearrange("p a b -> p (a b)")

            def results(slot):
                p = 1 if slot == 1 else ZX_END.get(slot - 2)
                if p:
                    store("ein_zx", w, 24, RS_LAYER, p, p + 1)

            for g in range(2):
                qg, kg = w[:, 4 * g:4 * g + 4, :], ob[:, 8 + 4 * g:12 + 4 * g, :]
                b = w[:, 8 + 4 * g:12 + 4 * g, :].rearrange("p a b -> p (a b)")

                def differences(level):
                    e = (ob[:, 16:20, :] if level % 2 else ob[:, 34:38, :]).rearrange("p a b -> p (a b)")
                    size = 2 ** level
                    half = size // 2
                    ev = e.rearrange("p (n s) -> p n s", s=size)
                    bv = b.rearrange("p (n s) -> p n s", s=size)
                    n = 1024 // size
                    if level <= 6:
                        mid = bv[:, :, half - 1:half].to_broadcast([P, n, half])
                        step.post(tt(ev[:, :, half:size], bv[:, :, half:size], mid, SUB))
                        ins = tt(ev[:, :, 0:half], mid, bv[:, :, 0:half], SUB)
                    elif level == 7:
                        step.post(cp(ev[:, :, 64:128], bv[:, :, 64:128]))
                        ins = tt(ev[:, :, 0:64], bv[:, :, 63:64].to_broadcast([P, n, 64]), bv[:, :, 0:64], SUB)
                    else:
                        def last(c):
                            return bv[:, :, 64 * c + 63:64 * c + 64].to_broadcast([P, n, 64])

                        step.post(cp(ev[:, :, 128:192], bv[:, :, 128:192]))
                        step.post(tt(ev[:, :, 192:256], bv[:, :, 192:256], last(2), ADD))
                        step.post(tt(ev[:, :, 64:128], last(1), bv[:, :, 64:128], SUB))
                        step(tt(ev[:, :, 0:64], last(0), bv[:, :, 0:64], SUB))
                        ins = tt(ev[:, :, 0:64], ev[:, :, 0:64], last(1), ADD)
                    ins.then_inc(hg_diff, 1)

                def scaled(level):
                    e = ob[:, 16:20, :] if level % 2 else ob[:, 34:38, :]
                    dve.wait_ge(hg_exp, 8 * g + level)
                    if level > 1:
                        dve.wait_ge(hg_lv_out, 9 * g + level)
                    elif g:
                        dve.wait_ge(hg_lv_out, 9)
                    size = 2 ** level

                    def halves(ap):
                        return ap.rearrange("p a b -> p (a b)").rearrange("p (n s) -> p n s", s=size)

                    lh, rh_ = slice(0, size // 2), slice(size // 2, size)
                    step.post(tt(halves(ob[:, 20:24, :])[:, :, rh_], halves(qg)[:, :, rh_], halves(e)[:, :, rh_], MUL))
                    tt(halves(ob[:, 24:28, :])[:, :, lh], halves(kg)[:, :, lh], halves(e)[:, :, lh],
                       MUL).then_inc(hg_lv_in, 1)
                    dve.wait_ge(hg_lv_in, 8 * g + level)

                def masked(level):
                    n = 9 * g + level
                    dve.wait_ge(hg_lv_out, n + 1)
                    if level < 8:
                        nc.vector.copy_predicated(
                            am[:, 0:1024].rearrange("p (n s) -> p n s", s=P),
                            lvl[:, level, :].unsqueeze(1).to_broadcast([P, 8, P]),
                            ps[:, 4:6, :].rearrange("p a b -> p (a b)").rearrange("p (n s) -> p n s", s=P),
                        ).then_inc(hg_masked, 1)
                    else:
                        cp(am[:, 1024:1536], ps[:, 4, :]).then_inc(hg_masked, 1)
                    dve.wait_ge(hg_masked, n + 1)

                if g:
                    dve.wait_ge(hg_o, 1)
                dve.wait_ge(consts_loaded, 16 * 6)
                step(nc.vector.memset(am[:, 0:1024], 0.0))
                differences(1)
                masked(0)
                results(9 * g)
                for level in range(1, 9):
                    if level < 8:
                        differences(level + 1)
                    scaled(level)
                    masked(level)
                    results(9 * g + level)
            store("ein_zx", w, 24, RS_LAYER, 7, 8)

            def convolve_block(n):
                xb_, xc = w[:, 32 + n, :], ob[:, 8 + n, :]

                def tap(k):
                    return col("b_conv_w", 1, 8 * k + n)

                step(ts(xc, xb_, tap(3), col("b_conv_b", 1, n), MUL, ADD))
                for k in (2, 1):
                    s = 3 - k
                    step(stt(xc[:, s:T], xb_[:, 0:T - s], tap(k), xc[:, s:T], MUL, ADD))
                stt(xc[:, 3:T], xb_[:, 0:T - 3], tap(0), xc[:, 3:T], MUL, ADD).then_inc(lr_conv, 1)

            for n in range(4):
                convolve_block(n)
            dve.wait_ge(hn_sums, 1)
            rh = ob[:, 32:40, :]
            ts(rh.rearrange("p a b -> p (a b)"), ps[:, 4:8, :].rearrange("p a b -> p (a b)"), 1.0 / P, EPS, MUL,
               ADD).then_inc(hn_var, 1)
            for n in range(4, 8):
                convolve_block(n)
            dve.wait_ge(lr_conv, 8)
            ya, z = w[:, 0:8, :], w[:, 24:32, :]
            dve.wait_ge(hn_gate, 5)
            step(tt(z, z, ob[:, 24:32, :], MUL))
            step(tt(z, z, wide(col("a_norm"), 8), MUL))
            dve.wait_ge(hg_ocopied, 4)
            step(tt(ya, ya, z, MUL))
            dve.wait_ge(hn_std, 2)
            newton(ob[:, 16:24, :], rh, ob[:, 24:32, :])
            tt(ya, ya, ob[:, 16:24, :], MUL).then_inc(hn_gate, 1)
            dve.wait_ge(hn_gate, 6)
            if upto < 2:
                return
            for p in range(2):
                store("ein_zb", w, 24, RS_LAYER, p, p + 1)
            th, t1, ig, xc, a = ob[:, 24:32, :], ob[:, 32:40, :], w[:, 16:24, :], ob[:, 8:16, :], ob[:, 16:24, :]
            y_lru = w[:, 32:40, :]
            dve.wait_ge(lr_act, 16)
            step(tt(ig, ig, xc, MUL))
            dve.wait_ge(lr_th, 16)
            step(tt(t1, a, a, MUL))
            stt(th, t1, 1.0, th, ADD, MUL).then_inc(lr_fix, 1)
            dve.wait_ge(lr_root, 1)
            step(tt(ig, ig, th, MUL))
            for n in range(8):
                step.post(nc.vector.tensor_tensor_scan(y_lru[:, n, :], a[:, n, :], ig[:, n, :], 0.0, MUL, ADD))
            step.wait()
            for j in range(4):
                split(w[:, 2 * j:2 * j + 2, :], None, xb, 2 * j, XR["y0"] + j + 1)
            store("ein_zb", w, 24, RS_LAYER, 2, 3)
            store("ein_zb", w, 24, RS_LAYER, 3, 4)
            for k in (0, 4):
                for p in (0,) if k == 0 else (1, 2, 3):
                    take_ple(0, p)
                if k == 0:
                    dve.wait_ge(lr_root, 2)
                yb, zb = w[:, 8 + k:12 + k, :], w[:, 24 + k:28 + k, :]
                step(tt(zb, zb, t1[:, k:k + 4, :], MUL))
                step(tt(yb, y_lru[:, k:k + 4, :], zb, MUL))
                for j in range(4 + k // 2, 6 + k // 2):
                    split(w[:, 2 * j:2 * j + 2, :], None, xb, 2 * j, XR["y0"] + j + 1)
            if upto < 3:
                return

            def tail(l, x_out, x_h, x_next, gain_next, x_next_buf):
                st = ST[f"ple{l}"]
                pairs_loop(dve, 8, lambda p, par: take(st, p, par, w[:, ds(p * 2 + 16, 2), :]), 4)
                so, xo = ST["eout" if l == 0 else "oout"], X[ST[f"gate{l}"].x]

                def out_pair(p, par):
                    hp = h[:, ds(p * 2, 2), :]
                    take(so, p, par, tb[:, :, :])
                    step(tt(hp, hp, tb[:, :, :], ADD))
                    split(hp, None, xo, p * 2, p + (XR[x_h] + 1))

                out_pair(0, 0)
                fold_squares(f"ple{l}")
                out_pair(1, 1)
                root(f"ple{l}", RS_PLE, D)
                pairs_loop(dve, 8, out_pair, 2, steps=step, per=2)
                sg = ST[f"gate{l}"]

                def gate_pair(p, par):
                    hp, pl = h[:, ds(p * 2, 2), :], w[:, ds(p * 2 + 16, 2), :]
                    pair = sg.pair0 + p
                    step(tt(pl, pl, along(rs[:, RS_PLE, :], 2), MUL))
                    step(tt(pl, pl, wide(col(f"ple_norm{l}", 2, p * 2), 2), MUL))
                    dve.wait_ge(cross_ready, pair + 1)
                    tt(tb[:, :, :], ps[:, banks(sg, par), 0:T], cross[:, (sg.pair0 + par) % 2, :, :],
                       ADD).then_inc(pair_out, 1)
                    dve.wait_ge(g_sig, p + (8 * l + 1))
                    step(tt(tb[:, :, :], tb[:, :, :], pl, MUL))
                    tt(hp, hp, tb[:, :, :], ADD).then_inc(h_ready, 1)
                    dve.wait_ge(h_ready, p + (HR[f"gate{l}"] + 1))
                    split(hp, col(gain_next, 2, p * 2), x_next_buf, p * 2, p + (XR[x_next] + 1))
                    if not (isinstance(p, int) and p < 2):
                        add_h(p - 1)

                def add_h(j):
                    for name in (("h1",) if l == 0 else ("first", "x2")):
                        add_squares(name, j)

                gate_pair(0, 0)
                gate_pair(1, 1)
                pairs_loop(dve, 8, gate_pair, 2, steps=step, per=5)
                add_h(7)

            tail(0, "eout", "h0", "h1", "o_norm", xb)
            if upto < 4:
                return
            root("h1", RS_LAYER, D)
            store("oqk", w, 0, RS_LAYER)
            store("ogate", w, 32, RS_LAYER)
            gx, gb, gm, t0, t1, t2, t3 = (w[:, 32 + i, :] for i in range(7))
            step(ts(gx, gx, col("c_gate_b"), None, ADD))
            step(ts(t0, gx, 0.0, None, ALU.min))
            stt(t1, gx, -1.0, gx, MUL, MAX).then_inc(mg_in, 1)
            dve.wait_ge(mg_exp, 1)
            log1p(t1, t2, t3, gm)
            step(tt(t0, t0, gm, SUB))
            step(ts(t2, t1, 0.0, 1.0, MUL, ADD))
            nc.vector.tensor_tensor_scan(gb, t2, t0, 0.0, MUL, ADD).then_inc(mg_lf, 1)
            dve.wait_ge(mg_lf, 1)

            def convolve(p, par):
                for b in range(2):
                    src, acc = w[:, ds(p * 2 + b, 1), :], w[:, 38 + 2 * par + b:39 + 2 * par + b, :]

                    def tap(k):
                        return col("c_conv_w", 1, p * 2 + (16 * k + b))

                    step(ts(acc, src, tap(3), col("c_conv_b", 1, p * 2 + b), MUL, ADD))
                    for k in (2, 1):
                        sh = 3 - k
                        step(stt(acc[:, :, sh:T], src[:, :, 0:T - sh], tap(k), acc[:, :, sh:T], MUL, ADD))
                    stt(acc[:, :, 3:T], src[:, :, 0:T - 3], tap(0), acc[:, :, 3:T], MUL, ADD).then_inc(cv_pre, 1)
                dve.wait_ge(cv_pre, p * 2 + 2)

            def silu(p, par):
                dve.wait_ge(cv_sig, p + 1)
                tt(w[:, ds(p * 2, 2), :], w[:, 38 + 2 * par:40 + 2 * par, :], sm[:, par, :, :], MUL).then_inc(cv_done, 1)
                dve.wait_ge(cv_done, p + 1)

            sv = ST["ov"]

            def values_pair(p, par):
                dst = w[:, ds(p * 2 + 16, 2), :]
                take(sv, p, par, dst)
                tt(dst, dst, along(rs[:, RS_LAYER, :], 2), MUL).then_inc(stored, 1)
                if not (isinstance(p, int) and p == 0):
                    silu(p - 1, 1 - par)
                convolve(p, par)

            values_pair(0, 0)
            values_pair(1, 1)
            dve.wait_ge(mg_g, 1)
            nc.vector.tensor_tensor_scan(gm, t2, ps[:, 6, 0:T], 0.0, MUL, MAX).then_inc(mg_max, 1)
            dve.wait_ge(mg_max, 1)
            pairs_loop(dve, 8, values_pair, 2, steps=step, per=6)
            silu(7, 1)
            if upto < 5:
                return
            store("ogz", oa, 0, RS_LAYER, 0, 3)

            def gates_chunk(c):
                if c % 2 == 0:
                    store("ogz", oa, 0, RS_LAYER, 3 + c // 2, 4 + c // 2)

            def finish(hd):
                hb, og, z = w[:, 16 + 2 * hd:18 + 2 * hd, :], oa[:, 4 * hd:4 * hd + 2, :], oa[:, 4 * hd + 2:4 * hd + 4, :]
                step.post(tt(hb, hb, wide(col("c_norm", 2, 2 * hd), 2), MUL))
                dve.wait_ge(y_gate, hd + 1)
                step(tt(z, z, w[:, 38:40, :], MUL))
                step(tt(hb, hb, w[:, 36:38, :], MUL))
                step(tt(hb, hb, z, MUL))
                split(hb, None, xa, 2 * hd, XR["y1"] + hd + 1)

            for hd in range(8):
                dve.wait_ge(ml_s, hd + 1)
                tt(sm[:, 0, :, :], masks[:, M_LSTM, :, :], along(ps[:, 5, 0:T], 2), ADD).then_inc(ml_mask, 1)
                gates_chunk(3 * hd)
                dve.wait_ge(ml_e, 4 * hd + 2)
                if hd:
                    dve.wait_ge(ml_o, hd)
                stt(pt[:, 0, :, :].rearrange("p a b -> p (a b)"), ps[:, 4, :], float(P) ** -0.5,
                    sm[:, 0, :, :].rearrange("p a b -> p (a b)"), MUL, MUL).then_inc(ml_p, 1)
                dve.wait_ge(ml_p, hd + 1)
                gates_chunk(3 * hd + 1)
                dve.wait_ge(ml_e, 4 * hd + 4)
                tt(w[:, 43, :], w[:, 40, :], w[:, 41, :], MAX).then_inc(ml_den, 1)
                dve.wait_ge(ml_den, hd + 1)
                step(nc.vector.reciprocal(w[:, 43, :], w[:, 43, :]))
                hb = w[:, 16 + 2 * hd:18 + 2 * hd, :]
                tt(hb, ps[:, 6, :].rearrange("p (a b) -> p a b", b=T), along(w[:, 43, :], 2), MUL).then_inc(ml_h, 1)
                dve.wait_ge(ml_sums, hd + 1)
                ts(w[:, 42, :], ps[:, 7, T:2 * T], 1.0 / (2 * P), EPS, MUL, ADD).then_inc(ml_var, 1)
                if hd:
                    finish(hd - 1)
                else:
                    streamed("p1", 0, 0, None, xs, 0)
                gates_chunk(3 * hd + 2)
                dve.wait_ge(ml_std, hd + 1)
                inverse(w[:, 41, :], w[:, 42, :], w[:, 43, :])
                step(tt(hb, hb, along(w[:, 41, :], 2), MUL))
            store("ogz", oa, 0, RS_LAYER, 15, 16)
            for p in range(4):
                take_ple(1, p)
            finish(7)
            if upto < 6:
                return
            tail(1, "oout", "h2", "x2", "ev_norm", xa)
            if upto < 7:
                return
            def memory(name, j, par, gain):
                streamed(name, j, par, col(gain, 2, j * 2), xb, j * 2)

            for j in range(2):
                memory("mem2", j, j, "ev_mem_norm")
            root("first", RS_Q, D)
            rf, rl, v = rs[:, RS_Q, :], rs[:, RS_LAYER, :], tb[:, 0, :]
            step(tt(rl, rf, rf, MUL))
            step(stt(v, ps[:, 7, T:2 * T], 1.0 / D, rl, MUL, MUL))
            ts(v, v, EPS, None, ADD).then_inc(var_ready, 1)
            dve.wait_ge(std_ready, ROOTS["x2"] + 1)
            inverse(rl, v, tb[:, 1, :])
            step(tt(rl, rl, rf, MUL))
            for p in range(3):
                store("evc", w, 29, RS_LAYER, p, p + 1)
                for j in (2 * p + 2, 2 * p + 3):
                    memory("mem2", j, j % 2, "ev_mem_norm")
            store("evkpe", w, 28, RS_LAYER)
            for j in range(2):
                split(w[:, 29 + 2 * j:31 + 2 * j, :], col("ev_q_norm", 2, 2 * j), xs, 2 * j, XR["cq"] + j + 1)
            split(w[:, 33:35, :], col("ev_kv_norm", 2, 0), xs, 4, XR["ckv"] + 1)
            step(tt(h[:, :, :], h[:, :, :], along(rf, 16), MUL))
            step(tt(h[:, :, :], h[:, :, :], wide(col("final_norm"), 16), MUL))
            store("evmem", w, 35, RS_MEM, 0, 2)
            add_squares("cq", 1)
            store("evmem", w, 35, RS_MEM, 2, 3)
            root("cq", RS_Q, 512)
            root("ckv", RS_KV, 256)
            store("evmem", w, 35, RS_MEM, 3, 4)
            store("uq", w, 0, RS_Q)
            if upto < 8:
                return

            def rotate(n, par, kind, at, nb):
                dve.wait_ge(rp_sums, n + 1)
                x = w[:, ds(at, nb), :]
                step.post(tt(tb[:, 0:nb, :], ps[:, 6 + par, 0:nb * T].rearrange("p (a b) -> p a b", b=T),
                             along(rope[:, kind, 1, :], nb), MUL))
                step(tt(x, x, along(rope[:, kind, 0, :], nb), MUL))
                tt(x, x, tb[:, 0:nb, :], ADD).then_inc(rp_taken, 1)
                dve.wait_ge(rp_taken, n + 1)

            for p in range(8):
                store("ukv", w, 20 if p < 4 else 4, RS_KV, p, p + 1)
                if p in (1, 2, 3):
                    rotate(p - 1, (p - 1) % 2, 0, *MLA_ROPE[p - 1])

            def softmax_in(heads, a):
                for i, hd in enumerate(heads):
                    s4 = small[:, 16 * i:16 * i + 16]
                    dve.wait_ge(at_s, a + i + 1)
                    if a + i >= 2:
                        dve.wait_ge(at_turned, a + i - 1)
                    dst, src = sm[:, i, :, :].rearrange("p a b -> p (a b)"), ps[:, 4 + i, :]
                    if hd["mask"] is None:
                        step(ts(dst, src, hd["scale"], None, MUL))
                    else:
                        step(stt(dst, src, hd["scale"], masks[:, hd["mask"], :, :].rearrange("p a b -> p (a b)"), MUL,
                                 ADD))
                    if hd["sink"] is None:
                        nc.vector.tensor_reduce(s4[:, 0:2], sm[:, i, :, :], AX, MAX, negate=True).then_inc(at_neg, 1)
                    else:
                        step(nc.vector.tensor_reduce(s4[:, 6:8], sm[:, i, :, :], AX, MAX))
                        ts(s4[:, 0:2], s4[:, 6:8], col("sinks", 1, hd["sink"]), -1.0, MAX, MUL).then_inc(at_neg, 1)

            def softmax_out(heads, a):
                for i, hd in enumerate(heads):
                    s4 = small[:, 16 * i:16 * i + 16]
                    dve.wait_ge(at_e, a + i + 1)
                    if hd["sink"] is not None:
                        step(tt(s4[:, 2:4], s4[:, 2:4], s4[:, 4:6], ADD))
                    step(nc.vector.reciprocal(s4[:, 2:4], s4[:, 2:4]))
                    tt(sm[:, i, :, :], sm[:, i, :, :], wide(s4[:, 2:4], 2), MUL).then_inc(at_p, 1)

            def keep(heads, a):
                for i, hd in enumerate(heads):
                    vb, v0, vn, p0 = hd["v"]
                    dve.wait_ge(at_o, a + i + 1)
                    cp(w[p0:p0 + vn, hd["o"], :], ps[p0:p0 + vn, 6 + i, 0:T]).then_inc(at_done, 1)

            gates = [16]

            def gate_in(st, p):
                pair = st.pair0 + p
                dve.wait_ge(cross_ready, pair + 1)
                step(tt(tb[:, :, :], ps[:, banks(st, p % 2), 0:T], cross[:, pair % 2, :, :], ADD))
                tt(tb[:, :, :], tb[:, :, :], along(rs[:, RS_LAYER, :], 2), MUL).then_inc(g_pre, 1)

            def gate_out(st, p, blocks, x_at, x_count):
                pair = st.pair0 + p
                dve.wait_ge(g_sig, gates[0] + 1)
                gates[0] += 1
                tt(tb[:, :, :], tb[:, :, :], cross[:, pair % 2, :, :], MUL).then_inc(pair_out, 1)
                dve.wait_ge(pair_out, pair + 1)
                step(tt(tb[:, :, :], tb[:, :, :], w[:, blocks[0]:blocks[0] + 2, :], MUL))
                split(tb[:, :, :], None, xb, x_at, x_count)

            def attend(couples, gate, a, x_at, x_count):
                st = ST[gate]
                softmax_in(couples[0], a)
                softmax_out(couples[0], a)
                for c, heads in enumerate(couples):
                    p, _, last = gate_chunk(couples, c)
                    if last == st.upp:
                        gate_in(st, p)
                    if c + 1 < len(couples):
                        softmax_in(couples[c + 1], a + 2 * c + 2)
                    keep(heads, a + 2 * c)
                    if last == st.upp:
                        dve.wait_ge(at_done, a + 2 * c + 2)
                        gate_out(st, p, heads[-1]["gate"], x_at + 2 * p, x_count + p + 1)
                    if c + 1 < len(couples):
                        softmax_out(couples[c + 1], a + 2 * c + 2)

            attend(MLA_COUPLES, "evgate_a", 0, 0, XR["y2"])

            def results_pair(name, rope_at, kind, nb, memory_behind=False):
                st = ST[name]

                def pair(p, par):
                    dst = w[:, ds(p * 2, 2), :]
                    take(st, p, par, dst)
                    tt(dst, dst, along(rs[:, RS_LAYER, :], 2), MUL).then_inc(stored, 1)
                    if memory_behind:
                        memory("mem3", p + 2, par, "od_mem_norm")
                    if nb:
                        dve.wait_ge(stored, p + STORED[name])
                        rotate(p + (rope_at - 1), (rope_at + 1 + par) % 2, kind, p * 2 - 2, nb)

                return pair

            store("evmoba", w, 0, RS_LAYER, 0, 1)
            pairs_loop(dve, 9, results_pair("evmoba", MOBA_ROT, 1, 2), 1, steps=step, per=2)
            store("evmoba", w, 0, RS_LAYER, 9)
            attend(MOBA_COUPLES, "evgate_b", 8, 8, XR["y2"] + 4)

            def add_out(name, x_next, gain):
                st = ST[name]

                def pair(p, par):
                    hp = h[:, ds(p * 2, 2), :]
                    take(st, p, par, tb[:, :, :])
                    tt(hp, hp, tb[:, :, :], ADD).then_inc(h_ready, 1)
                    dve.wait_ge(h_ready, p + (HR[name] + 1))
                    if x_next:
                        split(hp, col(gain, 2, p * 2), xa, p * 2, p + (XR[x_next] + 1))
                    if not (isinstance(p, int) and p < 2):
                        add_squares(norm, p - 1)

                norm = x_next or "last"
                pair(0, 0)
                pair(1, 1)
                pairs_loop(dve, 8, pair, 2, steps=step, per=2 if x_next else 0)
                add_squares(norm, 7)

            add_out("evout", "x3", "od_norm")
            if upto < 9:
                return
            for j in range(2):
                memory("mem3", j, j, "od_mem_norm")
            root("x3", RS_LAYER, D)
            dve.wait_ge(rope_loaded, 32 * 2)
            results_pair("odin", 0, 0, 0, True)(0, 0)
            pairs_loop(dve, 5, results_pair("odin", OD_ROT, 0, 2, True), 1, steps=step, per=4)
            results_pair("odin", OD_ROT, 0, 1, True)(5, 1)
            pairs_loop(dve, 12, results_pair("odin", OD_ROT, 1, 2), 6, steps=step, per=2)
            store("odin", w, 0, RS_LAYER, 12)
            store("odmem", w, 36, RS_MEM, 0, 2)
            store("odmem", w, 28, RS_MEM, 2, 4)
            attend(OD_COUPLES, "odgate", 20, 0, XR["y3"])
            add_out("odout", None, None)
            root("last", RS_LAYER, D)
            for k in range(4):
                hk = h[:, 4 * k:4 * k + 4, :]
                step(tt(hk, hk, along(rs[:, RS_LAYER, :], 4), MUL))
                tt(hk, hk, wide(col("final_norm_2", 4, 4 * k), 4), MUL).then_inc(h_ready, 1)


def _head(qk, v, o, mask, scale, gate=None, sink=None):
    return dict(qk=qk, v=v, o=o, mask=mask, scale=scale, gate=gate, sink=sink)


def _couples(heads):
    return [heads[i:i + 2] for i in range(0, len(heads), 2)]


MLA_ROPE, MLA_V = [(8, 2), (10, 2), (28, 1)], list(range(20, 28))
MOBA_ROT = len(MLA_ROPE)
OD_ROT = MOBA_ROT + 8
MLA_COUPLES = _couples([
    _head([(i, 12 + i, 0, 128), (8 + i // 2, 28, 64 * (i % 2), 64)], (20 + i, 0, 128, 0), i, 1, 192.0 ** -0.5,
          gate=(i - 1, i) if i % 2 else None) for i in range(8)])
MOBA_V = list(range(16, 24)) + list(range(39, 43))
MOBA_COUPLES = _couples([
    _head([(i, 8 + i, 0, 128)], (16 + i, 0, 128, 0), i, 1, 128.0 ** -0.5,
          gate=(i - 1, i) if i % 2 else None) for i in range(8)] + [
    _head([(24 + i, 35 + i, 0, 128)], (39 + i, 0, 128, 0), 24 + i, None, 128.0 ** -0.5,
          gate=(24 + i - 1, 24 + i) if i % 2 else None) for i in range(4)])
OD_V = [9] + list(range(22, 28)) + list(range(36, 40))
OD_COUPLES = _couples([
    _head([(j, 8, 64 * g, 64)], (9, 64 * g, 64, 64 * g), j, 2, 64.0 ** -0.5, sink=j + 8 * g,
          gate=(j - 1, j) if j % 2 and g else None) for j in range(8) for g in range(2)] + [
    _head([(10 + i, 16 + i, 0, 128)], (22 + i, 0, 128, 0), 10 + i, 3, 128.0 ** -0.5,
          gate=(10 + i - 1, 10 + i) if i % 2 else None) for i in range(6)] + [
    _head([(28 + i, 32 + i, 0, 128)], (36 + i, 0, 128, 0), 28 + i, None, 128.0 ** -0.5,
          gate=(28 + i - 1, 28 + i) if i % 2 else None) for i in range(4)])


def gate_chunk(couples, c):
    shared = [h[-1]["gate"] is None for h in couples]
    p = sum(h[-1]["gate"] is not None for h in couples[:c])
    if shared[c]:
        return p, 0, 4
    if c and shared[c - 1]:
        return p, 4, 8
    return p, 0, 8


def constants():
    f = np.float32
    ident = np.eye(P, dtype=f)
    gsel = np.zeros((P, 2, P), f)
    for i in range(8):
        gsel[ROW_I + i, 0, i] = 1.0
        gsel[ROW_F + i, 1, i] = -1.0
    pos = np.arange(T)
    q, k = pos[:, None], pos[None, :]

    def rows(m):
        return m.reshape(2, P, T).transpose(1, 0, 2)

    causal = np.where(k <= q, 0.0, NEG)
    swa = np.where((q - k >= 0) & (q - k <= 127), 0.0, NEG)
    hits = ((q >= k) & (q - k <= 128)).astype(int)
    for dil in (4, 16):
        hits = hits + ((q >= k) & ((q - k) % dil == 0) & ((q - k) // dil <= 128))
    dil = np.where(hits > 0, np.log(np.maximum(hits, 1)), NEG)
    mlstm = np.where(q >= k, -NEG, 0.0) * (q != k)
    mlstm = np.where(k >= q, 0.0, -NEG)
    masks = np.stack([rows(mlstm), rows(causal), rows(swa), rows(dil)], 1).astype(f)
    s, t = np.arange(P)[:, None], np.arange(P)[None, :]
    lvl = np.zeros((P, 4, 2, P), f).reshape(P, 8, P)
    lvl[:, 0, :] = s == t
    for level in range(1, 8):
        size = 2 ** level
        lvl[:, level, :] = (s // size == t // size) & (s % size < size // 2) & (t % size >= size // 2)

    def rope(width, dim):
        inv = (f(1.0) / np.power(f(500000.0), np.arange(0, dim, 2, dtype=f) / f(dim))).astype(f)
        ang = (np.arange(T, dtype=f)[:, None] * inv[None, :]).astype(f)
        c, sn = np.cos(ang).astype(f).T, np.sin(ang).astype(f).T
        cos, sin, m = np.ones((P, T), f), np.zeros((P, T), f), np.zeros((P, P), f)
        for at in range(0, P, width):
            hf = dim // 2
            cos[at:at + hf] = c
            cos[at + hf:at + dim] = c
            sin[at:at + hf] = sn
            sin[at + hf:at + dim] = sn
            for i in range(hf):
                m[at + hf + i, at + i] = -1.0
                m[at + i, at + hf + i] = 1.0
        return np.stack([cos, sin], 1), m

    kinds = [rope(64, 64), rope(128, 32), rope(64, 16), rope(128, 32)]
    out = dict(ident=ident, gsel=gsel, masks=masks, lvl=lvl.reshape(P, 4, T))
    for name, a, b in (("ev", 0, 1), ("od", 2, 3)):
        out["rope_" + name] = np.stack([kinds[a][0], kinds[b][0]], 1)
        out["rot_" + name] = np.stack([kinds[a][1], kinds[b][1]], 1)
    return out


def channel_cols(v):
    v = np.asarray(v)
    return np.ascontiguousarray(v.reshape(-1, P).T)


def token_blocks(x):
    x = np.asarray(x)
    return np.ascontiguousarray(x.T.reshape(-1, P, T).transpose(1, 0, 2))


def weight_pairs(wt, st):
    wt = np.asarray(wt)
    cells = wt.reshape(st.blocks, P, st.pairs, st.nb, P)
    return np.ascontiguousarray(cells.transpose(2, 1, 0, 3, 4)).reshape(st.pairs, P, -1)


def layout(i):
    ST = stages()
    i = {k: np.asarray(v) for k, v in i.items()}
    out = dict(constants())
    out["x"] = token_blocks(i["x"][0])
    out["p"] = np.stack([token_blocks(i["p"][l, 0]) for l in range(2)])
    out["mem"] = np.ascontiguousarray(token_blocks(i["mem_2"][0]).reshape(P, 8, 2, T).transpose(1, 0, 2, 3))
    for name in ("w_r", "w_i"):
        out[name] = np.ascontiguousarray(i["b_" + name][0].transpose(1, 0, 2)).reshape(P, 8 * P)
    gate_b = np.zeros((P, 1), np.float32)
    gate_b[ROW_I:ROW_I + 8, 0] = i["c_b_i"][0]
    gate_b[ROW_F:ROW_F + 8, 0] = i["c_b_f"][0]
    c = dict(
        e_norm=i["e_norm"][0], a_lb0=i["a_lb_logits"][0], a_lb1=i["a_lb_logits"][1], a_norm=i["a_norm"][0],
        b_conv_w=i["b_conv_w"][0], b_conv_b=i["b_conv_b"][0], b_b_r=i["b_b_r"][0], b_b_i=i["b_b_i"][0],
        b_lambda=i["b_lambda"][0], o_norm=i["o_norm"][0], c_conv_w=i["c_conv_w"][0], c_conv_b=i["c_conv_b"][0],
        c_norm=i["c_norm"][0], ple_norm0=i["ple_norm"][0], ple_norm1=i["ple_norm"][1], final_norm=i["final_norm"],
        ev_norm=i["ev_norm_g_2"][0], ev_q_norm=i["ev_q_norm_g_2"][0], ev_kv_norm=i["ev_kv_norm_g_2"][0],
        ev_mem_norm=i["ev_mem_norm_g_2"][0], od_norm=i["od_norm_g_2"][0], od_mem_norm=i["od_mem_norm_g_2"][0],
        final_norm_2=i["final_norm_g_2"])
    c = {k: channel_cols(v) for k, v in c.items()}
    c["c_gate_b"] = gate_b
    c["sinks"] = np.broadcast_to(i["od_sinks_2"][0], (P, 16))
    out["cols"] = np.ascontiguousarray(np.concatenate([c[n] for n, _ in COLS], 1))

    W = {}
    e = i["e_w_in"][0]
    W["ein"], W["ein_zx"], W["ein_zb"] = e[:, :3072], e[:, 3072:5120], e[:, 5120:]
    W["eout"], W["oout"] = i["e_w_out"][0], i["o_w_out"][0]
    for l in range(2):
        W[f"ple{l}"], W[f"gate{l}"] = i["ple_w"][l], i["ple_gate_w"][l]
    o = i["o_w_in"][0]
    W["oqk"], W["ov"] = o[:, 0:2048], o[:, 2048:4096]
    W["ogz"] = o[:, 4096:8192].reshape(D, 2, 8, 256).transpose(0, 2, 1, 3).reshape(D, 4096)
    g = np.zeros((D, P), np.float32)
    g[:, ROW_I:ROW_I + 8] = o[:, 8192:8200]
    g[:, ROW_F:ROW_F + 8] = o[:, 8200:8208]
    W["ogate"] = g
    e = i["ev_w_in_2"][0]
    W["evc"] = e[:, 0:768]
    W["evkpe"] = np.concatenate([e[:, 768:832], e[:, 768:832]], 1)
    W["evmoba"] = e[:, 832:832 + 3584]
    W["evgate_a"], W["evgate_b"] = e[:, 4416:4416 + 1024], e[:, 5440:]
    W["evmem"], o = i["ev_w_mem_kv_2"][0], i["od_w_mem_kv_2"][0]
    W["odmem"] = np.concatenate([o[:, 512:], o[:, :512]], 1)
    uq = i["ev_w_uq_2"][0].reshape(512, 8, 192)
    W["uq"] = np.concatenate([uq[:, :, :128].reshape(512, 1024), uq[:, :, 128:].reshape(512, 512)], 1)
    ukv = i["ev_w_ukv_2"][0].reshape(256, 8, 2, 128)
    W["ukv"] = np.concatenate([ukv[:, :, 1].reshape(256, 1024), ukv[:, :, 0].reshape(256, 1024)], 1)
    W["evout"] = i["ev_w_out_2"][0]
    swa = np.arange(1024).reshape(2, 8, 64).transpose(1, 0, 2).reshape(-1)
    o = i["od_w_in_2"][0]
    W["odin"] = np.concatenate([o[:, swa], o[:, 1024:4096]], 1)
    W["odgate"] = np.concatenate([o[:, 4096 + swa], o[:, 5120:]], 1)
    W["odout"] = np.concatenate([i["od_w_out_2"][0][swa], i["od_w_out_2"][0][1024:]], 0)
    for name, st in ST.items():
        out["w_" + name] = weight_pairs(W[name], st)
    return out


def kernel(**inputs):
    import concourse.bacc as bacc
    from concourse import mybir
    from concourse.bass_utils import run_bass_kernel_spmd

    arrays = layout(inputs)
    nc = bacc.Bacc("TRN2", target_bir_lowering=False, num_devices=1)
    A = {n: nc.dram_tensor(n + "_dram", a.shape, mybir.dt.from_np(a.dtype), kind="ExternalInput").ap()
         for n, a in arrays.items()}
    out = nc.dram_tensor("out_dram", (P, KD, T), mybir.dt.float32, kind="ExternalOutput").ap()
    build(nc, A, out)
    r = run_bass_kernel_spmd(nc, [{n + "_dram": a for n, a in arrays.items()}], core_ids=[0])
    got = r.results[0]["out_dram"]
    return got.transpose(1, 0, 2).reshape(D, T).T.reshape(1, T, D)
```
